# Optimizing a Trainium2 kernel written in Bass

```python
import jax, jax.numpy as jnp
from jax import lax
import numpy as np

D_MODEL = 2048
BATCH = 1
SEQ = 256
DEPTH = 2

HEAD_DIM = 128
D_MIX = D_MODEL
N_HEADS_A = 10
N_HEADS_B = 6
N_HEADS_C = 8
N_HEADS_D = 8
IDX_HEADS = 16
IDX_DIM = 64
TOPK_MAX = 256
DILATED = ((128, 1), (512, 4), (2048, 16))
BLOCK = 128
ROPE_THETA = 10000.0
EPS = 1e-6

A_Q = N_HEADS_A * HEAD_DIM
IDX_Q = IDX_HEADS * IDX_DIM
B_W = N_HEADS_B * HEAD_DIM
C_W = N_HEADS_C * HEAD_DIM
D_W = N_HEADS_D * HEAD_DIM
SPLIT0 = (A_Q, HEAD_DIM, HEAD_DIM, IDX_Q, IDX_DIM, IDX_HEADS, B_W, B_W, B_W, D_MIX)
SPLIT1 = (C_W, C_W, C_W, D_W, D_W, D_W, N_HEADS_D, D_MIX)
IN0 = sum(SPLIT0)
IN1 = sum(SPLIT1)


F32 = jnp.float32

def rmsnorm(x, g):
    xf = x.astype(F32)
    y = xf * lax.rsqrt(jnp.mean(xf * xf, axis=-1, keepdims=True) + EPS)
    return (y * g.astype(F32)).astype(x.dtype)

def rope(t, pos):
    half = t.shape[-1] // 2
    inv = ROPE_THETA ** (-jnp.arange(half, dtype=F32) / half)
    ang = pos.astype(F32)[:, None] * inv[None, :]
    cos = jnp.cos(ang)[None, :, None, :]
    sin = jnp.sin(ang)[None, :, None, :]
    tf = t.astype(F32)
    t1, t2 = tf[..., :half], tf[..., half:]
    return jnp.concatenate([t1 * cos - t2 * sin, t2 * cos + t1 * sin], axis=-1).astype(t.dtype)

def split_cols(t, sizes):
    offs, acc = [], 0
    for s in sizes[:-1]:
        acc += s
        offs.append(acc)
    return jnp.split(t, offs, axis=-1)

def blocks_to_seq(out):
    nb, bsz, q, h, d = out.shape
    return out.transpose(1, 0, 2, 3, 4).reshape(bsz, nb * q, h, d)

def dsa_attention(q, k, v, iq, ik, iw):
    S = q.shape[1]
    topk = min(TOPK_MAX, S // 4)
    key_pos = jnp.arange(S)
    ikf = ik.astype(F32)

    def block(b):
        start = b * BLOCK
        qb = lax.dynamic_slice_in_dim(q, start, BLOCK, axis=1)
        iqb = lax.dynamic_slice_in_dim(iq, start, BLOCK, axis=1).astype(F32)
        iwb = lax.dynamic_slice_in_dim(iw, start, BLOCK, axis=1).astype(F32)
        qpos = start + jnp.arange(BLOCK)
        dots = jnp.einsum('bqhd,bsd->bqhs', iqb, ikf) * (IDX_DIM ** -0.5)
        score = jnp.einsum('bqh,bqhs->bqs', iwb * (IDX_HEADS ** -0.5), jax.nn.relu(dots))
        causal = key_pos[None, :] <= qpos[:, None]
        score = jnp.where(causal[None], score, -jnp.inf)
        _, sel = lax.top_k(score, topk)
        valid = sel <= qpos[None, :, None]
        ks = jax.vmap(lambda kk, ii: kk[ii])(k, sel)
        vs = jax.vmap(lambda vv, ii: vv[ii])(v, sel)
        logits = jnp.einsum('bqhd,bqkd->bqhk', qb, ks).astype(F32) * (HEAD_DIM ** -0.5)
        logits = jnp.where(valid[:, :, None, :], logits, -jnp.inf)
        p = jax.nn.softmax(logits, axis=-1)
        return jnp.einsum('bqhk,bqkd->bqhd', p.astype(v.dtype), vs)

    return blocks_to_seq(lax.map(block, jnp.arange(S // BLOCK)))

def strided_band(q, k, v, dil, steps):
    bsz, S, H, hd = q.shape
    L = S // dil
    nb = -(-L // BLOCK)
    Lp = nb * BLOCK

    def to_blocks(t):
        t = t.reshape(bsz, L, dil, H, hd).transpose(0, 2, 1, 3, 4)
        t = jnp.pad(t, ((0, 0), (0, 0), (0, Lp - L), (0, 0), (0, 0)))
        return t.reshape(bsz, dil, nb, BLOCK, H, hd)

    def with_prev(t):
        prev = jnp.pad(t, ((0, 0), (0, 0), (1, 0), (0, 0), (0, 0), (0, 0)))[:, :, :-1]
        return jnp.concatenate([prev, t], axis=3)

    qb = to_blocks(q)
    kk = with_prev(to_blocks(k))
    vv = with_prev(to_blocks(v))
    logits = jnp.einsum('brnqhd,brnkhd->brnhqk', qb, kk).astype(F32) * (HEAD_DIM ** -0.5)
    qi = jnp.arange(BLOCK)[:, None] + BLOCK
    ki = jnp.arange(2 * BLOCK)[None, :]
    dist = qi - ki
    band = (dist >= 0) & (dist <= steps)
    blk = jnp.arange(nb)[:, None, None]
    valid = band[None] & ((ki[None] >= BLOCK) | (blk > 0))
    logits = jnp.where(valid[None, None, :, None], logits, -jnp.inf)
    m = jnp.max(logits, axis=-1, keepdims=True)
    p = jnp.exp(logits - m)
    l = jnp.sum(p, axis=-1, keepdims=True)
    o = jnp.einsum('brnhqk,brnkhd->brnhqd', p, vv.astype(F32)) / l
    lse = (m + jnp.log(l))[..., 0]
    o = o.transpose(0, 1, 2, 4, 3, 5).reshape(bsz, dil, Lp, H, hd)[:, :, :L]
    o = o.transpose(0, 2, 1, 3, 4).reshape(bsz, S, H, hd)
    lse = lse.transpose(0, 1, 2, 4, 3).reshape(bsz, dil, Lp, H)[:, :, :L]
    lse = lse.transpose(0, 2, 1, 3).reshape(bsz, S, H)
    return o, lse

def dilated_attention(q, k, v):
    outs, lses = [], []
    for window, dil in DILATED:
        o, lse = strided_band(q, k, v, dil, window // dil)
        outs.append(o)
        lses.append(lse)
    alpha = jax.nn.softmax(jnp.stack(lses, axis=0), axis=0)
    o = jnp.einsum('pbsh,pbshd->bshd', alpha, jnp.stack(outs, axis=0))
    return o.astype(q.dtype)

def stick_breaking_attention(q, k, v):
    S = q.shape[1]
    key_pos = jnp.arange(S)

    def block(b):
        start = b * BLOCK
        qb = lax.dynamic_slice_in_dim(q, start, BLOCK, axis=1)
        qpos = start + jnp.arange(BLOCK)
        z = jnp.einsum('bqhd,bshd->bhqs', qb, k).astype(F32) * (HEAD_DIM ** -0.5)
        before = (key_pos[None, :] < qpos[:, None])[None, None]
        log_1m = jnp.where(before, jax.nn.log_sigmoid(-z), 0.0)
        tail = lax.cumsum(log_1m, axis=3, reverse=True) - log_1m
        w = jnp.where(before, jnp.exp(jax.nn.log_sigmoid(z) + tail), 0.0)
        return jnp.einsum('bhqs,bshd->bqhd', w.astype(v.dtype), v)

    return blocks_to_seq(lax.map(block, jnp.arange(S // BLOCK)))

def forgetting_attention(q, k, v, log_f):
    S = q.shape[1]
    key_pos = jnp.arange(S)
    c = jnp.cumsum(log_f.astype(F32), axis=1).transpose(0, 2, 1)

    def block(b):
        start = b * BLOCK
        qb = lax.dynamic_slice_in_dim(q, start, BLOCK, axis=1)
        cb = lax.dynamic_slice_in_dim(c, start, BLOCK, axis=2)
        qpos = start + jnp.arange(BLOCK)
        logits = jnp.einsum('bqhd,bshd->bhqs', qb, k).astype(F32) * (HEAD_DIM ** -0.5)
        logits = logits + (cb[..., :, None] - c[..., None, :])
        causal = (key_pos[None, :] <= qpos[:, None])[None, None]
        p = jax.nn.softmax(jnp.where(causal, logits, -jnp.inf), axis=-1)
        return jnp.einsum('bhqs,bshd->bqhd', p.astype(v.dtype), v)

    return blocks_to_seq(lax.map(block, jnp.arange(S // BLOCK)))

def layer_even(x, norm_g, w_in, w_out):
    bsz, S, _ = x.shape
    pos = jnp.arange(S)
    h = rmsnorm(x, norm_g)
    qa, ka, va, iq, ik, iw, qb, kb, vb, gate = split_cols(h @ w_in, SPLIT0)
    qa = rope(qa.reshape(bsz, S, N_HEADS_A, HEAD_DIM), pos)
    ka = rope(ka.reshape(bsz, S, 1, HEAD_DIM), pos)[:, :, 0]
    iq = rope(iq.reshape(bsz, S, IDX_HEADS, IDX_DIM), pos)
    ik = rope(ik.reshape(bsz, S, 1, IDX_DIM), pos)[:, :, 0]
    o_a = dsa_attention(qa, ka, va, iq, ik, iw)
    qb = rope(qb.reshape(bsz, S, N_HEADS_B, HEAD_DIM), pos)
    kb = rope(kb.reshape(bsz, S, N_HEADS_B, HEAD_DIM), pos)
    vb = vb.reshape(bsz, S, N_HEADS_B, HEAD_DIM)
    o_b = dilated_attention(qb, kb, vb)
    y = jnp.concatenate([o_a.reshape(bsz, S, A_Q), o_b.reshape(bsz, S, B_W)], axis=-1)
    return x + (y * jax.nn.silu(gate)) @ w_out

def layer_odd(x, norm_g, w_in, b_f, w_out):
    bsz, S, _ = x.shape
    h = rmsnorm(x, norm_g)
    qc, kc, vc, qd, kd, vd, fl, gate = split_cols(h @ w_in, SPLIT1)
    shp_c = (bsz, S, N_HEADS_C, HEAD_DIM)
    shp_d = (bsz, S, N_HEADS_D, HEAD_DIM)
    o_c = stick_breaking_attention(qc.reshape(shp_c), kc.reshape(shp_c), vc.reshape(shp_c))
    log_f = jax.nn.log_sigmoid(fl.astype(F32) + b_f.astype(F32))
    o_d = forgetting_attention(qd.reshape(shp_d), kd.reshape(shp_d), vd.reshape(shp_d), log_f)
    y = jnp.concatenate([o_c.reshape(bsz, S, C_W), o_d.reshape(bsz, S, D_W)], axis=-1)
    return x + (y * jax.nn.silu(gate)) @ w_out

def first_inputs(seed: int = 0) -> dict:
    key = jax.random.key(seed)
    ks = jax.random.split(key, 10)
    nrm = jax.random.normal
    return {
        'x': nrm(ks[0], (BATCH, SEQ, D_MODEL), F32),
        'norm0': 1.0 + 0.02 * nrm(ks[1], (D_MODEL,), F32),
        'w_in0': nrm(ks[2], (D_MODEL, IN0), F32) * D_MODEL ** -0.5,
        'w_out0': nrm(ks[3], (D_MIX, D_MODEL), F32) * D_MIX ** -0.5,
        'norm1': 1.0 + 0.02 * nrm(ks[4], (D_MODEL,), F32),
        'w_in1': nrm(ks[5], (D_MODEL, IN1), F32) * D_MODEL ** -0.5,
        'b_f1': 2.0 + 0.5 * nrm(ks[6], (N_HEADS_D,), F32),
        'w_out1': nrm(ks[7], (D_MIX, D_MODEL), F32) * D_MIX ** -0.5,
        'norm_f': 1.0 + 0.02 * nrm(ks[8], (D_MODEL,), F32),
    }

def first_block(x, norm0, w_in0, w_out0, norm1, w_in1, b_f1, w_out1, norm_f):
    for i in range(DEPTH):
        if i % 2 == 0:
            x = layer_even(x, norm0, w_in0, w_out0)
        else:
            x = layer_odd(x, norm1, w_in1, b_f1, w_out1)
    return rmsnorm(x, norm_f)


DEPTH_2 = 1

MIX_WIDTH = D_MODEL
NSA_HEADS = 8
NSA_KV_HEADS = 2
HEAD_DIM_2 = MIX_WIDTH // 2 // NSA_HEADS
NSA_WIDTH = NSA_HEADS * HEAD_DIM_2
GQA_GROUP = NSA_HEADS // NSA_KV_HEADS
KV_WIDTH = NSA_KV_HEADS * HEAD_DIM_2
ROPE_DIM = HEAD_DIM_2 // 4
ROPE_THETA_2 = 500000.0
CMP_LEN = 32
CMP_STRIDE = 16
CMP_HIDDEN = 2 * HEAD_DIM_2
SEL_LEN = 64
SEL_TOPK = 16
WINDOW = 512
Q_BLOCK = 128
N_GATES = 3
LRU_WIDTH = MIX_WIDTH - NSA_WIDTH
LRU_BLOCKS = 8
LRU_BLOCK_DIM = LRU_WIDTH // LRU_BLOCKS
CONV_WIDTH = 4
LRU_C = 8.0
D_FF = 5632
PLE_DIM = 256
IN_WIDTH = NSA_WIDTH + 6 * KV_WIDTH + NSA_HEADS * N_GATES + 2 * LRU_WIDTH
RMS_EPS = 1e-6
NEG = -1e30
SEL_FORCE = 1e4


def rmsnorm_2(x, g):
    xf = x.astype(jnp.float32)
    y = xf * lax.rsqrt(jnp.mean(xf * xf, axis=-1, keepdims=True) + RMS_EPS)
    return (y * g.astype(jnp.float32)).astype(x.dtype)

def swiglu(x, w_gate, w_up, w_down):
    return (jax.nn.silu(x @ w_gate) * (x @ w_up)) @ w_down

def partial_rope(x, positions):
    half = ROPE_DIM // 2
    inv_freq = ROPE_THETA_2 ** (-jnp.arange(half, dtype=jnp.float32) / half)
    ang = positions.astype(jnp.float32)[..., None] * inv_freq
    cos = jnp.cos(ang)[:, :, None, :]
    sin = jnp.sin(ang)[:, :, None, :]
    xr = x[..., :ROPE_DIM].astype(jnp.float32)
    x1, x2 = xr[..., :half], xr[..., half:]
    rot = jnp.concatenate([x1 * cos - x2 * sin, x2 * cos + x1 * sin], axis=-1)
    return jnp.concatenate([rot.astype(x.dtype), x[..., ROPE_DIM:]], axis=-1)

def masked_softmax(s, mask):
    s = jnp.where(mask, s.astype(jnp.float32), NEG)
    return jax.nn.softmax(s, axis=-1) * mask

def compress(kv, pos_emb, w1, w2):
    B, T, G, dh = kv.shape
    n_cmp = (T - CMP_LEN) // CMP_STRIDE + 1
    idx = jnp.arange(n_cmp)[:, None] * CMP_STRIDE + jnp.arange(CMP_LEN)[None, :]
    blocks = kv[:, idx] + pos_emb[:, None, :]
    blocks = blocks.transpose(0, 1, 3, 2, 4).reshape(B, n_cmp, G, CMP_LEN * dh)
    return jax.nn.gelu(blocks @ w1) @ w2

def nsa_attention(q, k_cmp, v_cmp, k_sel, v_sel, k_win, v_win, gates,
                  pos_k, pos_v, k_w1, k_w2, v_w1, v_w2):
    B, T = q.shape[:2]
    G, R, dh = NSA_KV_HEADS, GQA_GROUP, HEAD_DIM_2
    scale = HEAD_DIM_2 ** -0.5
    kc = compress(k_cmp, pos_k, k_w1, k_w2)
    vc = compress(v_cmp, pos_v, v_w1, v_w2)
    n_cmp = kc.shape[1]
    cmp_start = jnp.arange(n_cmp) * CMP_STRIDE
    cmp_end = cmp_start + CMP_LEN - 1
    n_sel = T // SEL_LEN
    top_k = min(SEL_TOPK, n_sel)
    sel_start = jnp.arange(n_sel) * SEL_LEN
    overlap = ((cmp_start[:, None] < sel_start[None, :] + SEL_LEN)
               & (cmp_end[:, None] >= sel_start[None, :])).astype(jnp.float32)
    kb = k_sel.reshape(B, n_sel, SEL_LEN, G, dh).transpose(0, 3, 1, 2, 4)
    vb = v_sel.reshape(B, n_sel, SEL_LEN, G, dh).transpose(0, 3, 1, 2, 4)
    kw = jnp.pad(k_win, ((0, 0), (WINDOW, 0), (0, 0), (0, 0)))
    vw = jnp.pad(v_win, ((0, 0), (WINDOW, 0), (0, 0), (0, 0)))
    qg = q.reshape(B, T, G, R, dh)
    bi = jnp.arange(B)[:, None, None, None]
    gi = jnp.arange(G)[None, :, None, None]
    blk = jnp.arange(n_sel)

    def query_block(i):
        t0 = i * Q_BLOCK
        qb = lax.dynamic_slice_in_dim(qg, t0, Q_BLOCK, 1)
        gb = lax.dynamic_slice_in_dim(gates, t0, Q_BLOCK, 1).reshape(B, Q_BLOCK, G, R, N_GATES)
        t = t0 + jnp.arange(Q_BLOCK)
        s = jnp.einsum('btgrd,bcgd->bgrtc', qb, kc) * scale
        pc = masked_softmax(s, cmp_end[None, :] <= t[:, None])
        o_cmp = jnp.einsum('bgrtc,bcgd->btgrd', pc.astype(vc.dtype), vc)
        imp = jnp.einsum('bgrtc,cs->bgts', pc, overlap)
        forced = (blk[None, :] == (t // SEL_LEN)[:, None]) | (blk[None, :] == 0)
        valid = sel_start[None, :] <= t[:, None]
        imp = jnp.where(forced, SEL_FORCE, jnp.where(valid, imp, -SEL_FORCE))
        _, idx = lax.top_k(imp, top_k)
        ks = kb[bi, gi, idx]
        vs = vb[bi, gi, idx]
        kpos = idx[..., None] * SEL_LEN + jnp.arange(SEL_LEN)
        ms = (kpos <= t[:, None, None]).reshape(B, G, 1, Q_BLOCK, top_k * SEL_LEN)
        s = jnp.einsum('btgrd,bgtkjd->bgrtkj', qb, ks).reshape(B, G, R, Q_BLOCK, top_k * SEL_LEN) * scale
        ps = masked_softmax(s, ms).reshape(B, G, R, Q_BLOCK, top_k, SEL_LEN)
        o_sel = jnp.einsum('bgrtkj,bgtkjd->btgrd', ps.astype(vs.dtype), vs)
        kwb = lax.dynamic_slice_in_dim(kw, t0, WINDOW + Q_BLOCK, 1)
        vwb = lax.dynamic_slice_in_dim(vw, t0, WINDOW + Q_BLOCK, 1)
        kp = t0 - WINDOW + jnp.arange(WINDOW + Q_BLOCK)
        mw = (kp[None, :] <= t[:, None]) & (kp[None, :] > t[:, None] - WINDOW) & (kp[None, :] >= 0)
        s = jnp.einsum('btgrd,bsgd->bgrts', qb, kwb) * scale
        pw = masked_softmax(s, mw)
        o_win = jnp.einsum('bgrts,bsgd->btgrd', pw.astype(vwb.dtype), vwb)
        o = gb[..., 0, None] * o_cmp + gb[..., 1, None] * o_sel + gb[..., 2, None] * o_win
        return o.reshape(B, Q_BLOCK, NSA_WIDTH)

    out = lax.map(query_block, jnp.arange(T // Q_BLOCK))
    return out.transpose(1, 0, 2, 3).reshape(B, T, NSA_WIDTH)

def rglru_block(xb, yb, conv_w, conv_b, w_a, b_a, w_i, b_i, lam):
    B, T, C = xb.shape
    xc = lax.conv_general_dilated(xb, conv_w[:, None, :], window_strides=(1,),
                                  padding=[(CONV_WIDTH - 1, 0)],
                                  dimension_numbers=('NWC', 'WIO', 'NWC'),
                                  feature_group_count=C) + conv_b
    xh = xc.reshape(B, T, LRU_BLOCKS, LRU_BLOCK_DIM)
    r = jax.nn.sigmoid(jnp.einsum('bthi,hij->bthj', xh, w_a).reshape(B, T, C) + b_a)
    ig = jax.nn.sigmoid(jnp.einsum('bthi,hij->bthj', xh, w_i).reshape(B, T, C) + b_i)
    log_a = -LRU_C * r.astype(jnp.float32) * jax.nn.softplus(-lam.astype(jnp.float32))
    a = jnp.exp(log_a)
    u = jnp.sqrt(-jnp.expm1(2.0 * log_a)) * (ig * xc).astype(jnp.float32)

    def combine(left, right):
        a1, b1 = left
        a2, b2 = right
        return a1 * a2, a2 * b1 + b2

    _, h = lax.associative_scan(combine, (a, u), axis=1)
    return h.astype(xb.dtype) * jax.nn.gelu(yb)

def second_inputs(seed: int = 0) -> dict:
    key = jax.random.key(seed)
    ks = iter(jax.random.split(key, 64))
    L = DEPTH_2
    f32 = jnp.float32

    def nrm(shape, fan_in):
        return jax.random.normal(next(ks), shape, f32) * fan_in ** -0.5

    def gain(shape):
        return 1.0 + 0.02 * jax.random.normal(next(ks), shape, f32)

    def small(shape, s=0.01):
        return s * jax.random.normal(next(ks), shape, f32)

    x = jax.random.normal(next(ks), (BATCH, SEQ, D_MODEL), f32)
    p = jax.random.normal(next(ks), (DEPTH_2, BATCH, SEQ, PLE_DIM), f32)
    positions = (jax.random.randint(next(ks), (BATCH, 1), 0, 1024) + jnp.arange(SEQ)[None, :]).astype(jnp.int32)
    d = {'x': x, 'p': p, 'positions': positions}
    d['ff1_pre_g'] = gain((L, D_MODEL))
    d['ff1_post_g'] = gain((L, D_MODEL))
    d['ff1_w_gate'] = nrm((L, D_MODEL, D_FF), D_MODEL)
    d['ff1_w_up'] = nrm((L, D_MODEL, D_FF), D_MODEL)
    d['ff1_w_down'] = nrm((L, D_FF, D_MODEL), D_FF)
    d['mix_pre_g'] = gain((L, D_MODEL))
    d['mix_post_g'] = gain((L, D_MODEL))
    d['w_in'] = nrm((L, D_MODEL, IN_WIDTH), D_MODEL)
    d['cmp_pos_k'] = small((L, CMP_LEN, HEAD_DIM_2), 0.1)
    d['cmp_pos_v'] = small((L, CMP_LEN, HEAD_DIM_2), 0.1)
    d['cmp_k_w1'] = nrm((L, CMP_LEN * HEAD_DIM_2, CMP_HIDDEN), CMP_LEN * HEAD_DIM_2)
    d['cmp_k_w2'] = nrm((L, CMP_HIDDEN, HEAD_DIM_2), CMP_HIDDEN)
    d['cmp_v_w1'] = nrm((L, CMP_LEN * HEAD_DIM_2, CMP_HIDDEN), CMP_LEN * HEAD_DIM_2)
    d['cmp_v_w2'] = nrm((L, CMP_HIDDEN, HEAD_DIM_2), CMP_HIDDEN)
    d['nsa_gate_b'] = small((L, NSA_HEADS, N_GATES))
    d['conv_w'] = nrm((L, CONV_WIDTH, LRU_WIDTH), CONV_WIDTH)
    d['conv_b'] = small((L, LRU_WIDTH))
    d['rg_w_a'] = nrm((L, LRU_BLOCKS, LRU_BLOCK_DIM, LRU_BLOCK_DIM), LRU_BLOCK_DIM)
    d['rg_b_a'] = small((L, LRU_WIDTH))
    d['rg_w_i'] = nrm((L, LRU_BLOCKS, LRU_BLOCK_DIM, LRU_BLOCK_DIM), LRU_BLOCK_DIM)
    d['rg_b_i'] = small((L, LRU_WIDTH))
    a_c = jax.random.uniform(next(ks), (L, LRU_WIDTH), f32, 0.9, 0.999)
    a0 = a_c ** (1.0 / LRU_C)
    d['rg_lambda'] = jnp.log(a0) - jnp.log1p(-a0)
    d['attn_out_g'] = gain((L, NSA_WIDTH))
    d['rec_out_g'] = gain((L, LRU_WIDTH))
    d['w_out'] = nrm((L, MIX_WIDTH, D_MODEL), MIX_WIDTH)
    d['ff2_pre_g'] = gain((L, D_MODEL))
    d['ff2_post_g'] = gain((L, D_MODEL))
    d['ff2_w_gate'] = nrm((L, D_MODEL, D_FF), D_MODEL)
    d['ff2_w_up'] = nrm((L, D_MODEL, D_FF), D_MODEL)
    d['ff2_w_down'] = nrm((L, D_FF, D_MODEL), D_FF)
    d['ple_pre_g'] = gain((L, D_MODEL))
    d['ple_post_g'] = gain((L, D_MODEL))
    d['w_ple_gate'] = nrm((L, D_MODEL, D_MODEL), D_MODEL)
    d['w_ple_proj'] = nrm((L, PLE_DIM, D_MODEL), PLE_DIM)
    return d

def second_block(x, p, positions,
              ff1_pre_g, ff1_post_g, ff1_w_gate, ff1_w_up, ff1_w_down,
              mix_pre_g, mix_post_g, w_in,
              cmp_pos_k, cmp_pos_v, cmp_k_w1, cmp_k_w2, cmp_v_w1, cmp_v_w2, nsa_gate_b,
              conv_w, conv_b, rg_w_a, rg_b_a, rg_w_i, rg_b_i, rg_lambda,
              attn_out_g, rec_out_g, w_out,
              ff2_pre_g, ff2_post_g, ff2_w_gate, ff2_w_up, ff2_w_down,
              ple_pre_g, ple_post_g, w_ple_gate, w_ple_proj):
    B, T, _ = x.shape
    G = NSA_KV_HEADS
    offs = np.cumsum([NSA_WIDTH] + [KV_WIDTH] * 6 + [NSA_HEADS * N_GATES, LRU_WIDTH]).tolist()

    def heads(t, n):
        return t.reshape(B, T, n, HEAD_DIM_2)

    h = x
    for i in range(DEPTH_2):
        u = rmsnorm_2(h, ff1_pre_g[i])
        h = h + 0.5 * rmsnorm_2(swiglu(u, ff1_w_gate[i], ff1_w_up[i], ff1_w_down[i]), ff1_post_g[i])
        u = rmsnorm_2(h, mix_pre_g[i])
        z = u @ w_in[i]
        zq, zkc, zvc, zks, zvs, zkw, zvw, zg, zx, zy = jnp.split(z, offs, axis=-1)
        q = partial_rope(heads(zq, NSA_HEADS), positions)
        k_cmp = partial_rope(heads(zkc, G), positions)
        k_sel = partial_rope(heads(zks, G), positions)
        k_win = partial_rope(heads(zkw, G), positions)
        gates = jax.nn.sigmoid(zg.reshape(B, T, NSA_HEADS, N_GATES) + nsa_gate_b[i])
        o_attn = nsa_attention(q, k_cmp, heads(zvc, G), k_sel, heads(zvs, G), k_win, heads(zvw, G), gates,
                               cmp_pos_k[i], cmp_pos_v[i], cmp_k_w1[i], cmp_k_w2[i], cmp_v_w1[i], cmp_v_w2[i])
        o_rec = rglru_block(zx, zy, conv_w[i], conv_b[i], rg_w_a[i], rg_b_a[i],
                            rg_w_i[i], rg_b_i[i], rg_lambda[i])
        o = jnp.concatenate([rmsnorm_2(o_attn, attn_out_g[i]), rmsnorm_2(o_rec, rec_out_g[i])], axis=-1)
        h = h + rmsnorm_2(o @ w_out[i], mix_post_g[i])
        u = rmsnorm_2(h, ff2_pre_g[i])
        h = h + 0.5 * rmsnorm_2(swiglu(u, ff2_w_gate[i], ff2_w_up[i], ff2_w_down[i]), ff2_post_g[i])
        gate = jax.nn.sigmoid(rmsnorm_2(h, ple_pre_g[i]) @ w_ple_gate[i])
        h = h + rmsnorm_2(gate * (p[i] @ w_ple_proj[i]), ple_post_g[i])
    return h


def setup_inputs(seed=0):
    out = dict(first_inputs(seed))
    for name, value in second_inputs(seed + 1).items():
        if name != "x":
            out[name + "_2"] = value
    return out


def reference(
    x, norm0, w_in0, w_out0, norm1, w_in1, b_f1, w_out1, norm_f, p_2, positions_2, ff1_pre_g_2,
    ff1_post_g_2, ff1_w_gate_2, ff1_w_up_2, ff1_w_down_2, mix_pre_g_2, mix_post_g_2, w_in_2,
    cmp_pos_k_2, cmp_pos_v_2, cmp_k_w1_2, cmp_k_w2_2, cmp_v_w1_2, cmp_v_w2_2, nsa_gate_b_2,
    conv_w_2, conv_b_2, rg_w_a_2, rg_b_a_2, rg_w_i_2, rg_b_i_2, rg_lambda_2, attn_out_g_2,
    rec_out_g_2, w_out_2, ff2_pre_g_2, ff2_post_g_2, ff2_w_gate_2, ff2_w_up_2, ff2_w_down_2,
    ple_pre_g_2, ple_post_g_2, w_ple_gate_2, w_ple_proj_2,
):
    x = first_block(
        x, norm0, w_in0, w_out0, norm1, w_in1, b_f1, w_out1, norm_f,
    )
    return second_block(
        x, p_2, positions_2, ff1_pre_g_2, ff1_post_g_2, ff1_w_gate_2, ff1_w_up_2, ff1_w_down_2,
        mix_pre_g_2, mix_post_g_2, w_in_2, cmp_pos_k_2, cmp_pos_v_2, cmp_k_w1_2, cmp_k_w2_2,
        cmp_v_w1_2, cmp_v_w2_2, nsa_gate_b_2, conv_w_2, conv_b_2, rg_w_a_2, rg_b_a_2, rg_w_i_2,
        rg_b_i_2, rg_lambda_2, attn_out_g_2, rec_out_g_2, w_out_2, ff2_pre_g_2, ff2_post_g_2,
        ff2_w_gate_2, ff2_w_up_2, ff2_w_down_2, ple_pre_g_2, ple_post_g_2, w_ple_gate_2,
        w_ple_proj_2,
    )


_drawn_inputs = setup_inputs


def setup_inputs(seed=0):
    import zlib

    import numpy as np

    out = dict(_drawn_inputs(seed))
    spreads = {}
    factors = {'norm0': 3.512,
     'norm1': 4.839,
     'ff1_pre_g_2': 4.094,
     'ff1_post_g_2': 5.879,
     'mix_pre_g_2': 3.349,
     'mix_post_g_2': 13.265,
     'cmp_pos_k_2': 6.599,
     'nsa_gate_b_2': 46.309,
     'rg_b_a_2': 54.633,
     'rg_b_i_2': 40.988,
     'attn_out_g_2': 26.37,
     'rec_out_g_2': 26.669,
     'ff2_pre_g_2': 22.841,
     'ff2_post_g_2': 36.728,
     'ple_pre_g_2': 34.367,
     'ple_post_g_2': 25.248,
     'cmp_pos_v_2': 5.906,
     'conv_b_2': 4.946}
    for name, (base, spread) in spreads.items():
        noise = np.random.default_rng([zlib.crc32(name.encode()), seed]).standard_normal(out[name].shape)
        drawn = base * np.exp(spread * noise) if base else spread * noise
        out[name] = __import__('jax').numpy.asarray(drawn.astype(out[name].dtype))
    for name, factor in factors.items():
        out[name] = (out[name] * factor).astype(out[name].dtype)
    return out
```

```python
from contextlib import ExitStack

import numpy as np

import concourse.bass as bass
from concourse import mybir

F32 = mybir.dt.float32
F32R = mybir.dt.float32r
I32 = mybir.dt.int32
ACT = mybir.ActivationFunctionType
ALU = mybir.AluOpType
AX_X = mybir.AxisListType.X

P = 128
SEQ = 256
NT = SEQ // P
D = 2048
KC = D // P
BW = 512
UC = 4
UNIT = UC * BW
RAW = 4
PARTS = 2
DFF = 5632
FB = DFF // BW
HD = 128
BIG = 1.0e30
TAKEN = -2.0e38
EPS = 1e-6
SCALE = HD ** -0.5
LRU = 1024
LB = LRU // P
TWO_PI = (6.28125, 0.0019350051879882812, 2 * np.pi - 6.28125 - 0.0019350051879882812)
ROUND = 12582912.0

QA, KA, VA, IQ, IK, IW, QB, KB, VB, G0 = 0, 1280, 1408, 1536, 2560, 2624, 2640, 3408, 4176, 4944
W0 = 6992
QC, KCC, VC, QD, KD, VD, FL, G1 = 0, 1024, 2048, 3072, 4096, 5120, 6144, 6152
W1 = 8200
ZQ, ZKC, ZVC, ZKS, ZVS, ZKW, ZVW, ZG, ZX, ZY = 0, 1024, 1280, 1536, 1792, 2048, 2304, 2560, 2584, 3608
W2 = 4632
NCMP = (SEQ - 32) // 16 + 1


def constants():
    c = {}
    c["ident"] = np.eye(P, dtype=np.float32)
    pos = np.arange(SEQ, dtype=np.float32)

    def tables(half):
        inv = (np.float32(10000.0) ** (-np.arange(half, dtype=np.float32) / np.float32(half))).astype(np.float32)
        ang = (pos[:, None] * inv[None, :]).astype(np.float32).astype(np.float64)
        both = np.stack([np.cos(ang), np.sin(ang)], 1).astype(np.float32)
        return both.reshape(NT, P, 2, half).transpose(1, 2, 0, 3).reshape(P, 2 * NT * half)

    c["rope128"] = tables(64)
    c["rope64"] = tables(32)
    q = np.arange(SEQ)[:, None]
    k = np.arange(SEQ)[None, :]

    def keys(full):
        return np.concatenate([full[0:P, 0:P], full[P:SEQ, :]], 1).astype(np.float32)

    c["causal"] = keys(np.where(k <= q, 0.0, BIG))
    c["strict"] = keys(np.where(k < q, 0.0, BIG))
    d = q - k
    n = ((d >= 0) & (d <= 128)).astype(int) + ((d >= 0) & (d % 4 == 0)) + ((d >= 0) & (d % 16 == 0))
    c["dilated"] = keys(np.where(n > 0, -np.log(np.maximum(n, 1).astype(np.float64)), BIG))
    c["upto"] = (q <= k).astype(np.float32).reshape(NT, P, SEQ).transpose(1, 0, 2).reshape(P, NT * SEQ)
    end = np.arange(NCMP) * 16 + 31
    ok = (end[None, :] <= q).astype(np.float32).reshape(NT, P, NCMP).transpose(1, 0, 2)
    c["cmp_ok"] = np.repeat(ok[:, None], 8, 1).reshape(P, 8 * NT * NCMP)
    inv = (np.float32(500000.0) ** (-np.arange(16, dtype=np.float32) / np.float32(16))).astype(np.float32)
    c["inv"] = np.tile(inv[None, :], (P, 1))
    return {n: np.ascontiguousarray(a, dtype=np.float32) for n, a in c.items()}


def build(nc, t):
    blocks = []

    def plan(w, c0, widths, chunks=KC):
        first = len(blocks)
        for width in widths:
            u = blocks[-1][0] + len(blocks[-1][4]) if blocks else 0
            blocks.append((u, w, c0, width, [(k, min(UC, chunks - k)) for k in range(0, chunks, UC)]))
            c0 += width
        return first

    def plan_other(units):
        blocks.append((blocks[-1][0] + len(blocks[-1][4]), None, 0, 0, [None] * units))
        return len(blocks) - 1

    L0_QKV = plan(t["w_in0"], 0, [BW] * 9 + [G0 - 9 * BW])
    L0_GATE = plan(t["w_in0"], G0, [BW] * 4)
    L0_OUT = plan(t["w_out0"], 0, [BW] * 4)
    L1_QKV = plan(t["w_in1"], 0, [BW] * 12)
    L1_GATE = plan(t["w_in1"], FL, [BW] * 3 + [260, 260])
    L1_OUT = plan(t["w_out1"], 0, [BW] * 4)
    FF1 = plan_other(12 * FB)
    MIX_REC = plan(t["w_in_2"], ZG, [BW] * 3 + [268, 268])
    MIX_QKV = plan(t["w_in_2"], 0, [BW] * 5)
    CMP = plan_other(4)
    plan_other(4)
    MIX_OUT = plan(t["w_out_2"], 0, [BW] * 4)
    FF2 = plan_other(12 * FB)
    PLE_GATE = plan(t["w_ple_gate_2"], 0, [BW] * 4)
    PLE_PROJ = plan(t["w_ple_proj_2"], 0, [BW] * 4, 2)
    N_UNITS = blocks[-1][0] + 1
    first_unit = [b[0] for b in blocks]
    pair_of, drains_before, drains = {}, {}, [0, 0]
    for b in range(len(blocks)):
        if b not in (FF1, FF2):
            pair_of[b] = sum(drains) % 2
            drains_before[b] = drains[pair_of[b]]
            drains[pair_of[b]] += 1
    block_of = {}
    for b, blk in enumerate(blocks):
        for n in range(len(blk[4])):
            block_of[blk[0] + n] = (b, n)

    turned_before, scaled_before, n_turned, n_scaled = {}, {}, 0, 0
    for name, steps, normed in (("n0", 8, True), ("y0", 8, False), ("n1", 8, True), ("y1", 8, False),
                                ("ff1", 8, True), ("h1", 2 * FB, False), ("mix", 8, True), ("attn", 4, True),
                                ("ff2", 8, True), ("h2", 2 * FB, False), ("ple", 8, True), ("p", 2, False)):
        turned_before[name], scaled_before[name] = n_turned, n_scaled
        n_turned += steps
        n_scaled += steps if normed else 0

    with ExitStack() as ctx:
        def sb(name, shape, dt=F32):
            return ctx.enter_context(nc.sbuf_tensor(name, shape, dt))

        def sem(name):
            return ctx.enter_context(nc.semaphore(name))

        res = sb("res", [P, NT, D])
        raw = sb("raw", [P, RAW, UNIT])
        w_hi = sb("w_hi", [P, PARTS, UNIT], F32R)
        w_lo = sb("w_lo", [P, PARTS, UNIT], F32R)
        x_hi = sb("x_hi", [P, KC, SEQ], F32R)
        x_lo = sb("x_lo", [P, KC, SEQ], F32R)
        ident = sb("ident", [P, P])
        ones = sb("ones", [P, P])
        causal = sb("causal", [P, 3 * P])
        other_mask = sb("other_mask", [P, 3 * P])
        upto = sb("upto", [P, NT, SEQ])
        rope128 = sb("rope128", [P, 2, NT, 64])
        rope64 = sb("rope64", [P, 2, NT, 32])
        cols = sb("cols", [P, 256])
        st = sb("st", [P, 416])
        cmp_ok = sb("cmp_ok", [P, 8 * NT * NCMP])
        position = sb("position", [P, NT], I32)
        z = sb("z", [P, 2 * W1])
        with nc.sbuf_tensor("work", [P, 4096], F32) as work:
            pass
        scaled = sb("scaled", [P, 2, BW])
        gained = sb("gained", [P, 2, UC, P])
        h_hi = sb("h_hi", [P, UC, SEQ], F32R)
        h_lo = sb("h_lo", [P, UC, SEQ], F32R)
        ps = ctx.enter_context(nc.psum_tensor("ps", [P, 8, BW], F32))

        z0 = z[:, 0:2 * W0].rearrange("p (t n) -> p t n", t=NT)
        z1 = z[:, 0:2 * W1].rearrange("p (t n) -> p t n", t=NT)
        z2 = z[:, 0:2 * W2].rearrange("p (t n) -> p t n", t=NT)
        rot_a, rot_b = z[:, 13984:14752], z[:, 14752:15520]
        ik_twice = z[:, 15520:15776].rearrange("p (t n) -> p t n", t=NT)
        grow = z[:, 12288:14336]
        out2 = z[:, 2048:6144].rearrange("p (t n) -> p t n", t=NT)
        silu = z[:, 0:1024].rearrange("p (t n) -> p t n", t=NT)
        hid = z[:, 1024:2048].rearrange("p (t n) -> p t n", t=NT)
        ple_gate = z[:, 6144:10240].rearrange("p (t n) -> p t n", t=NT)
        p_in = z[:, 10240:10752].rearrange("p (t n) -> p t n", t=NT)
        qkT = work[:, 0:1024].rearrange("p (b n) -> p b n", b=2)
        neg = work[:, 1024:1792].rearrange("p (b n) -> p b n", b=2)
        prob = work[:, 1792:2560].rearrange("p (b n) -> p b n", b=2)
        probT = work[:, 2560:2944]
        rest_a = work[:, 2944:3456]
        rest_b = work[:, 3456:3840]
        GAIN = {"n0": 0, "n1": 16, "ff1": 32, "mix": 48, "attn": 64, "rec": 72, "ff2": 80, "ple": 96}
        CONV, CONVB, BA, BI, LAM, INV, POSK, POSV = 112, 144, 152, 160, 168, 176, 192, 224
        m4sp = st[:, 0:8]
        ssq, root, rstd = st[:, 8:10], st[:, 10:12], st[:, 12:14]
        low = st[:, 16:20].rearrange("p (b n) -> p b n", b=2)
        total = st[:, 20:24].rearrange("p (b n) -> p b n", b=2)
        inv = st[:, 24:26]
        share = st[:, 26:28]
        neg_log_f = st[:, 32:48].rearrange("p (t h) -> p t h", t=NT)
        forget_b, gate_bias = st[:, 48:56], st[:, 56:80]
        nsa_gates = st[:, 80:128].rearrange("p (t h) -> p t h", t=NT)
        best8 = st[:, 128:144].rearrange("p (t n) -> p t n", t=NT)
        idx_w = st[:, 144:176].rearrange("p (t n) -> p t n", t=NT)
        pos_f = st[:, 176:178]
        turn_tab = st[:, 192:256].rearrange("p (c t n) -> p c t n", c=2, t=NT)
        ang, cyc = (st[:, o:o + 32].rearrange("p (t n) -> p t n", t=NT) for o in (256, 288))
        half_ba, half_bi = st[:, 320:328], st[:, 328:336]
        lam_x, lam_s, lam_s2, lam_q = (st[:, o:o + 8] for o in (352, 360, 368, 376))
        forget_x, forget_e = (st[:, o:o + 16].rearrange("p (t h) -> p t h", t=NT) for o in (384, 400))
        r_pad = z[:, 9264:9264 + LB * 259].rearrange("p (b n) -> p b n", b=LB)
        r0, r1, r2 = z[:, 9264:11312], z[:, 11336:13384], z[:, 13384:15432]
        r3, r4 = z[:, ZX:ZX + 2 * LRU], z[:, W2 + ZX:W2 + ZX + 2 * LRU]
        rg = work[:, 2048:4096].rearrange("p (m b j) -> p m b j", m=2, b=LB)
        by_block = lambda a: a.rearrange("p (b n) -> p b n", b=LB)
        o_attn = r2.rearrange("p (t n) -> p t n", t=NT)
        cmp_w2 = z[:, 15432:15944].rearrange("p (m k n) -> p m k n", m=2, k=2)
        cmp_kT = z[:, 15944:15976]
        cmp_v = z[:, 15976:16232].rearrange("p (g n) -> p g n", g=2)
        cmp_x = [work[:, 1024 * m:1024 * m + 1024] for m in range(2)]
        cmp_hid = [work[0:32, 2048 + 256 * m:2304 + 256 * m] for m in range(2)]
        cmp_hidT = [work[:, 2560 + 64 * m:2624 + 64 * m] for m in range(2)]
        cmp_logits = work[:, 3456:3696]
        cmp_low = work[:, 3696:3712]
        cmp_sum = work[:, 3712:3728]

        x_landed = sem("x_landed")
        const_landed = sem("const_landed")
        raw_landed = [sem(f"raw_landed_{j}") for j in range(RAW)]
        hi_ready = sem("hi_ready")
        parts_ready = sem("parts_ready")
        parts_used = sem("parts_used")
        drained = [sem("even_drained"), sem("odd_drained")]
        st_scaled, st_turned, st_gained, st_hi, st_done = (
            sem(n) for n in ("chunks_scaled", "chunks_turned", "chunks_gained", "chunks_hi", "chunks_done"))
        root_ready, rstd_ready = sem("root_ready"), sem("rstd_ready")
        act_chain, dve_chain, pool_chain = sem("act_chain"), sem("dve_chain"), sem("pool_chain")
        res_ready = sem("res_ready")
        gate_tanh = sem("gate_tanh")
        idx_turned, idx_copied, dots_ready, relu_ready, scored = (
            sem(n) for n in ("idx_turned", "idx_copied", "dots_ready", "relu_ready", "scored"))
        rotated = sem("rotated")
        qk_turned, qk_copied, logits_ready, negated, probs_ready, probs_turned, probs_copied, mixed, out_written = (
            sem(n) for n in ("qk_turned", "qk_copied", "logits_ready", "negated", "probs_ready", "probs_turned",
                             "probs_copied", "mixed", "out_written"))
        softplus_ready, arg_ready = sem("softplus_ready"), sem("arg_ready")
        vec_small, act_small, pe_small, pool_small = (
            sem(n) for n in ("small_by_vector", "small_by_scalar", "small_by_tensor", "small_by_pool"))
        ff_tanh, ff_silu, hid_ready, added = (sem(n) for n in ("ff_tanh", "ff_silu", "hid_ready", "added"))
        strict_landed, p_landed, mix_landed = sem("strict_landed"), sem("p_landed"), sem("mix_landed")
        y_ready = sem("y_ready")
        grow_landed = sem("grow_landed")
        out_landed = sem("out_landed")

        block = ctx.enter_context(nc.Block())

        made = {n: sem(n) for n in (
            "rec_x_turned", "rec_y_turned", "rec_padded", "rec_y_gelu", "rec_conv", "rec_r_product", "rec_r_tanh",
            "rec_log_a", "rec_a", "rec_i_product", "rec_i_tanh", "rec_square", "rec_root", "rec_out_squared",
            "rec_summed", "rec_norm_root", "rec_ready", "rec_hi", "rec_lo", "lam_exp",
            "cmp_turned", "cmp_summed", "cmp_hi", "cmp_lo", "cmp_hid_turned", "cmp_hidT_ready", "cmp_kv_made",
            "cmp_kv_ready", "cmp_negated", "cmp_probs", "cmp_weighted", "cmp_p_turned", "cmp_p_copied", "cmp_mixed",
            "cmp_added", "angle_ready", "angle_sin", "nsa_gate_sum", "nsa_gate_tanh", "forget_sum", "forget_ln",
            "weights_landed", "const_made")}
        drain_kind = {}
        gate_no = {}
        for b in range(len(blocks)):
            if b < L0_GATE or L1_QKV <= b < L1_GATE or MIX_REC <= b < CMP or MIX_OUT <= b < FF2:
                drain_kind[b] = "copy"
            elif b < L0_OUT or L1_GATE <= b < L1_OUT:
                gate_no[b] = len(gate_no) + 1
                drain_kind[b] = "gate"
            elif b < L1_QKV or L1_OUT <= b < FF1:
                drain_kind[b] = "residual"
            elif CMP <= b < MIX_OUT:
                drain_kind[b] = "gelu"
            elif PLE_GATE <= b < PLE_PROJ:
                drain_kind[b] = "tanh"
            elif b >= PLE_PROJ:
                drain_kind[b] = "gated"

        def place_of(b):
            _, _, c0, width, _ = blocks[b]
            if b < L0_OUT:
                return z0[:, :, c0:c0 + width]
            if L1_QKV <= b < L1_OUT:
                return z1[:, :, c0:c0 + width]
            if MIX_REC <= b < CMP:
                return z2[:, :, c0:c0 + width]
            if MIX_OUT <= b < FF2 or b >= PLE_PROJ:
                return out2[:, :, c0:c0 + width]
            if b >= PLE_GATE:
                return ple_gate[:, :, c0:c0 + width]
            return res[:, :, c0:c0 + width]

        def added_before(no):
            return no * (4 * FB + 1) + 1

        def summed(b):
            return ps[:, 2 * pair_of[b]:2 * pair_of[b] + 2, 0:blocks[b][3]]

        def each(eng, count, body):
            pairs = count // 2
            if pairs >= 3:
                with eng.Fori(0, pairs) as i:
                    for r in range(2):
                        body(i * 2 + r, i, r)
            else:
                for n in range(2 * pairs):
                    body(n, n // 2, n % 2)
            for n in range(2 * pairs, count):
                body(n, n // 2, n % 2)

        def all_drained(eng, b):
            for pair in range(2):
                eng.wait_ge(drained[pair], sum(1 for x in pair_of if x < b and pair_of[x] == pair))

        jobs = []
        for h in range(10):
            jobs.append((z0, QA + h * HD, KA, VA, "sparse"))
        for h in range(6):
            jobs.append((z0, QB + h * HD, KB + h * HD, VB + h * HD, "dilated"))
        for h in range(8):
            jobs.append((z1, QC + h * HD, KCC + h * HD, VC + h * HD, "stick"))
        for h in range(8):
            jobs.append((z1, QD + h * HD, KD + h * HD, VD + h * HD, "forget"))
        for h in range(8):
            jobs.append((z2, ZQ + h * HD, ZKS + h // 4 * HD, ZVS + h // 4 * HD, "selected"))
            jobs.append((z2, ZQ + h * HD, ZKW + h // 4 * HD, ZVW + h // 4 * HD, "window"))
        ROT_STEPS = 12
        beside_rot = [1 if n % 3 == 2 else 0 for n in range(ROT_STEPS)]
        beside_idx = [1] * 8
        beside = [1] * 4 + [0] * 12 + [2] * 4 + [1] * 12 + [0] * 16
        keys_of = (slice(0, P), slice(P, 3 * P))

        @block.sync
        def _(sp):
            sp.dma_start(res[:], t["x"]).then_inc(x_landed, 16)

            def load(u, j, dst, src, first=False):
                if not first:
                    sp.wait_ge(parts_ready, u - (RAW - 1))
                sp.dma_start(dst, src).then_inc(raw_landed[j], 16)

            def slot(j, chunks, width):
                return raw[:, j, :].rearrange("p (k n) -> p k n", k=UC)[:, 0:chunks, 0:width]

            def load_block(b):
                u, w, c0, width, units = blocks[b]
                for g, (k0, n) in enumerate(units):
                    j = (u + g) % RAW
                    load(u + g, j, slot(j, n, width),
                         w[k0 * P:(k0 + n) * P, c0:c0 + width].rearrange("(k p) n -> p k n", p=P), u < RAW)

            def load_run(b, count):
                u, w, c0, width, units = blocks[b]

                def body(n, i, r):
                    for j, (k0, m) in enumerate(units):
                        load(n * 4 + (u + j), j, slot(j, m, width),
                             w[k0 * P:(k0 + m) * P, bass.ds(n * BW + c0, BW)].rearrange("(k p) n -> p k n", p=P))

                each(sp, count, body)

            def load_ff(b, gate, up, down, then):
                u0 = first_unit[b]

                def gate_up(u, i):
                    for m, w in enumerate((gate, up)):
                        for j in range(4):
                            load(u + (4 * m + j), j, slot(j, UC, BW),
                                 w[j * BW:(j + 1) * BW, bass.ds(i * BW, BW)].rearrange("(k p) n -> p k n", p=P))

                def down4(u, i):
                    for j in range(4):
                        load(u + j, j, slot(j, UC, BW),
                             down[bass.ds(i * BW, BW), j * BW:(j + 1) * BW].rearrange("(k p) n -> p k n", p=P))

                gate_up(u0, 0)
                then()
                with sp.Fori(0, FB - 1) as i:
                    gate_up(i * 12 + (u0 + 8), i + 1)
                    down4(i * 12 + (u0 + 16), i)
                down4(u0 + 12 * FB - 4, FB - 1)

            def load_gain(row):
                sp.dma_start(grow, t["rows"][row:row + 1, :].to_broadcast([P, D])).then_inc(grow_landed, 16)

            load_block(L0_QKV)
            load_run(L0_QKV + 1, 8)
            load_block(L0_QKV + 9)
            for b in range(4):
                load_block(L0_GATE + b)
            for b in range(4):
                load_block(L0_OUT + b)
            sp.wait_ge(y_ready, 1)
            sp.dma_start(other_mask[:], t["strict"]).then_inc(strict_landed, 16)
            load_run(L1_QKV, 12)
            for b in range(5):
                load_block(L1_GATE + b)
            for b in range(4):
                load_block(L1_OUT + b)
            sp.wait_ge(y_ready, 2)
            load_gain(0)

            def ff1_gain():
                sp.wait_ge(res_ready, 1)
                load_gain(1)

            load_ff(FF1, t["ff1_w_gate"], t["ff1_w_up"], t["ff1_w_down"], ff1_gain)
            for b in range(5):
                load_block(MIX_REC + b)
            sp.wait_ge(st_done, turned_before["mix"] + 8)
            for m, name in enumerate(("rg_w_a", "rg_w_i")):
                sp.dma_start(rg[:, m], t[name].rearrange("b i j -> i b j")).then_inc(mix_landed, 16)
            for m, name in enumerate(("cmp_k_w2", "cmp_v_w2")):
                sp.dma_start(cmp_w2[:, m], t[name].rearrange("(k p) n -> p k n", p=P)).then_inc(mix_landed, 16)
            for b in range(5):
                load_block(MIX_QKV + b)
            for m, name in enumerate(("cmp_k_w1", "cmp_v_w1")):
                for j in range(4):
                    load(first_unit[CMP] + 4 * m + j, j, raw[:, j, :].rearrange("p (l n) -> p l n", l=8),
                         t[name][j * 1024:(j + 1) * 1024, :].rearrange("(l p) n -> p l n", p=P))
            for b in range(4):
                load_block(MIX_OUT + b)
            sp.wait_ge(st_scaled, scaled_before["attn"] + 4)
            load_gain(2)

            def ff2_gain():
                sp.wait_ge(res_ready, 3)
                load_gain(3)
                sp.dma_start(p_in, t["p"]).then_inc(p_landed, 16)

            load_ff(FF2, t["ff2_w_gate"], t["ff2_w_up"], t["ff2_w_down"], ff2_gain)
            for b in range(4):
                load_block(PLE_GATE + b)
            for b in range(4):
                load_block(PLE_PROJ + b)
            sp.wait_ge(res_ready, 4)
            load_gain(4)
            sp.wait_ge(res_ready, 5)
            sp.dma_start(t["out"], res[:]).then_inc(out_landed, 16)
            sp.wait_ge(out_landed, 16)

        CONSTANTS = (("ident", ident), ("causal", causal), ("dilated", other_mask), ("upto", upto),
                     ("rope128", rope128), ("rope64", rope64), ("cmp_ok", cmp_ok), ("cols", cols),
                     ("positions", position))

        @block.gpsimd
        def _(pool):
            for name, tile in CONSTANTS:
                shape = tile[:]
                if name in ("upto",):
                    shape = shape.rearrange("p t n -> p (t n)")
                if name.startswith("rope"):
                    shape = shape.rearrange("p c t n -> p (c t n)")
                pool.dma_start(shape, t[name]).then_inc(const_landed, 16)
            pool.dma_start(forget_b, t["b_f1"].to_broadcast([P, 8])).then_inc(const_landed, 16)
            pool.dma_start(gate_bias, t["nsa_gate_b"].to_broadcast([P, 24])).then_inc(const_landed, 16)
            nc.gpsimd.memset(ones[:], 1.0).then_inc(made["const_made"], 1)

        ALL_CONST = 16 * (len(CONSTANTS) + 2)

        @block.tensor
        def _(pe):
            at = [0]

            def unit(u, j, k0, n, width, bank, first, last, x=(x_hi, x_lo)):
                pe.wait_ge(parts_ready, u + 1)
                hi = w_hi[:, j % PARTS, :].rearrange("p (k n) -> p k n", k=UC)
                lo = w_lo[:, j % PARTS, :].rearrange("p (k n) -> p k n", k=UC)
                for c in range(n):
                    for tt in range(NT):
                        o = ps[:, bank + tt, 0:width]
                        s = slice(tt * P, (tt + 1) * P)
                        nc.tensor.matmul(o, x[0][:, k0 + c, s], hi[:, c, 0:width], start=first and c == 0, stop=False)
                        nc.tensor.matmul(o, x[0][:, k0 + c, s], lo[:, c, 0:width], start=False, stop=False)
                        m = nc.tensor.matmul(o, x[1][:, k0 + c, s], hi[:, c, 0:width], start=False,
                                             stop=last and c == n - 1)
                m.then_inc(parts_used, 1)

            def advance(n, x=(x_hi, x_lo)):
                for _ in range(n):
                    u = at[0]
                    b, place = block_of[u]
                    _, _, _, width, units = blocks[b]
                    if place == 0 and drains_before[b]:
                        pe.wait_ge(drained[pair_of[b]], drains_before[b])
                    unit(u, u % RAW, *units[place], width, 2 * pair_of[b], place == 0, place == len(units) - 1, x)
                    at[0] += 1

            def run(b, count):
                u, _, _, width, units = blocks[b]

                def body(n, i, r):
                    pair = pair_of[b + r]
                    pe.wait_ge(drained[pair], i + drains_before[b + r])
                    for j, (k0, m) in enumerate(units):
                        unit(n * 4 + (u + j), j, k0, m, width, 2 * pair, j == 0, j == len(units) - 1)

                each(pe, count, body)
                at[0] = u + 4 * count

            def turn(name, s, chunks, r=None):
                r = s % 2 if r is None else r
                k = s + turned_before[name]
                if not isinstance(k, int) or k >= 2:
                    pe.wait_ge(st_done, k - 1)
                for c, chunk in enumerate(chunks):
                    m = nc.tensor.transpose(ps[:, 6 + r, c * P:(c + 1) * P], chunk, ident[:])
                m.then_inc(st_turned, 1)

            def turn_scaled(name, s):
                pe.wait_ge(st_scaled, scaled_before[name] + s + 1)
                turn(name, s, [scaled[:, s % 2, c * P:(c + 1) * P] for c in range(UC)])

            def first_block(name, turn_step, steps=8):
                for s in range(4):
                    turn_step(s)
                for g in range(4):
                    pe.wait_ge(st_done, turned_before[name] + min(2 * g + 2, steps))
                    advance(1)
                    for s in range(2 * g + 4, min(2 * g + 6, steps)):
                        turn_step(s)

            def normed(name):
                first_block(name, lambda s: turn_scaled(name, s))

            def plain(name, src):
                first_block(name, lambda s: turn(name, s, [src(s % 2, (s // 2) * UC + c) for c in range(UC)]))

            def turn_qk(n):
                zz, q, k, _, _ = jobs[n]
                if n:
                    pe.wait_ge(qk_copied, n)
                for m, c0 in enumerate((q, k)):
                    for tt in range(NT):
                        i = nc.tensor.transpose(ps[:, 7, (2 * m + tt) * P:(2 * m + tt + 1) * P],
                                                zz[:, tt, c0:c0 + HD], ident[:])
                i.then_inc(qk_turned, 1)

            def logits(n):
                kind = jobs[n][4]
                pe.wait_ge(qk_copied, n + 1)
                if n:
                    pe.wait_ge(negated, n)
                qT, kT = qkT[:, n % 2, 0:SEQ], qkT[:, n % 2, SEQ:2 * SEQ]
                for tt, keys in enumerate((P, SEQ)):
                    o = ps[:, 4, keys_of[tt]]
                    more = kind == "forget"
                    i = nc.tensor.matmul(o, qT[:, tt * P:(tt + 1) * P], kT[:, 0:keys], start=True, stop=not more)
                    if more:
                        nc.tensor.matmul(o, ones[:], rest_a[:, 0:keys], start=False, stop=tt == 0)
                        i = None
                    if more and tt == 1:
                        i = nc.tensor.matmul(ps[:, 4, 2 * P:3 * P], ones[:], rest_a[:, SEQ + P:2 * SEQ],
                                             start=False, stop=True)
                if kind == "selected":
                    g = (n - 32) // 2 // 4
                    for tt in range(NT):
                        i = nc.tensor.matmul(ps[:, 4, 384 + 16 * tt:384 + 16 * tt + NCMP], qT[:, tt * P:(tt + 1) * P],
                                             cmp_kT[:, 16 * g:16 * g + NCMP], start=True, stop=True)
                i.then_inc(logits_ready, 1)

            def turn_probs(n):
                pe.wait_ge(probs_ready, n + 1)
                if n:
                    pe.wait_ge(probs_copied, n)
                for c in range(3):
                    i = nc.tensor.transpose(ps[:, 5, c * P:(c + 1) * P], prob[:, n % 2, c * P:(c + 1) * P], ident[:])
                i.then_inc(probs_turned, 1)

            def mix(n):
                zz, _, _, vv, _ = jobs[n]
                pe.wait_ge(probs_copied, n + 1)
                if n:
                    pe.wait_ge(out_written, n)
                nc.tensor.matmul(ps[:, 6, 0:HD], probT[:, 0:P], zz[:, 0, vv:vv + HD], start=True, stop=True)
                nc.tensor.matmul(ps[:, 6, HD:2 * HD], probT[:, P:2 * P], zz[:, 0, vv:vv + HD], start=True, stop=False)
                nc.tensor.matmul(ps[:, 6, HD:2 * HD], probT[:, 2 * P:3 * P], zz[:, 1, vv:vv + HD],
                                 start=False, stop=True).then_inc(mixed, 1)

            def heads(n0, n1):
                turn_qk(n0)
                logits(n0)
                for n in range(n0, n1):
                    if n + 1 < n1:
                        turn_qk(n + 1)
                    if n > n0:
                        mix(n - 1)
                    advance(beside[n])
                    if n + 1 < n1:
                        logits(n + 1)
                    turn_probs(n)
                mix(n1 - 1)

            pe.wait_ge(const_landed, ALL_CONST)
            pe.wait_ge(made["const_made"], 1)
            normed("n0")
            advance(4)
            run(L0_QKV + 2, 7)
            advance(4)
            for n in range(ROT_STEPS):
                advance(beside_rot[n])
            pe.wait_ge(rotated, 1)

            def turn_idx(p):
                if p:
                    pe.wait_ge(idx_copied, p)
                for tt in range(NT):
                    i = nc.tensor.transpose(ps[:, 7, tt * P:(tt + 1) * P],
                                            z0[:, tt, IQ + p * P:IQ + (p + 1) * P], ident[:])
                if p == 0:
                    for tt in range(NT):
                        i = nc.tensor.transpose(ps[:, 7, (2 + tt) * P:(3 + tt) * P], ik_twice[:, tt, :], ident[:])
                i.then_inc(idx_turned, 1)

            turn_idx(0)
            for p in range(8):
                if p < 7:
                    turn_idx(p + 1)
                pe.wait_ge(idx_copied, p + 1)
                for h in (2 * p, 2 * p + 1):
                    if h >= 2:
                        pe.wait_ge(relu_ready, h - 1)
                    half = slice(64 * (h % 2), 64 * (h % 2) + 64)
                    for tt, keys in enumerate((P, SEQ)):
                        i = nc.tensor.matmul(ps[:, 4 + h % 2, keys_of[tt]], qkT[half, p % 2, tt * P:(tt + 1) * P],
                                             probT[half, 0:keys], start=True, stop=True)
                    i.then_inc(dots_ready, 1)
                advance(beside_idx[p])
            pe.wait_ge(scored, 17)
            heads(0, 16)
            pe.wait_ge(y_ready, 1)
            plain("y0", lambda tt, c: z0[:, tt, G0 + c * P:G0 + (c + 1) * P])
            advance(12)

            normed("n1")
            advance(4)
            run(L1_QKV + 2, 10)
            all_drained(pe, L1_GATE)
            heads(16, 24)
            heads(24, 32)
            pe.wait_ge(y_ready, 2)
            plain("y1", lambda tt, c: z1[:, tt, G1 + c * P:G1 + (c + 1) * P])
            advance(12)

            def feed_forward(b, no, name, hname):
                u0 = first_unit[b]
                all_drained(pe, b)
                h0 = no * FB
                a0 = added_before(no)

                def product(u, bank):
                    for j in range(4):
                        unit(u + j, j, j * UC, UC, BW, bank, j == 0, j == 3)

                def turn_hidden(i):
                    pe.wait_ge(hid_ready, i + (h0 + 1))
                    pe.wait_ge(added, i * 4 + a0)
                    for s in range(2):
                        turn(hname, i * 2 + s, [hid[:, s, c * P:(c + 1) * P] for c in range(UC)], s)

                def down(u, i):
                    pe.wait_ge(st_done, i * 2 + (turned_before[hname] + 2))
                    for j in range(4):
                        if j >= 2:
                            pe.wait_ge(added, i * 4 + (a0 + j - 1))
                        unit(u + j, j, 0, UC, BW, 4 + 2 * (j % 2), True, True, (h_hi, h_lo))

                for s in range(4):
                    turn_scaled(name, s)
                for g in range(4):
                    pe.wait_ge(st_done, turned_before[name] + 2 * g + 2)
                    unit(u0 + g, g, g * UC, UC, BW, 0, g == 0, g == 3)
                    for s in range(2 * g + 4, min(2 * g + 6, 8)):
                        turn_scaled(name, s)
                product(u0 + 4, 2)
                with pe.Fori(0, FB - 1) as i:
                    pe.wait_ge(hid_ready, i + (h0 + 1))
                    product(i * 12 + (u0 + 8), 0)
                    turn_hidden(i)
                    product(i * 12 + (u0 + 12), 2)
                    down(i * 12 + (u0 + 16), i)
                turn_hidden(FB - 1)
                down(u0 + 12 * FB - 4, FB - 1)
                at[0] = u0 + 12 * FB

            feed_forward(FF1, 0, "ff1", "h1")

            pe.wait_ge(added, added_before(0) + 4 * FB)
            normed("mix")
            advance(16)
            all_drained(pe, MIX_QKV)
            pe.wait_ge(st_done, turned_before["mix"] + 8)

            def turn_channels(c0):
                for b in range(LB):
                    for tt in range(NT):
                        i = nc.tensor.transpose(ps[:, 4 + b // 2, (b % 2) * SEQ + tt * P:(b % 2) * SEQ + (tt + 1) * P],
                                                z2[:, tt, c0 + b * P:c0 + (b + 1) * P], ident[:])
                return i

            turn_channels(ZX).then_inc(made["rec_x_turned"], 1)
            pe.wait_ge(made["rec_padded"], 1)
            turn_channels(ZY).then_inc(made["rec_y_turned"], 1)
            pe.wait_ge(made["rec_y_gelu"], 1)
            pe.wait_ge(made["rec_conv"], 1)
            pe.wait_ge(mix_landed, 64)
            for m, (done, free) in enumerate((("rec_r_product", None), ("rec_i_product", "rec_r_tanh"))):
                if free:
                    pe.wait_ge(made[free], 1)
                for b in range(LB):
                    i = nc.tensor.matmul(ps[:, 4 + b // 2, (b % 2) * SEQ:(b % 2 + 1) * SEQ], rg[:, m, b, :],
                                         by_block(r1)[:, b, :], start=True, stop=True)
                i.then_inc(made[done], 1)
            advance(20)
            pe.wait_ge(made["rec_out_squared"], 1)
            for b in range(LB):
                i = nc.tensor.matmul(ps[:, 4, 0:SEQ], ones[:], by_block(r2)[:, b, :], start=b == 0, stop=b == LB - 1)
            i.then_inc(made["rec_summed"], 1)
            all_drained(pe, CMP)
            pe.wait_ge(rotated, 2)
            pe.wait_ge(made["rec_norm_root"], 1)
            for m, c0 in enumerate((ZKC, ZVC)):
                for g in range(2):
                    for tt in range(NT):
                        i = nc.tensor.transpose(ps[:, 4 + m, g * SEQ + tt * P:g * SEQ + (tt + 1) * P],
                                                z2[:, tt, c0 + g * HD:c0 + (g + 1) * HD], ident[:])
                i.then_inc(made["cmp_turned"], 1)
            xf = [x[:].rearrange("p k s -> p (k s)") for x in (x_hi, x_lo)]
            for m in range(2):
                b = CMP + m
                pe.wait_ge(made["cmp_lo"], m + 1)
                pe.wait_ge(drained[pair_of[b]], drains_before[b])
                for j in range(4):
                    u = first_unit[b] + j
                    pe.wait_ge(parts_ready, u + 1)
                    hi, lo = (w[:, j % PARTS, :].rearrange("p (l n) -> p l n", l=8) for w in (w_hi, w_lo))
                    for l in range(8):
                        c = 1024 * m + (8 * j + l) * 32
                        o = ps[0:32, 2 * pair_of[b], 0:256]
                        nc.tensor.matmul(o, xf[0][:, c:c + 32], hi[:, l, :], start=j + l == 0, stop=False)
                        nc.tensor.matmul(o, xf[0][:, c:c + 32], lo[:, l, :], start=False, stop=False)
                        i = nc.tensor.matmul(o, xf[1][:, c:c + 32], hi[:, l, :], start=False, stop=j == 3 and l == 7)
                    i.then_inc(parts_used, 1)
            at[0] = first_unit[MIX_OUT]
            for m in range(2):
                pe.wait_ge(drained[pair_of[CMP + m]], drains_before[CMP + m] + 1)
                for k in range(2):
                    i = nc.tensor.transpose(ps[:, 6, 64 * m + 32 * k:64 * m + 32 * k + 32],
                                            cmp_hid[m][:, k * P:(k + 1) * P], ident[0:32, 0:32])
            i.then_inc(made["cmp_hid_turned"], 1)
            pe.wait_ge(made["cmp_hidT_ready"], 1)
            for k in range(2):
                nc.tensor.matmul(ps[:, 7, 0:32], cmp_w2[:, 0, k, :], cmp_hidT[0][:, 32 * k:32 * k + 32],
                                 start=k == 0, stop=k == 1)
            for g in range(2):
                for k in range(2):
                    i = nc.tensor.matmul(ps[0:NCMP, 7, P * (g + 1):P * (g + 2)],
                                         cmp_hidT[1][:, 32 * k + 16 * g:32 * k + 16 * g + NCMP], cmp_w2[:, 1, k, :],
                                         start=k == 0, stop=k == 1)
            i.then_inc(made["cmp_kv_made"], 1)
            pe.wait_ge(made["cmp_kv_ready"], 1)
            heads(32, 48)
            pe.wait_ge(made["cmp_weighted"], 1)
            pe.wait_ge(out_written, 48)
            for h in range(8):
                if h:
                    pe.wait_ge(made["cmp_p_copied"], h)
                for tt in range(NT):
                    i = nc.tensor.transpose(ps[0:NCMP, 5, tt * P:(tt + 1) * P],
                                            rest_a[:, 240 + (2 * h + tt) * NCMP:240 + (2 * h + tt + 1) * NCMP], ident[:])
                i.then_inc(made["cmp_p_turned"], 1)
                pe.wait_ge(made["cmp_p_copied"], h + 1)
                if h:
                    pe.wait_ge(made["cmp_added"], h)
                for tt in range(NT):
                    i = nc.tensor.matmul(ps[:, 6, tt * HD:(tt + 1) * HD], probT[0:NCMP, tt * P:(tt + 1) * P],
                                         cmp_v[0:NCMP, h // 4, :], start=True, stop=True)
                i.then_inc(made["cmp_mixed"], 1)
            pe.wait_ge(y_ready, 3)
            for s in range(4):
                turn_scaled("attn", s)
            pe.wait_ge(st_done, turned_before["attn"] + 4)
            pe.wait_ge(made["rec_lo"], 1)
            advance(16)

            feed_forward(FF2, 1, "ff2", "h2")

            pe.wait_ge(added, added_before(1) + 4 * FB)
            normed("ple")
            advance(12)
            pe.wait_ge(p_landed, 16)
            for s in range(2):
                turn("p", s, [p_in[:, s, c * P:(c + 1) * P] for c in range(2)])
            pe.wait_ge(st_done, turned_before["p"] + 2)
            advance(4, (h_hi, h_lo))

        @block.scalar
        def _(act):
            at = [0]
            chain = [0]
            norms = [0]

            def link(ins):
                chain[0] += 1
                ins.then_inc(act_chain, 1)
                act.wait_ge(act_chain, chain[0])

            def split_hi(u, j):
                act.wait_ge(raw_landed[j], u * 4 + (16 - 4 * j))
                if not isinstance(u, int) or u >= PARTS:
                    act.wait_ge(parts_used, u - (PARTS - 1))
                nc.scalar.activation(w_hi[:, j % PARTS, :], raw[:, j, :], ACT.Copy).then_inc(hi_ready, 1)

            def splits(u, j0, n):
                for k in range(n):
                    split_hi(u + k, (j0 + k) % RAW)

            def split_next(u):
                if u < N_UNITS:
                    split_hi(u, u % RAW)

            def drain(b):
                kind = drain_kind[b]
                if kind in ("residual", "gated"):
                    return
                act.wait_ge(parts_used, first_unit[b] + len(blocks[b][4]))
                if kind == "copy":
                    nc.scalar.activation(place_of(b), summed(b), ACT.Copy).then_inc(drained[pair_of[b]], 1)
                elif kind == "gate":
                    skip = 8 if b == L1_GATE else 0
                    if skip:
                        nc.scalar.activation(place_of(b)[:, :, 0:skip], summed(b)[:, :, 0:skip], ACT.Copy)
                    nc.scalar.activation(place_of(b)[:, :, skip:], summed(b)[:, :, skip:], ACT.Tanh,
                                         scale=0.5).then_inc(gate_tanh, 1)
                elif kind == "tanh":
                    nc.scalar.activation(place_of(b), summed(b), ACT.Tanh, scale=0.5).then_inc(drained[pair_of[b]], 1)
                elif kind == "gelu":
                    nc.scalar.activation(cmp_hid[b - CMP], ps[0:32, 2 * pair_of[b], 0:256],
                                         ACT.Gelu_apprx_tanh).then_inc(drained[pair_of[b]], 1)

            def advance(n):
                for _ in range(n):
                    u = at[0]
                    split_next(u + PARTS)
                    b, place = block_of[u]
                    if place == len(blocks[b][4]) - 1:
                        drain(b)
                    at[0] += 1

            def run(b, count, zz, c0):
                u = first_unit[b]

                def body(n, i, r):
                    splits(n * 4 + (u + 2), 2, 4)
                    pair = pair_of[b + r]
                    act.wait_ge(parts_used, n * 4 + (u + 4))
                    nc.scalar.activation(zz[:, :, bass.ds(n * BW + c0, BW)], ps[:, 2 * pair:2 * pair + 2, :],
                                         ACT.Copy).then_inc(drained[pair], 1)

                each(act, count, body)
                at[0] = u + 4 * count

            def rms(src, n, scale=1.0):
                for tt in range(NT):
                    link(nc.scalar.activation(work[:, 0:n], src(tt), ACT.Square, scale=scale,
                                              accum_out=ssq[:, tt:tt + 1]))
                link(nc.scalar.activation(root, ssq, ACT.Copy, scale=1.0 / n, bias=EPS))
                nc.scalar.activation(root, root, ACT.Sqrt).then_inc(root_ready, 1)
                norms[0] += 1

            def stage(name, steps, src, dst, unscaled=None):
                def scale_rows(s):
                    k = turned_before[name] + s
                    if k >= 2:
                        act.wait_ge(st_turned, k - 1)
                    nc.scalar.activation(scaled[:, s % 2, :], src(s), ACT.Copy,
                                         scale=rstd[:, s % 2:s % 2 + 1]).then_inc(st_scaled, 1)

                if src:
                    act.wait_ge(rstd_ready, norms[0])
                    scale_rows(0)
                    scale_rows(1)
                for s in range(steps):
                    if src:
                        act.wait_ge(st_gained, scaled_before[name] + s + 1)
                        nc.scalar.activation(dst(s), gained[:, s % 2], ACT.Copy).then_inc(st_hi, 1)
                        if s + 2 < steps:
                            scale_rows(s + 2)
                    else:
                        act.wait_ge(st_turned, turned_before[name] + s + 1)
                        nc.scalar.activation(dst(s), ps[:, 6 + s % 2, :].rearrange("p (k n) -> p k n", k=UC),
                                             ACT.Copy).then_inc(st_hi, 1)

            def chunk_rows(a):
                return lambda s: a[:, s % 2, (s // 2) * BW:(s // 2 + 1) * BW]

            def x_part(s):
                return x_hi[:, (s // 2) * UC:(s // 2 + 1) * UC, (s % 2) * P:(s % 2 + 1) * P]

            def copy_qk(n):
                kind = jobs[n][4]
                act.wait_ge(qk_turned, n + 1)
                if n >= 2:
                    act.wait_ge(logits_ready, n - 1)
                if kind == "forget":
                    h = n - 24
                    if n > 24:
                        act.wait_ge(logits_ready, n)
                    for tt in range(NT):
                        nc.scalar.activation(rest_a[:, tt * SEQ:(tt + 1) * SEQ], upto[:, tt, :], ACT.Copy,
                                             scale=neg_log_f[:, tt, h:h + 1])
                nc.scalar.activation(qkT[:, n % 2, :], ps[:, 7, :], ACT.Copy).then_inc(qk_copied, 1)

            def exponents(n):
                act.wait_ge(negated, n + 1)
                if n >= 2:
                    act.wait_ge(probs_turned, n - 1)
                for tt in range(NT):
                    i = nc.scalar.activation(prob[:, n % 2, keys_of[tt]], neg[:, n % 2, keys_of[tt]], ACT.Exp,
                                             scale=-1.0, bias=low[:, n % 2, tt:tt + 1],
                                             accum_out=total[:, n % 2, tt:tt + 1])
                i.then_inc(probs_ready, 1)

            def softplus(n):
                act.wait_ge(negated, n + 1)
                link(nc.scalar.activation(rest_a[:, 0:384], neg[:, n % 2, :], ACT.Abs))
                link(nc.scalar.activation(rest_a[:, 0:384], rest_a[:, 0:384], ACT.Exp, scale=-1.0))
                nc.scalar.activation(rest_a[:, 0:384], rest_a[:, 0:384], ACT.Ln, bias=1.0).then_inc(softplus_ready, 1)

            def stick_exponents(n):
                act.wait_ge(arg_ready, n - 15)
                if n >= 2:
                    act.wait_ge(probs_turned, n - 1)
                nc.scalar.activation(prob[:, n % 2, :], neg[:, n % 2, :], ACT.Exp).then_inc(probs_ready, 1)

            def heads(n0, n1):
                copy_qk(n0)
                for n in range(n0, n1):
                    if n + 1 < n1:
                        copy_qk(n + 1)
                    if jobs[n][4] == "stick":
                        softplus(n)
                        advance(beside[n])
                        stick_exponents(n)
                    else:
                        exponents(n)
                        advance(beside[n])

            splits(0, 0, 2)
            act.wait_ge(x_landed, 16)
            rms(lambda tt: res[:, tt, :], D)
            stage("n0", 8, chunk_rows(res), x_part)
            advance(4)
            advance(4)
            run(L0_QKV + 2, 7, z0, 2 * BW)
            advance(4)
            for n in range(ROT_STEPS):
                advance(beside_rot[n])

            def copy_idx(p):
                act.wait_ge(idx_turned, p + 1)
                if p >= 2:
                    act.wait_ge(dots_ready, 2 * p - 2)
                if p == 0:
                    nc.scalar.activation(probT[:, 0:SEQ], ps[:, 7, SEQ:2 * SEQ], ACT.Copy)
                nc.scalar.activation(qkT[:, p % 2, 0:SEQ], ps[:, 7, 0:SEQ], ACT.Copy).then_inc(idx_copied, 1)

            copy_idx(0)
            for p in range(8):
                if p < 7:
                    copy_idx(p + 1)
                for h in (2 * p, 2 * p + 1):
                    act.wait_ge(dots_ready, h + 1)
                    if h >= 2:
                        act.wait_ge(scored, h - 1)
                    nc.scalar.activation(neg[:, h % 2, :], ps[:, 4 + h % 2, 0:384], ACT.Relu,
                                         scale=0.125).then_inc(relu_ready, 1)
                advance(beside_idx[p])
            heads(0, 16)
            stage("y0", 8, None, x_part)
            advance(16)

            all_drained(act, L1_QKV)
            rms(lambda tt: res[:, tt, :], D)
            stage("n1", 8, chunk_rows(res), x_part)
            advance(8)
            run(L1_QKV + 2, 10, z1, 2 * BW)

            def forget_gates():
                act.wait_ge(made["forget_sum"], 1)
                link(nc.scalar.activation(forget_e, forget_x, ACT.Abs))
                link(nc.scalar.activation(forget_e, forget_e, ACT.Exp, scale=-1.0))
                nc.scalar.activation(forget_e, forget_e, ACT.Ln, bias=1.0).then_inc(made["forget_ln"], 1)
                act.wait_ge(made["forget_ln"], 2)

            heads(16, 24)
            forget_gates()
            heads(24, 32)
            stage("y1", 8, None, x_part)
            advance(16)
            all_drained(act, FF1)
            rms(lambda tt: res[:, tt, :], D)

            def feed_forward(b, no, name, hname):
                u0 = first_unit[b]
                h0 = no * FB
                rms(lambda tt: res[:, tt, :], D)
                stage(name, 8, chunk_rows(res), x_part)

                def hidden_hi(i):
                    for s in range(2):
                        act.wait_ge(st_turned, i * 2 + (turned_before[hname] + s + 1))
                        nc.scalar.activation(h_hi[:, :, s * P:(s + 1) * P],
                                             ps[:, 6 + s, :].rearrange("p (k n) -> p k n", k=UC),
                                             ACT.Copy).then_inc(st_hi, 1)

                def gate_tanhs(u, i):
                    act.wait_ge(parts_used, u + 4)
                    if not isinstance(i, int) or i or h0:
                        act.wait_ge(hid_ready, i + h0)
                    nc.scalar.activation(silu, ps[:, 0:2, :], ACT.Tanh, scale=0.5).then_inc(ff_tanh, 1)

                splits(u0 + 2, 2, 4)
                gate_tanhs(u0, 0)
                splits(u0 + 6, 2, 4)
                with act.Fori(0, FB - 1) as i:
                    u = i * 12 + (u0 + 8)
                    splits(u + 2, 2, 4)
                    hidden_hi(i)
                    gate_tanhs(u, i + 1)
                    splits(u + 6, 2, 4)
                    splits(u + 10, 2, 4)
                hidden_hi(FB - 1)
                splits(u0 + 12 * FB - 2, 2, 4)
                at[0] = u0 + 12 * FB
                act.wait_ge(added, added_before(no) + 4 * FB)
                rms(lambda tt: out2[:, tt, :], D)

            act.wait_ge(res_ready, 1)
            feed_forward(FF1, 0, "ff1", "h1")
            act.wait_ge(res_ready, 2)
            rms(lambda tt: res[:, tt, :], D)
            stage("mix", 8, chunk_rows(res), x_part)
            act.wait_ge(made["angle_ready"], 1)
            nc.scalar.activation(turn_tab, turn_tab, ACT.Sin).then_inc(made["angle_sin"], 1)
            link(nc.scalar.activation(lam_x, cols[:, LAM:LAM + 8], ACT.Abs))
            nc.scalar.activation(lam_x, lam_x, ACT.Exp, scale=-1.0).then_inc(made["lam_exp"], 1)
            advance(20)
            act.wait_ge(made["rec_x_turned"], 1)
            four = lambda: ps[:, 4:8, :].rearrange("p k (b n) -> p (k b) n", b=2)
            nc.scalar.activation(r_pad[:, :, 3:3 + SEQ], four(), ACT.Copy).then_inc(made["rec_padded"], 1)
            act.wait_ge(made["rec_y_turned"], 1)
            nc.scalar.activation(work[:, 0:2048].rearrange("p (b n) -> p b n", b=LB), four(),
                                 ACT.Gelu_apprx_tanh).then_inc(made["rec_y_gelu"], 1)
            act.wait_ge(made["rec_r_product"], 1)
            for b in range(LB):
                i = nc.scalar.activation(by_block(r2)[:, b, :], four()[:, b, :], ACT.Tanh, scale=0.5,
                                         bias=half_ba[:, b:b + 1])
            i.then_inc(made["rec_r_tanh"], 1)
            act.wait_ge(made["rec_i_product"], 1)
            for b in range(LB):
                i = nc.scalar.activation(by_block(r4)[:, b, :], four()[:, b, :], ACT.Tanh, scale=0.5,
                                         bias=half_bi[:, b:b + 1])
            i.then_inc(made["rec_i_tanh"], 1)
            act.wait_ge(made["rec_log_a"], 1)
            nc.scalar.activation(r3, r2, ACT.Exp)
            nc.scalar.activation(r0, r2, ACT.Tanh).then_inc(made["rec_a"], 1)
            act.wait_ge(made["rec_square"], 1)
            nc.scalar.activation(r2, r2, ACT.Sqrt, scale=-1.0).then_inc(made["rec_root"], 1)
            advance(20)
            act.wait_ge(made["rec_summed"], 1)
            link(nc.scalar.activation(r0[:, 0:SEQ], ps[:, 4, 0:SEQ], ACT.Copy, scale=1.0 / LRU, bias=EPS))
            nc.scalar.activation(r0[:, 0:SEQ], r0[:, 0:SEQ], ACT.Sqrt).then_inc(made["rec_norm_root"], 1)
            act.wait_ge(made["rec_ready"], 1)
            nc.scalar.activation(x_hi[:, LB:2 * LB, :], by_block(r1), ACT.Copy).then_inc(made["rec_hi"], 1)
            xf = x_hi[:].rearrange("p k s -> p (k s)")
            for m in range(2):
                act.wait_ge(made["cmp_summed"], m + 1)
                nc.scalar.activation(xf[:, 1024 * m:1024 * (m + 1)], cmp_x[m], ACT.Copy).then_inc(made["cmp_hi"], 1)
            act.wait_ge(made["nsa_gate_sum"], 1)
            nc.scalar.activation(nsa_gates, nsa_gates, ACT.Tanh, scale=0.5).then_inc(made["nsa_gate_tanh"], 1)
            advance(8)
            act.wait_ge(made["cmp_hid_turned"], 1)
            for m in range(2):
                i = nc.scalar.activation(cmp_hidT[m], ps[:, 6, 64 * m:64 * m + 64], ACT.Copy)
            i.then_inc(made["cmp_hidT_ready"], 1)
            act.wait_ge(made["cmp_kv_made"], 1)
            nc.scalar.activation(cmp_kT, ps[:, 7, 0:32], ACT.Copy)
            nc.scalar.activation(cmp_v[0:NCMP], ps[0:NCMP, 7, P:3 * P].rearrange("p (g n) -> p g n", g=2),
                                 ACT.Copy).then_inc(made["cmp_kv_ready"], 1)
            heads(32, 48)
            act.wait_ge(made["cmp_negated"], 1)
            nc.scalar.activation(rest_a[:, 240:480], cmp_logits, ACT.Exp, scale=-1.0).then_inc(made["cmp_probs"], 1)
            for h in range(8):
                act.wait_ge(made["cmp_p_turned"], h + 1)
                if h:
                    act.wait_ge(made["cmp_mixed"], h)
                nc.scalar.activation(probT[0:NCMP, 0:SEQ], ps[0:NCMP, 5, 0:SEQ],
                                     ACT.Copy).then_inc(made["cmp_p_copied"], 1)
            act.wait_ge(y_ready, 3)
            rms(lambda tt: o_attn[:, tt, :], LRU)
            stage("attn", 4, chunk_rows(o_attn), x_part)
            advance(16)
            all_drained(act, FF2)
            rms(lambda tt: out2[:, tt, :], D)
            act.wait_ge(res_ready, 3)
            feed_forward(FF2, 1, "ff2", "h2")
            act.wait_ge(res_ready, 4)
            rms(lambda tt: res[:, tt, :], D)
            stage("ple", 8, chunk_rows(res), x_part)
            advance(16)
            for s in range(2):
                act.wait_ge(st_turned, turned_before["p"] + s + 1)
                nc.scalar.activation(h_hi[:, 0:2, s * P:(s + 1) * P],
                                     ps[:, 6 + s, 0:2 * P].rearrange("p (k n) -> p k n", k=2),
                                     ACT.Copy).then_inc(st_hi, 1)
            advance(4)
            all_drained(act, len(blocks))
            rms(lambda tt: out2[:, tt, :], D, 0.5)

        @block.vector
        def _(dve):
            at = [0]
            chain = [0]
            norms = [0]
            V = nc.vector

            def link(ins):
                chain[0] += 1
                ins.then_inc(dve_chain, 1)
                dve.wait_ge(dve_chain, chain[0])

            def split_lo(u, j):
                dve.wait_ge(hi_ready, u + 1)
                V.tensor_tensor(w_lo[:, j % PARTS, :], raw[:, j, :], w_hi[:, j % PARTS, :].bitcast(F32),
                                ALU.subtract).then_inc(parts_ready, 1)

            def splits(u, j0, n):
                for k in range(n):
                    split_lo(u + k, (j0 + k) % RAW)

            def drain(b):
                kind = drain_kind[b]
                done = lambda: dve.wait_ge(parts_used, first_unit[b] + len(blocks[b][4]))
                if kind == "residual":
                    done()
                    V.scalar_tensor_tensor(place_of(b), summed(b), 0.5, place_of(b), ALU.mult,
                                           ALU.add).then_inc(drained[pair_of[b]], 1)
                elif kind == "gate":
                    skip = 8 if b == L1_GATE else 0
                    dve.wait_ge(gate_tanh, gate_no[b])
                    V.scalar_tensor_tensor(place_of(b)[:, :, skip:], place_of(b)[:, :, skip:], 1.0,
                                           summed(b)[:, :, skip:], ALU.add, ALU.mult).then_inc(drained[pair_of[b]], 1)
                elif kind == "gated":
                    done()
                    c0, width = blocks[b][2:4]
                    V.scalar_tensor_tensor(place_of(b), ple_gate[:, :, c0:c0 + width], 1.0, summed(b), ALU.add,
                                           ALU.mult).then_inc(drained[pair_of[b]], 1)

            def advance(n):
                for _ in range(n):
                    u = at[0]
                    if u + PARTS < N_UNITS:
                        split_lo(u + PARTS, (u + PARTS) % RAW)
                    b, place = block_of[u]
                    if place == len(blocks[b][4]) - 1:
                        drain(b)
                    at[0] += 1

            def run(b, count):
                u = first_unit[b]
                each(dve, count, lambda n, i, r: splits(n * 4 + (u + 2), 2, 4))
                at[0] = u + 4 * count

            def reciprocal_root():
                norms[0] += 1
                dve.wait_ge(root_ready, norms[0])
                V.reciprocal(rstd, root).then_inc(rstd_ready, 1)

            def stage(name, steps, gain, dst_hi, dst_lo):
                def apply_gain(s):
                    dve.wait_ge(st_turned, turned_before[name] + s + 1)
                    g = cols[:, GAIN[gain] + (s // 2) * UC:GAIN[gain] + (s // 2 + 1) * UC]
                    V.tensor_tensor(gained[:, s % 2], ps[:, 6 + s % 2, :].rearrange("p (k n) -> p k n", k=UC),
                                    g.unsqueeze(2).to_broadcast([P, UC, P]), ALU.mult).then_inc(st_gained, 1)

                if gain:
                    apply_gain(0)
                for s in range(steps):
                    if gain and s + 1 < steps:
                        apply_gain(s + 1)
                    dve.wait_ge(st_hi, turned_before[name] + s + 1)
                    src = gained[:, s % 2] if gain else ps[:, 6 + s % 2, :].rearrange("p (k n) -> p k n", k=UC)
                    V.tensor_tensor(dst_lo(s), src, dst_hi(s).bitcast(F32), ALU.subtract).then_inc(st_done, 1)

            def x_part(x):
                return lambda s: x[:, (s // 2) * UC:(s // 2 + 1) * UC, (s % 2) * P:(s % 2 + 1) * P]

            def x_stage(name, gain, steps=8):
                stage(name, steps, gain, x_part(x_hi), x_part(x_lo))

            def add_normed(no, factor):
                reciprocal_root()
                dve.wait_ge(rstd_ready, norms[0])
                dve.wait_ge(grow_landed, 16 * no)
                for tt in range(NT):
                    i = V.scalar_tensor_tensor(out2[:, tt, :], out2[:, tt, :], rstd[:, tt:tt + 1], grow,
                                               ALU.mult, ALU.mult)
                link(i)
                for tt in range(NT):
                    i = V.scalar_tensor_tensor(res[:, tt, :], out2[:, tt, :], factor, res[:, tt, :],
                                               ALU.mult, ALU.add)
                i.then_inc(res_ready, 1)

            def rotate(zz, tt, c0, n, step, half, cos, sin, last=None):
                v = zz[:, tt, c0:c0 + n * step].rearrange("p (h e) -> p h e", h=n)[:, :, 0:2 * half]
                v = v.rearrange("p h (w e) -> p h w e", w=2)
                a, b = (r[:, 0:n * 2 * half].rearrange("p (h w e) -> p h w e", h=n, w=2) for r in (rot_a, rot_b))
                both = lambda tab: tab.unsqueeze(1).unsqueeze(1).to_broadcast([P, n, 2, half])
                V.tensor_tensor(a, v, both(cos), ALU.mult)
                link(V.tensor_tensor(b, v, both(sin), ALU.mult))
                V.tensor_tensor(v[:, :, 0, :], a[:, :, 0, :], b[:, :, 1, :], ALU.subtract)
                i = V.tensor_tensor(v[:, :, 1, :], a[:, :, 1, :], b[:, :, 0, :], ALU.add)
                if last is None:
                    link(i)
                else:
                    i.then_inc(last, 1)

            def copy_probs(n):
                dve.wait_ge(probs_turned, n + 1)
                if n:
                    dve.wait_ge(mixed, n)
                V.tensor_copy(probT, ps[:, 5, 0:384]).then_inc(probs_copied, 1)

            def negate(n):
                kind = jobs[n][4]
                dve.wait_ge(logits_ready, n + 1)
                if n >= 2:
                    dve.wait_ge(probs_ready, n - 1)
                mask = {"sparse": rest_a[:, 0:384], "dilated": other_mask[:]}.get(kind, causal[:])
                if kind == "selected":
                    h = (n - 32) // 2
                    V.tensor_copy(cmp_logits[:, 30 * h:30 * h + 30].rearrange("p (t c) -> p t c", t=NT),
                                  ps[:, 4, 384:416].rearrange("p (t c) -> p t c", t=NT)[:, :, 0:NCMP])
                link(V.scalar_tensor_tensor(neg[:, n % 2, :], ps[:, 4, 0:384], -SCALE, mask, ALU.mult, ALU.add))
                for tt in range(NT):
                    i = V.tensor_reduce(low[:, n % 2, tt:tt + 1], neg[:, n % 2, keys_of[tt]], AX_X, ALU.min)
                i.then_inc(negated, 1)

            def stick_logits(n):
                dve.wait_ge(logits_ready, n + 1)
                if n >= 2:
                    dve.wait_ge(probs_ready, n - 1)
                V.scalar_tensor_tensor(neg[:, n % 2, :], ps[:, 4, 0:384], SCALE, other_mask[:], ALU.mult,
                                       ALU.subtract).then_inc(negated, 1)

            def stick_sums(n):
                dve.wait_ge(softplus_ready, n - 15)
                link(V.scalar_tensor_tensor(rest_a[:, 0:384], neg[:, n % 2, :], 0.0, rest_a[:, 0:384],
                                            ALU.max, ALU.add))
                for tt, (a, b) in enumerate(((0, P), (P, 3 * P))):
                    back = slice(b - 1, a - 1 if a else None, -1)
                    i = V.tensor_tensor_scan(rest_b[:, back], ones_row(b - a), rest_a[:, back], 0.0,
                                             ALU.mult, ALU.add)
                link(i)
                V.tensor_tensor(neg[:, n % 2, :], neg[:, n % 2, :], rest_b, ALU.subtract).then_inc(arg_ready, 1)

            def ones_row(n):
                return ones[:, 0:1].to_broadcast([P, n])

            def write_out(n):
                zz, q, _, _, kind = jobs[n]
                dve.wait_ge(mixed, n + 1)
                o = ps[:, 6, 0:2 * HD].rearrange("p (t d) -> p t d", t=NT)
                if kind == "stick":
                    V.tensor_copy(zz[:, :, q:q + HD], o).then_inc(out_written, 1)
                    return
                link(V.reciprocal(inv, total[:, n % 2, :]))
                if kind in ("selected", "window"):
                    h = (n - 32) // 2
                    c = 3 * h + (1 if kind == "selected" else 2)
                    link(V.tensor_tensor(share, inv, nsa_gates[:, :, c], ALU.mult))
                for tt in range(NT):
                    if kind in ("selected", "window"):
                        dst = o_attn[:, tt, h * HD:(h + 1) * HD]
                        if kind == "selected":
                            i = V.tensor_scalar(dst, o[:, tt, :], share[:, tt:tt + 1], None, ALU.mult)
                        else:
                            i = V.scalar_tensor_tensor(dst, o[:, tt, :], share[:, tt:tt + 1], dst, ALU.mult, ALU.add)
                    else:
                        i = V.tensor_scalar(zz[:, tt, q:q + HD], o[:, tt, :], inv[:, tt:tt + 1], None, ALU.mult)
                i.then_inc(out_written, 1)

            def heads(n0, n1):
                for n in range(n0, n1):
                    if n > n0:
                        copy_probs(n - 1)
                    stick = jobs[n][4] == "stick"
                    (stick_logits if stick else negate)(n)
                    if n > n0:
                        write_out(n - 1)
                    advance(beside[n])
                    if stick:
                        stick_sums(n)
                copy_probs(n1 - 1)
                write_out(n1 - 1)

            def gate_heads(zz, pairs):
                gated[0] += 1
                dve.wait_ge(out_written, 16 * gated[0])
                all_drained(dve, L0_OUT if gated[0] == 1 else L1_OUT)
                for g, y, width in pairs:
                    i = V.tensor_tensor(zz[:, :, g:g + width], zz[:, :, g:g + width], zz[:, :, y:y + width], ALU.mult)
                i.then_inc(y_ready, 1)

            gated = [0]

            splits(0, 0, 2)
            dve.wait_ge(const_landed, ALL_CONST)
            reciprocal_root()
            x_stage("n0", "n0")
            advance(4)
            advance(4)
            run(L0_QKV + 2, 7)
            advance(4)
            all_drained(dve, L0_GATE)
            rot = [(c0, n, step, half, tab) for c0, n, step, half, tab in (
                (IQ, 12, 64, 32, rope64), (IQ + 12 * 64, 5, 64, 32, rope64), (QA, 6, 128, 64, rope128),
                (QA + 6 * 128, 5, 128, 64, rope128), (QB, 6, 128, 64, rope128), (KB, 6, 128, 64, rope128))]
            assert len(rot) * NT == ROT_STEPS
            n = 0
            for c0, k, step, half, tab in rot:
                for tt in range(NT):
                    rotate(z0, tt, c0, k, step, half, tab[:, 0, tt, :], tab[:, 1, tt, :])
                    advance(beside_rot[n])
                    n += 1
            link(V.tensor_scalar(idx_w, z0[:, :, IW:IW + 16], 0.25, None, ALU.mult))
            for m in range(2):
                i = V.tensor_copy(ik_twice[:, :, 64 * m:64 * m + 64], z0[:, :, IK:IK + 64])
            i.then_inc(rotated, 1)
            score = rest_b
            for h in range(16):
                dve.wait_ge(relu_ready, h + 1)
                for tt in range(NT):
                    s, r, w = score[:, keys_of[tt]], neg[:, h % 2, keys_of[tt]], idx_w[:, tt, h:h + 1]
                    if h == 0:
                        i = V.tensor_scalar(s, r, w, None, ALU.mult)
                    else:
                        if tt == 0:
                            dve.wait_ge(scored, h)
                        i = V.scalar_tensor_tensor(s, r, w, s, ALU.mult, ALU.add)
                i.then_inc(scored, 1)
                if h % 2:
                    advance(beside_idx[h // 2])
            dve.wait_ge(scored, 16)
            link(V.tensor_tensor(score, score, causal[:], ALU.subtract))
            for _ in range(8):
                for tt in range(NT):
                    i = V.max(best8[:, tt, :], score[:, keys_of[tt]])
                link(i)
                for tt in range(NT):
                    i = V.match_replace(score[:, keys_of[tt]], best8[:, tt, :], score[:, keys_of[tt]], TAKEN)
                link(i)
            link(V.tensor_scalar(rest_a[:, 0:384], score, TAKEN / 2, BIG, ALU.is_gt, ALU.mult))
            V.tensor_tensor(rest_a[:, 0:384], rest_a[:, 0:384], causal[:], ALU.add).then_inc(scored, 1)
            dve.wait_ge(scored, 17)
            heads(0, 16)
            gate_heads(z0, ((G0, QA, 1280), (G0 + 1280, QB, 768)))
            x_stage("y0", None)
            advance(16)

            reciprocal_root()
            x_stage("n1", "n1")
            advance(8)
            run(L1_QKV + 2, 10)

            def forget_gates():
                dve.wait_ge(gate_tanh, gate_no[L1_GATE])
                b = forget_b.unsqueeze(1).to_broadcast([P, NT, 8])
                V.tensor_tensor(forget_x, z1[:, :, FL:FL + 8], b, ALU.add).then_inc(made["forget_sum"], 1)
                dve.wait_ge(made["forget_ln"], 1)
                link(V.tensor_scalar(forget_x, forget_x, -1.0, 0.0, ALU.mult, ALU.max))
                link(V.tensor_tensor(forget_x, forget_x, forget_e, ALU.add))
                V.tensor_scalar(neg_log_f, forget_x, 1.0 / SCALE, None, ALU.mult).then_inc(made["forget_ln"], 1)

            dve.wait_ge(strict_landed, 16)
            heads(16, 24)
            forget_gates()
            heads(24, 32)
            gate_heads(z1, ((G1, QC, 1024), (G1 + 1024, QD, 1024)))
            x_stage("y1", None)
            advance(16)
            reciprocal_root()
            dve.wait_ge(rstd_ready, norms[0])
            dve.wait_ge(grow_landed, 16)
            for tt in range(NT):
                i = V.scalar_tensor_tensor(res[:, tt, :], res[:, tt, :], rstd[:, tt:tt + 1], grow, ALU.mult, ALU.mult)
            i.then_inc(res_ready, 1)

            def feed_forward(b, no, name, hname, factor_no):
                u0 = first_unit[b]
                h0 = no * FB
                reciprocal_root()
                V.memset(out2, 0.0).then_inc(added, 1)
                x_stage(name, name)
                dve.wait_ge(added, added_before(no))

                def hidden_lo(i):
                    for s in range(2):
                        dve.wait_ge(st_hi, i * 2 + (turned_before[hname] + s + 1))
                        V.tensor_tensor(h_lo[:, :, s * P:(s + 1) * P],
                                        ps[:, 6 + s, :].rearrange("p (k n) -> p k n", k=UC),
                                        h_hi[:, :, s * P:(s + 1) * P].bitcast(F32), ALU.subtract).then_inc(st_done, 1)

                def product(u, i):
                    dve.wait_ge(ff_tanh, i + (h0 + 1))
                    dve.wait_ge(parts_used, u + 8)
                    V.scalar_tensor_tensor(silu, silu, 1.0, ps[:, 0:2, :], ALU.add, ALU.mult).then_inc(ff_silu, 1)
                    dve.wait_ge(ff_silu, i + (h0 + 1))
                    V.scalar_tensor_tensor(hid, silu, 0.5, ps[:, 2:4, :], ALU.mult, ALU.mult).then_inc(hid_ready, 1)

                def down_added(u, i, j):
                    dve.wait_ge(parts_used, u + (j + 1))
                    bank = 4 + 2 * (j % 2)
                    o = out2[:, :, j * BW:(j + 1) * BW]
                    V.tensor_tensor(o, o, ps[:, bank:bank + 2, :], ALU.add).then_inc(added, 1)

                splits(u0 + 2, 2, 4)
                splits(u0 + 6, 2, 4)
                product(u0, 0)
                with dve.Fori(0, FB - 1) as i:
                    u = i * 12 + (u0 + 8)
                    splits(u + 2, 2, 4)
                    hidden_lo(i)
                    splits(u + 6, 2, 4)
                    product(u, i + 1)
                    for j in range(4):
                        splits(u + (10 + j), 2 + j, 1)
                        down_added(u + 8, i, j)
                u = u0 + 12 * FB - 4
                hidden_lo(FB - 1)
                for j in range(4):
                    splits(u + 2 + j, 2 + j, 1)
                    down_added(u, FB - 1, j)
                at[0] = u0 + 12 * FB
                add_normed(factor_no, 0.5)

            feed_forward(FF1, 0, "ff1", "h1", 2)

            reciprocal_root()
            x_stage("mix", "mix")
            link(V.tensor_copy(pos_f, position[:]))
            for tt in range(NT):
                i = V.tensor_scalar(ang[:, tt, :], cols[:, INV:INV + 16], pos_f[:, tt:tt + 1], None, ALU.mult)
            link(i)
            link(V.tensor_scalar(cyc, ang, float(np.float32(0.5 / np.pi)), ROUND, ALU.mult, ALU.add))
            link(V.tensor_scalar(cyc, cyc, ROUND, None, ALU.subtract))
            for part in TWO_PI:
                link(V.scalar_tensor_tensor(ang, cyc, -part, ang, ALU.mult, ALU.add))
            half_pi = float(np.float32(np.pi / 2))
            link(V.tensor_scalar(cyc, ang, half_pi, -2 * float(np.float32(np.pi)), ALU.is_gt, ALU.mult))
            link(V.scalar_tensor_tensor(turn_tab[:, 0], ang, half_pi, cyc, ALU.add, ALU.add))
            link(V.tensor_copy(turn_tab[:, 1], ang))
            pi = float(np.nextafter(np.float32(np.pi), np.float32(0)))
            V.tensor_scalar(turn_tab, turn_tab, pi, -pi, ALU.min, ALU.max).then_inc(made["angle_ready"], 1)
            V.tensor_scalar(half_ba, cols[:, BA:BA + 8], 0.5, None, ALU.mult)
            V.tensor_scalar(half_bi, cols[:, BI:BI + 8], 0.5, None, ALU.mult)
            dve.wait_ge(made["lam_exp"], 1)
            link(V.tensor_scalar(lam_s, lam_x, 2.0, None, ALU.add))
            link(V.reciprocal(lam_s, lam_s))
            link(V.tensor_tensor(lam_s, lam_s, lam_x, ALU.mult))
            link(V.tensor_tensor(lam_s2, lam_s, lam_s, ALU.mult))
            link(V.tensor_scalar(lam_q, lam_s2, 1.0 / 17, None, ALU.mult))
            for odd in (15, 13, 11, 9, 7, 5, 3):
                link(V.scalar_tensor_tensor(lam_q, lam_q, 1.0 / odd, lam_s2, ALU.add, ALU.mult))
            link(V.scalar_tensor_tensor(lam_q, lam_q, 1.0, lam_s, ALU.add, ALU.mult))
            link(V.tensor_scalar(lam_s, cols[:, LAM:LAM + 8], -1.0, 0.0, ALU.mult, ALU.max))
            link(V.scalar_tensor_tensor(lam_s, lam_q, 2.0, lam_s, ALU.mult, ALU.add))
            link(V.tensor_scalar(m4sp, lam_s, -4.0, None, ALU.mult))
            V.memset(r_pad[:, :, 0:3], 0.0)
            advance(20)
            dve.wait_ge(made["rec_padded"], 1)
            for tap in range(4):
                for b in range(LB):
                    w = cols[:, CONV + 8 * tap + b:CONV + 8 * tap + b + 1]
                    src, dst = r_pad[:, b, tap:tap + SEQ], by_block(r1)[:, b, :]
                    if tap == 0:
                        i = V.tensor_scalar(dst, src, w, cols[:, CONVB + b:CONVB + b + 1], ALU.mult, ALU.add)
                    else:
                        i = V.scalar_tensor_tensor(dst, src, w, dst, ALU.mult, ALU.add)
                if tap < 3:
                    link(i)
            i.then_inc(made["rec_conv"], 1)
            dve.wait_ge(made["rec_r_tanh"], 1)
            for b in range(LB):
                i = V.tensor_scalar(by_block(r2)[:, b, :], by_block(r2)[:, b, :], m4sp[:, b:b + 1], m4sp[:, b:b + 1],
                                    ALU.mult, ALU.add)
            i.then_inc(made["rec_log_a"], 1)
            dve.wait_ge(made["rec_a"], 1)
            link(V.tensor_tensor(r2, r3, r3, ALU.mult))
            V.scalar_tensor_tensor(r2, r2, 1.0, r0, ALU.add, ALU.mult).then_inc(made["rec_square"], 1)
            dve.wait_ge(made["rec_i_tanh"], 1)
            link(V.scalar_tensor_tensor(r4, r4, 1.0, r1, ALU.add, ALU.mult))
            dve.wait_ge(made["rec_root"], 1)
            link(V.scalar_tensor_tensor(r4, r4, 0.5, r2, ALU.mult, ALU.mult))
            for b in range(LB):
                i = V.tensor_tensor_scan(by_block(r0)[:, b, :], by_block(r3)[:, b, :], by_block(r4)[:, b, :], 0.0,
                                         ALU.mult, ALU.add)
            link(i)
            dve.wait_ge(made["rec_y_gelu"], 1)
            link(V.tensor_tensor(r1, r0, work[:, 0:2048], ALU.mult))
            V.tensor_tensor(r2, r1, r1, ALU.mult).then_inc(made["rec_out_squared"], 1)
            advance(20)
            all_drained(dve, CMP)
            dve.wait_ge(made["rec_norm_root"], 1)
            link(V.reciprocal(r0[:, SEQ:2 * SEQ], r0[:, 0:SEQ]))
            link(V.tensor_tensor(by_block(r1), by_block(r1),
                                 r0[:, SEQ:2 * SEQ].unsqueeze(1).to_broadcast([P, LB, SEQ]), ALU.mult))
            V.tensor_tensor(by_block(r1), by_block(r1),
                            cols[:, GAIN["rec"]:GAIN["rec"] + LB].unsqueeze(2).to_broadcast([P, LB, SEQ]),
                            ALU.mult).then_inc(made["rec_ready"], 1)
            dve.wait_ge(made["angle_sin"], 1)
            for c0, k in ((ZQ, 10), (ZKS, 2), (ZKW, 2)):
                for tt in range(NT):
                    rotate(z2, tt, c0, k, HD, 16, turn_tab[:, 0, tt, :], turn_tab[:, 1, tt, :],
                           rotated if c0 == ZKW and tt == NT - 1 else None)
            dve.wait_ge(made["rec_hi"], 1)
            V.tensor_tensor(x_lo[:, LB:2 * LB, :], by_block(r1), x_hi[:, LB:2 * LB, :].bitcast(F32),
                            ALU.subtract).then_inc(made["rec_lo"], 1)
            link(V.memset(work[:, 0:2048], 0.0))
            for m, pos in enumerate((POSK, POSV)):
                dve.wait_ge(made["cmp_turned"], m + 1)
                x = cmp_x[m].rearrange("p (l g c) -> p l g c", l=32, g=2)
                for g in range(2):
                    for half in range(2):
                        src = ps[:, 4 + m, g * SEQ:(g + 1) * SEQ].rearrange("p (c l) -> p l c", l=16)
                        i = V.tensor_tensor(
                            x[:, 16 * half:16 * half + 16, g, 0:NCMP], src[:, :, half:half + NCMP],
                            cols[:, pos + 16 * half:pos + 16 * half + 16].unsqueeze(2).to_broadcast([P, 16, NCMP]),
                            ALU.add)
                i.then_inc(made["cmp_summed"], 1)
            bias = gate_bias.unsqueeze(1).to_broadcast([P, NT, 24])
            V.tensor_tensor(nsa_gates, z2[:, :, ZG:ZG + 24], bias, ALU.add).then_inc(made["nsa_gate_sum"], 1)
            xf = [x[:].rearrange("p k s -> p (k s)") for x in (x_hi, x_lo)]
            for m in range(2):
                dve.wait_ge(made["cmp_hi"], m + 1)
                V.tensor_tensor(xf[1][:, 1024 * m:1024 * (m + 1)], cmp_x[m],
                                xf[0][:, 1024 * m:1024 * (m + 1)].bitcast(F32), ALU.subtract
                                ).then_inc(made["cmp_lo"], 1)
            dve.wait_ge(made["nsa_gate_tanh"], 1)
            link(V.tensor_scalar(nsa_gates, nsa_gates, 0.5, 0.5, ALU.mult, ALU.add))
            advance(8)
            heads(32, 48)
            cl = cmp_logits.rearrange("p (h c) -> p h c", c=NCMP)
            away = rest_a[:, 0:240]
            link(V.tensor_scalar(away, cmp_ok[:], -BIG, BIG, ALU.mult, ALU.add))
            link(V.scalar_tensor_tensor(cmp_logits, cmp_logits, -SCALE, away, ALU.mult, ALU.add))
            link(V.tensor_reduce(cmp_low, cl, AX_X, ALU.min))
            V.tensor_tensor(cl, cl, cmp_low.unsqueeze(2).to_broadcast([P, 16, NCMP]),
                            ALU.subtract).then_inc(made["cmp_negated"], 1)
            dve.wait_ge(made["cmp_probs"], 1)
            cp = rest_a[:, 240:480]
            link(V.tensor_reduce(cmp_sum, cp.rearrange("p (h c) -> p h c", c=NCMP), AX_X, ALU.add))
            link(V.reciprocal(cmp_sum, cmp_sum))
            gates0 = nsa_gates.rearrange("p t (h j) -> p h t j", j=3)[:, :, :, 0]
            cs = cmp_sum.rearrange("p (h t) -> p h t", t=NT)
            link(V.tensor_tensor(cs, cs, gates0, ALU.mult))
            V.tensor_tensor(cp, cp, cmp_ok[:], ALU.mult).then_inc(made["cmp_weighted"], 1)
            for h in range(8):
                dve.wait_ge(made["cmp_mixed"], h + 1)
                for tt in range(NT):
                    dst = o_attn[:, tt, h * HD:(h + 1) * HD]
                    i = V.scalar_tensor_tensor(dst, ps[:, 6, tt * HD:(tt + 1) * HD], cs[:, h, tt:tt + 1], dst,
                                               ALU.mult, ALU.add)
                i.then_inc(made["cmp_added"] if h < 7 else y_ready, 1)
            reciprocal_root()
            x_stage("attn", "attn", 4)
            advance(16)
            add_normed(3, 1.0)
            feed_forward(FF2, 1, "ff2", "h2", 4)
            reciprocal_root()
            x_stage("ple", "ple")
            advance(16)
            for s in range(2):
                dve.wait_ge(st_hi, turned_before["p"] + s + 1)
                V.tensor_tensor(h_lo[:, 0:2, s * P:(s + 1) * P],
                                ps[:, 6 + s, 0:2 * P].rearrange("p (k n) -> p k n", k=2),
                                h_hi[:, 0:2, s * P:(s + 1) * P].bitcast(F32), ALU.subtract).then_inc(st_done, 1)
            advance(4)
            add_normed(5, 0.5)


_WEIGHTS = {"w_in0": "w_in0", "w_out0": "w_out0", "w_in1": "w_in1", "w_out1": "w_out1", "w_in_2": "w_in_2",
            "w_out_2": "w_out_2", "w_ple_gate_2": "w_ple_gate_2", "w_ple_proj_2": "w_ple_proj_2",
            "ff1_w_gate": "ff1_w_gate_2", "ff1_w_up": "ff1_w_up_2", "ff1_w_down": "ff1_w_down_2",
            "ff2_w_gate": "ff2_w_gate_2", "ff2_w_up": "ff2_w_up_2", "ff2_w_down": "ff2_w_down_2",
            "rg_w_a": "rg_w_a_2", "rg_w_i": "rg_w_i_2", "cmp_k_w1": "cmp_k_w1_2", "cmp_v_w1": "cmp_v_w1_2",
            "cmp_k_w2": "cmp_k_w2_2", "cmp_v_w2": "cmp_v_w2_2"}


def kernel(**inputs):
    import concourse.bacc as bacc
    from concourse.bass_utils import run_bass_kernel_spmd as run

    g = {n: np.asarray(a) for n, a in inputs.items()}
    arrays = {}
    for name, source in _WEIGHTS.items():
        a = g[source]
        arrays[name] = a.reshape(a.shape[1:]) if source[-2:] == "_2" else a

    def by_columns(v):
        return v.reshape(-1, P).T

    const = constants()
    arrays["x"] = g["x"].reshape(SEQ, D)
    arrays["p"] = g["p_2"].reshape(SEQ, -1)
    arrays["positions"] = g["positions_2"].reshape(NT, P).T.astype(np.int32)
    arrays["rows"] = np.stack([g["norm_f"], g["ff1_post_g_2"][0], g["mix_post_g_2"][0], g["ff2_post_g_2"][0],
                               g["ple_post_g_2"][0]])
    arrays["cols"] = np.concatenate(
        [by_columns(v) for v in (g["norm0"], g["norm1"], g["ff1_pre_g_2"][0], g["mix_pre_g_2"][0],
                                 g["attn_out_g_2"][0], g["rec_out_g_2"][0], g["ff2_pre_g_2"][0],
                                 g["ple_pre_g_2"][0])]
        + [by_columns(g["conv_w_2"][0][k]) for k in range(4)]
        + [by_columns(g[n][0]) for n in ("conv_b_2", "rg_b_a_2", "rg_b_i_2", "rg_lambda_2")]
        + [const.pop("inv"), g["cmp_pos_k_2"][0].T, g["cmp_pos_v_2"][0].T], axis=1)
    arrays["b_f1"] = g["b_f1"].reshape(1, 8)
    arrays["nsa_gate_b"] = g["nsa_gate_b_2"].reshape(1, 24)
    arrays.update(const)
    arrays = {n: np.ascontiguousarray(a) for n, a in arrays.items()}

    nc = bacc.Bacc("TRN2", target_bir_lowering=False, num_devices=1)
    t = {n: nc.dram_tensor(f"in_{n}", a.shape, mybir.dt.from_np(a.dtype), kind="ExternalInput").ap()
         for n, a in arrays.items()}
    t["out"] = nc.dram_tensor("result", (SEQ, D), F32, kind="ExternalOutput").ap()
    for n in ("x", "p", "out"):
        t[n] = t[n].rearrange("(t p) d -> p t d", p=P)
    build(nc, t)
    r = run(nc, [{f"in_{n}": a for n, a in arrays.items()}], core_ids=[0])
    return r.results[0]["result"].reshape(1, SEQ, D)
```

```python
from contextlib import ExitStack

import numpy as np

import concourse.bass as bass
from concourse import mybir

F32 = mybir.dt.float32
F32R = mybir.dt.float32r
I32 = mybir.dt.int32
ACT = mybir.ActivationFunctionType
ALU = mybir.AluOpType
AX_X = mybir.AxisListType.X

P = 128
SEQ = 256
NT = SEQ // P
D = 2048
KC = D // P
BW = 512
UC = 4
UNIT = UC * BW
RAW = 4
PARTS = 2
DFF = 5632
FB = DFF // BW
HD = 128
BIG = 1.0e30
TAKEN = -2.0e38
EPS = 1e-6
SCALE = HD ** -0.5
LRU = 1024
LB = LRU // P
TWO_PI = (6.28125, 0.0019350051879882812, 2 * np.pi - 6.28125 - 0.0019350051879882812)
ROUND = 12582912.0

QA, KA, VA, IQ, IK, IW, QB, KB, VB, G0 = 0, 1280, 1408, 1536, 2560, 2624, 2640, 3408, 4176, 4944
W0 = 6992
QC, KCC, VC, QD, KD, VD, FL, G1 = 0, 1024, 2048, 3072, 4096, 5120, 6144, 6152
W1 = 8200
ZQ, ZKC, ZVC, ZKS, ZVS, ZKW, ZVW, ZG, ZX, ZY = 0, 1024, 1280, 1536, 1792, 2048, 2304, 2560, 2584, 3608
W2 = 4632
NCMP = (SEQ - 32) // 16 + 1


def constants():
    c = {}
    c["ident"] = np.eye(P, dtype=np.float32)
    pos = np.arange(SEQ, dtype=np.float32)

    def tables(half):
        inv = (np.float32(10000.0) ** (-np.arange(half, dtype=np.float32) / np.float32(half))).astype(np.float32)
        ang = (pos[:, None] * inv[None, :]).astype(np.float32).astype(np.float64)
        both = np.stack([np.cos(ang), np.sin(ang)], 1).astype(np.float32)
        return both.reshape(NT, P, 2, half).transpose(1, 2, 0, 3).reshape(P, 2 * NT * half)

    c["rope128"] = tables(64)
    c["rope64"] = tables(32)
    q = np.arange(SEQ)[:, None]
    k = np.arange(SEQ)[None, :]

    def keys(full):
        return np.concatenate([full[0:P, 0:P], full[P:SEQ, :]], 1).astype(np.float32)

    c["causal"] = keys(np.where(k <= q, 0.0, BIG))
    c["strict"] = keys(np.where(k < q, 0.0, BIG))
    d = q - k
    n = ((d >= 0) & (d <= 128)).astype(int) + ((d >= 0) & (d % 4 == 0)) + ((d >= 0) & (d % 16 == 0))
    c["dilated"] = keys(np.where(n > 0, -np.log(np.maximum(n, 1).astype(np.float64)), BIG))
    c["upto"] = (q <= k).astype(np.float32).reshape(NT, P, SEQ).transpose(1, 0, 2).reshape(P, NT * SEQ)
    end = np.arange(NCMP) * 16 + 31
    ok = (end[None, :] <= q).astype(np.float32).reshape(NT, P, NCMP).transpose(1, 0, 2)
    c["cmp_ok"] = np.repeat(ok[:, None], 8, 1).reshape(P, 8 * NT * NCMP)
    inv = (np.float32(500000.0) ** (-np.arange(16, dtype=np.float32) / np.float32(16))).astype(np.float32)
    c["inv"] = np.tile(inv[None, :], (P, 1))
    return {n: np.ascontiguousarray(a, dtype=np.float32) for n, a in c.items()}


def build(nc, t):
    blocks = []

    def plan(w, c0, widths, chunks=KC):
        first = len(blocks)
        for width in widths:
            u = blocks[-1][0] + len(blocks[-1][4]) if blocks else 0
            blocks.append((u, w, c0, width, [(k, min(UC, chunks - k)) for k in range(0, chunks, UC)]))
            c0 += width
        return first

    def plan_other(units):
        blocks.append((blocks[-1][0] + len(blocks[-1][4]), None, 0, 0, [None] * units))
        return len(blocks) - 1

    L0_QKV = plan(t["w_in0"], 0, [BW] * 9 + [G0 - 9 * BW])
    L0_GATE = plan(t["w_in0"], G0, [BW] * 4)
    L0_OUT = plan(t["w_out0"], 0, [BW] * 4)
    L1_QKV = plan(t["w_in1"], 0, [BW] * 12)
    L1_GATE = plan(t["w_in1"], FL, [BW] * 3 + [260, 260])
    L1_OUT = plan(t["w_out1"], 0, [BW] * 4)
    FF1 = plan_other(12 * FB)
    MIX_REC = plan(t["w_in_2"], ZG, [BW] * 3 + [268, 268])
    MIX_QKV = plan(t["w_in_2"], 0, [BW] * 5)
    CMP = plan_other(4)
    plan_other(4)
    MIX_OUT = plan(t["w_out_2"], 0, [BW] * 4)
    FF2 = plan_other(12 * FB)
    PLE_GATE = plan(t["w_ple_gate_2"], 0, [BW] * 4)
    PLE_PROJ = plan(t["w_ple_proj_2"], 0, [BW] * 4, 2)
    N_UNITS = blocks[-1][0] + 1
    first_unit = [b[0] for b in blocks]
    pair_of, drains_before, drains = {}, {}, [0, 0]
    for b in range(len(blocks)):
        if b not in (FF1, FF2):
            pair_of[b] = sum(drains) % 2
            drains_before[b] = drains[pair_of[b]]
            drains[pair_of[b]] += 1
    block_of = {}
    for b, blk in enumerate(blocks):
        for n in range(len(blk[4])):
            block_of[blk[0] + n] = (b, n)

    turned_before, gained_before, n_turned, n_gained = {}, {}, 0, 0
    for name, steps, normed in (("n0", 8, True), ("y0", 8, False), ("n1", 8, True), ("y1", 8, False),
                                ("ff1", 8, True), ("h1", 2 * FB, False), ("mix", 8, True), ("attn", 4, True),
                                ("ff2", 8, True), ("h2", 2 * FB, False), ("ple", 8, True), ("p", 2, False)):
        turned_before[name], gained_before[name] = n_turned, n_gained
        n_turned += steps
        n_gained += steps if normed else 0

    with ExitStack() as ctx:
        def sb(name, shape, dt=F32):
            return ctx.enter_context(nc.sbuf_tensor(name, shape, dt))

        def sem(name):
            return ctx.enter_context(nc.semaphore(name))

        res = sb("res", [P, NT, D])
        raw = sb("raw", [P, RAW, UNIT])
        w_hi = sb("w_hi", [P, PARTS, UNIT], F32R)
        w_lo = sb("w_lo", [P, PARTS, UNIT], F32R)
        x_hi = sb("x_hi", [P, KC, SEQ], F32R)
        x_lo = sb("x_lo", [P, KC, SEQ], F32R)
        ident = sb("ident", [P, P])
        ones = sb("ones", [P, P])
        causal = sb("causal", [P, 3 * P])
        other_mask = sb("other_mask", [P, 3 * P])
        upto = sb("upto", [P, NT, SEQ])
        rope128 = sb("rope128", [P, 2, NT, 64])
        rope64 = sb("rope64", [P, 2, NT, 32])
        cols = sb("cols", [P, 256])
        st = sb("st", [P, 416])
        cmp_ok = sb("cmp_ok", [P, 8 * NT * NCMP])
        position = sb("position", [P, NT], I32)
        z = sb("z", [P, 2 * W1])
        with nc.sbuf_tensor("work", [P, 4096], F32) as work:
            pass
        scaled = sb("scaled", [P, 2, BW])
        gained = sb("gained", [P, 2, UC, P])
        h_hi = sb("h_hi", [P, UC, SEQ], F32R)
        h_lo = sb("h_lo", [P, UC, SEQ], F32R)
        ps = ctx.enter_context(nc.psum_tensor("ps", [P, 8, BW], F32))

        z0 = z[:, 0:2 * W0].rearrange("p (t n) -> p t n", t=NT)
        z1 = z[:, 0:2 * W1].rearrange("p (t n) -> p t n", t=NT)
        z2 = z[:, 0:2 * W2].rearrange("p (t n) -> p t n", t=NT)
        rot_a, rot_b = z[:, 13984:14752], z[:, 14752:15520]
        ik_twice = z[:, 15520:15776].rearrange("p (t n) -> p t n", t=NT)
        grow = z[:, 12288:14336]
        out2 = z[:, 2048:6144].rearrange("p (t n) -> p t n", t=NT)
        silu = z[:, 0:1024].rearrange("p (t n) -> p t n", t=NT)
        hid = z[:, 1024:2048].rearrange("p (t n) -> p t n", t=NT)
        ple_gate = z[:, 6144:10240].rearrange("p (t n) -> p t n", t=NT)
        p_in = z[:, 10240:10752].rearrange("p (t n) -> p t n", t=NT)
        qkT = work[:, 0:1024].rearrange("p (b n) -> p b n", b=2)
        neg = work[:, 1024:1792].rearrange("p (b n) -> p b n", b=2)
        prob = work[:, 1792:2560].rearrange("p (b n) -> p b n", b=2)
        probT = work[:, 2560:2944]
        rest_a = work[:, 2944:3456]
        rest_b = work[:, 3456:3840]
        GAIN = {"n0": 0, "n1": 16, "ff1": 32, "mix": 48, "attn": 64, "rec": 72, "ff2": 80, "ple": 96}
        CONV, CONVB, BA, BI, LAM, INV, POSK, POSV = 112, 144, 152, 160, 168, 176, 192, 224
        m4sp = st[:, 0:8]
        ssq, root, rstd, half_rstd, half_square = (st[:, o:o + 2] for o in (8, 10, 12, 14, 28))
        output_rstd, first_rstd, next_factor, next_mean = (st[:, o:o + 2] for o in (30, 178, 180, 182))
        post_ssq, next_ssq, small = (st[:, o:o + 8].rearrange("p (t j) -> p t j", t=NT) for o in (336, 344, 184))
        ff_weighted = z[:, 6144:10240].rearrange("p (t n) -> p t n", t=NT)
        last_weighted = [z[:, o:o + 2 * BW].rearrange("p (t n) -> p t n", t=NT) for o in (0, 1024, 10752, 14336)]
        low = st[:, 16:20].rearrange("p (b n) -> p b n", b=2)
        total = st[:, 20:24].rearrange("p (b n) -> p b n", b=2)
        inv = st[:, 24:26]
        share = st[:, 26:28]
        neg_log_f = st[:, 32:48].rearrange("p (t h) -> p t h", t=NT)
        forget_b, gate_bias = st[:, 48:56], st[:, 56:80]
        nsa_gates = st[:, 80:128].rearrange("p (t h) -> p t h", t=NT)
        best8 = st[:, 128:144].rearrange("p (t n) -> p t n", t=NT)
        idx_w = st[:, 144:176].rearrange("p (t n) -> p t n", t=NT)
        pos_f = st[:, 176:178]
        turn_tab = st[:, 192:256].rearrange("p (c t n) -> p c t n", c=2, t=NT)
        ang, cyc = (st[:, o:o + 32].rearrange("p (t n) -> p t n", t=NT) for o in (256, 288))
        half_ba, half_bi = st[:, 320:328], st[:, 328:336]
        lam_x, lam_s, lam_s2, lam_q = (st[:, o:o + 8] for o in (352, 360, 368, 376))
        forget_x, forget_e = (st[:, o:o + 16].rearrange("p (t h) -> p t h", t=NT) for o in (384, 400))
        r_pad = z[:, 9264:9264 + LB * 259].rearrange("p (b n) -> p b n", b=LB)
        r0, r1, r2 = z[:, 9264:11312], z[:, 11336:13384], z[:, 13384:15432]
        r3, r4 = z[:, ZX:ZX + 2 * LRU], z[:, W2 + ZX:W2 + ZX + 2 * LRU]
        rg = work[:, 2048:4096].rearrange("p (m b j) -> p m b j", m=2, b=LB)
        by_block = lambda a: a.rearrange("p (b n) -> p b n", b=LB)
        o_attn = r2.rearrange("p (t n) -> p t n", t=NT)
        cmp_w2 = z[:, 15432:15944].rearrange("p (m k n) -> p m k n", m=2, k=2)
        cmp_kT = z[:, 15944:15976]
        cmp_v = z[:, 15976:16232].rearrange("p (g n) -> p g n", g=2)
        cmp_x = [work[:, 1024 * m:1024 * m + 1024] for m in range(2)]
        cmp_hid = [work[0:32, 2048 + 256 * m:2304 + 256 * m] for m in range(2)]
        cmp_hidT = [work[:, 2560 + 64 * m:2624 + 64 * m] for m in range(2)]
        cmp_logits = work[:, 3456:3696]
        cmp_low = work[:, 3696:3712]
        cmp_sum = work[:, 3712:3728]

        x_landed = [sem(f"x_landed_{g}") for g in range(4)]
        const_landed = sem("const_landed")
        raw_landed = [sem(f"raw_landed_{j}") for j in range(RAW)]
        hi_ready = sem("hi_ready")
        parts_ready = sem("parts_ready")
        parts_used = sem("parts_used")
        drained = [sem("even_drained"), sem("odd_drained")]
        st_scaled, st_turned, st_gained, st_hi, st_done = (
            sem(n) for n in ("chunks_scaled", "chunks_turned", "chunks_gained", "chunks_hi", "chunks_done"))
        root_ready, rstd_ready = sem("root_ready"), sem("rstd_ready")
        act_chain, dve_chain = sem("act_chain"), sem("dve_chain")
        res_ready = sem("res_ready")
        gate_tanh = sem("gate_tanh")
        idx_turned, idx_copied, dots_ready, relu_ready, scored = (
            sem(n) for n in ("idx_turned", "idx_copied", "dots_ready", "relu_ready", "scored"))
        rotated = sem("rotated")
        qk_turned, qk_copied, logits_ready, negated, probs_ready, probs_turned, probs_copied, mixed, out_written = (
            sem(n) for n in ("qk_turned", "qk_copied", "logits_ready", "negated", "probs_ready", "probs_turned",
                             "probs_copied", "mixed", "out_written"))
        softplus_ready, arg_ready = sem("softplus_ready"), sem("arg_ready")
        first_landed, group_gated = sem("first_constants_landed"), sem("group_gated")
        grow_used, res_updated, res_gained, first_squared, output_squared = (
            sem(n) for n in ("grow_used", "res_updated", "res_gained", "first_squared", "output_squared"))
        ff_tanh, ff_silu, hid_ready, added = (sem(n) for n in ("ff_tanh", "ff_silu", "hid_ready", "added"))
        strict_landed, p_landed, mix_landed = sem("strict_landed"), sem("p_landed"), sem("mix_landed")
        y_ready = sem("y_ready")
        grow_landed = sem("grow_landed")
        out_landed = sem("out_landed")

        block = ctx.enter_context(nc.Block())

        made = {n: sem(n) for n in (
            "rec_x_turned", "rec_y_turned", "rec_padded", "rec_y_gelu", "rec_conv", "rec_r_product", "rec_r_tanh",
            "rec_log_a", "rec_a", "rec_i_product", "rec_i_tanh", "rec_square", "rec_root", "rec_out_squared",
            "rec_summed", "rec_norm_root", "rec_ready", "rec_hi", "rec_lo", "lam_exp",
            "cmp_turned", "cmp_summed", "cmp_hi", "cmp_lo", "cmp_hid_turned", "cmp_hidT_ready", "cmp_kv_made",
            "cmp_kv_ready", "cmp_negated", "cmp_probs", "cmp_weighted", "cmp_p_turned", "cmp_p_copied", "cmp_mixed",
            "cmp_added", "angle_ready", "angle_sin", "nsa_gate_sum", "nsa_gate_tanh", "forget_sum", "forget_ln",
            "cmp_cleared", "const_made")}
        drain_kind = {}
        gate_no = {}
        for b in range(len(blocks)):
            if b < L0_GATE or L1_QKV <= b < L1_GATE or MIX_REC <= b < CMP:
                drain_kind[b] = "copy"
            elif MIX_OUT <= b < FF2:
                drain_kind[b] = "output"
            elif b < L0_OUT or L1_GATE <= b < L1_OUT:
                gate_no[b] = len(gate_no) + 1
                drain_kind[b] = "gate"
            elif b < L1_QKV or L1_OUT <= b < FF1:
                drain_kind[b] = "residual"
            elif CMP <= b < MIX_OUT:
                drain_kind[b] = "gelu"
            elif PLE_GATE <= b < PLE_PROJ:
                drain_kind[b] = "tanh"
            elif b >= PLE_PROJ:
                drain_kind[b] = "gated"

        def place_of(b):
            _, _, c0, width, _ = blocks[b]
            if b < L0_OUT:
                return z0[:, :, c0:c0 + width]
            if L1_QKV <= b < L1_OUT:
                return z1[:, :, c0:c0 + width]
            if MIX_REC <= b < CMP:
                return z2[:, :, c0:c0 + width]
            if MIX_OUT <= b < FF2 or b >= PLE_PROJ:
                return out2[:, :, c0:c0 + width]
            if b >= PLE_GATE:
                return ple_gate[:, :, c0:c0 + width]
            return res[:, :, c0:c0 + width]

        def added_before(no):
            return no * (4 * FB + 1) + 1

        def summed(b):
            return ps[:, 2 * pair_of[b]:2 * pair_of[b] + 2, 0:blocks[b][3]]

        def each(eng, count, body):
            pairs = count // 2
            if pairs >= 3:
                with eng.Fori(0, pairs) as i:
                    for r in range(2):
                        body(i * 2 + r, i, r)
            else:
                for n in range(2 * pairs):
                    body(n, n // 2, n % 2)
            for n in range(2 * pairs, count):
                body(n, n // 2, n % 2)

        def unit_size(u):
            return 2 * BW if isinstance(u, int) and u >= first_unit[PLE_PROJ] else UNIT

        def drained_before(b, pair):
            return sum(1 for x in pair_of if x < b and pair_of[x] == pair)

        def all_drained(eng, b):
            for pair in range(2):
                eng.wait_ge(drained[pair], drained_before(b, pair))

        jobs = []
        for h in range(10):
            jobs.append((z0, QA + h * HD, KA, VA, "sparse"))
        for h in range(6):
            jobs.append((z0, QB + h * HD, KB + h * HD, VB + h * HD, "dilated"))
        for h in range(8):
            jobs.append((z1, QC + h * HD, KCC + h * HD, VC + h * HD, "stick"))
        for h in range(8):
            jobs.append((z1, QD + h * HD, KD + h * HD, VD + h * HD, "forget"))
        for h in range(8):
            jobs.append((z2, ZQ + h * HD, ZKS + h // 4 * HD, ZVS + h // 4 * HD, "selected"))
            jobs.append((z2, ZQ + h * HD, ZKW + h // 4 * HD, ZVW + h // 4 * HD, "window"))
        beside = [1, 0] * 8 + [3] + [4] * 3 + [3] * 4 + [2] * 7 + [1] + [0] * 16

        def lagging(advance):
            held = [0]

            def before(n):
                if beside[n]:
                    advance(held[0])

            def after(n):
                if beside[n]:
                    advance(beside[n] - 1)
                else:
                    advance(held[0])
                held[0] = 1 if beside[n] else 0

            def flush():
                advance(held[0])

            return before, after, flush

        keys_of = (slice(0, P), slice(P, 3 * P))

        @block.sync
        def _(sp):
            def load(u, j, dst, src, first=False):
                if not first:
                    sp.wait_ge(parts_ready, u - (RAW - 1))
                sp.dma_start(dst, src).then_inc(raw_landed[j], 16)

            def slot(j, chunks, width):
                return raw[:, j, :].rearrange("p (k n) -> p k n", k=UC)[:, 0:chunks, 0:width]

            def load_block(b):
                u, w, c0, width, units = blocks[b]
                for g, (k0, n) in enumerate(units):
                    if b == L0_QKV:
                        if g == 0:
                            sp.dma_start(ident[:], t["ident"]).then_inc(first_landed, 16)
                            sp.dma_start(cols[:], t["cols"]).then_inc(first_landed, 16)
                        c = slice(g * BW, (g + 1) * BW)
                        sp.dma_start(res[:, :, c], t["x"][:, :, c]).then_inc(x_landed[g], 16)
                    j = (u + g) % RAW
                    load(u + g, j, slot(j, n, width),
                         w[k0 * P:(k0 + n) * P, c0:c0 + width].rearrange("(k p) n -> p k n", p=P), u < RAW)

            def load_run(b, count):
                u, w, c0, width, units = blocks[b]

                def body(n, i, r):
                    for j, (k0, m) in enumerate(units):
                        load(n * 4 + (u + j), j, slot(j, m, width),
                             w[k0 * P:(k0 + m) * P, bass.ds(n * BW + c0, BW)].rearrange("(k p) n -> p k n", p=P))

                each(sp, count, body)

            def load_ff(b, gate, up, down, then):
                u0 = first_unit[b]

                def gate_up(u, i):
                    for m, w in enumerate((gate, up)):
                        for j in range(4):
                            load(u + (4 * m + j), j, slot(j, UC, BW),
                                 w[j * BW:(j + 1) * BW, bass.ds(i * BW, BW)].rearrange("(k p) n -> p k n", p=P))

                def down4(u, i):
                    for j in range(4):
                        load(u + j, j, slot(j, UC, BW),
                             down[bass.ds(i * BW, BW), j * BW:(j + 1) * BW].rearrange("(k p) n -> p k n", p=P))

                gate_up(u0, 0)
                then()
                with sp.Fori(0, FB - 1) as i:
                    gate_up(i * 12 + (u0 + 8), i + 1)
                    down4(i * 12 + (u0 + 16), i)
                down4(u0 + 12 * FB - 4, FB - 1)

            def load_gain(row):
                sp.dma_start(grow, t["rows"][row:row + 1, :].to_broadcast([P, D])).then_inc(grow_landed, 16)

            load_block(L0_QKV)
            load_run(L0_QKV + 1, 8)
            load_block(L0_QKV + 9)
            for b in range(4):
                load_block(L0_GATE + b)
            for b in range(4):
                load_block(L0_OUT + b)
            sp.wait_ge(group_gated, 4)
            sp.dma_start(other_mask[:], t["strict"]).then_inc(strict_landed, 16)
            load_run(L1_QKV, 12)
            for b in range(5):
                load_block(L1_GATE + b)
            for b in range(4):
                load_block(L1_OUT + b)
                if b == 0:
                    sp.wait_ge(group_gated, 8)
                    load_gain(0)

            def ff1_gain():
                sp.wait_ge(res_gained, 4)
                load_gain(1)

            load_ff(FF1, t["ff1_w_gate"], t["ff1_w_up"], t["ff1_w_down"], ff1_gain)
            for b in range(5):
                load_block(MIX_REC + b)
            sp.wait_ge(st_done, turned_before["mix"] + 8)
            for m, name in enumerate(("rg_w_a", "rg_w_i")):
                sp.dma_start(rg[:, m], t[name].rearrange("b i j -> i b j")).then_inc(mix_landed, 16)
            for m, name in enumerate(("cmp_k_w2", "cmp_v_w2")):
                sp.dma_start(cmp_w2[:, m], t[name].rearrange("(k p) n -> p k n", p=P)).then_inc(mix_landed, 16)
            for b in range(5):
                load_block(MIX_QKV + b)
            for m, name in enumerate(("cmp_k_w1", "cmp_v_w1")):
                for j in range(4):
                    load(first_unit[CMP] + 4 * m + j, j, raw[:, j, :].rearrange("p (l n) -> p l n", l=8),
                         t[name][j * 1024:(j + 1) * 1024, :].rearrange("(l p) n -> p l n", p=P))
            for b in range(4):
                load_block(MIX_OUT + b)
                if b == 0:
                    sp.wait_ge(st_scaled, 4)
                    load_gain(2)

            def ff2_gain():
                all_drained(sp, FF2)
                load_gain(3)
                sp.dma_start(p_in, t["p"]).then_inc(p_landed, 16)

            load_ff(FF2, t["ff2_w_gate"], t["ff2_w_up"], t["ff2_w_down"], ff2_gain)
            for b in range(4):
                load_block(PLE_GATE + b)
            sp.wait_ge(grow_used, 2)
            load_gain(4)
            for b in range(4):
                load_block(PLE_PROJ + b)
            for g in range(4):
                sp.wait_ge(res_updated, 24 + 2 * g + 2)
                c = slice(g * BW, (g + 1) * BW)
                sp.dma_start(t["out"][:, :, c], res[:, :, c]).then_inc(out_landed, 16)
            sp.wait_ge(out_landed, 64)

        CONSTANTS = (("causal", causal), ("dilated", other_mask), ("upto", upto),
                     ("rope128", rope128), ("rope64", rope64), ("cmp_ok", cmp_ok),
                     ("positions", position))

        @block.gpsimd
        def _(pool):
            for name, tile in CONSTANTS:
                shape = tile[:]
                if name in ("upto",):
                    shape = shape.rearrange("p t n -> p (t n)")
                if name.startswith("rope"):
                    shape = shape.rearrange("p c t n -> p (c t n)")
                pool.dma_start(shape, t[name]).then_inc(const_landed, 16)
            pool.dma_start(forget_b, t["b_f1"].to_broadcast([P, 8])).then_inc(const_landed, 16)
            pool.dma_start(gate_bias, t["nsa_gate_b"].to_broadcast([P, 24])).then_inc(const_landed, 16)
            nc.gpsimd.memset(ones[:], 1.0).then_inc(made["const_made"], 1)
            pool.wait_ge(group_gated, 8)
            nc.gpsimd.memset(out2, 0.0).then_inc(added, 1)
            pool.wait_ge(made["rec_out_squared"], 1)
            nc.gpsimd.memset(work[:, 0:2048], 0.0).then_inc(made["cmp_cleared"], 1)
            pool.wait_ge(res_updated, 16)
            nc.gpsimd.memset(out2, 0.0).then_inc(added, 1)

        ALL_CONST = 16 * (len(CONSTANTS) + 2)

        @block.tensor
        def _(pe):
            at = [0]

            def unit(u, j, k0, n, width, bank, first, last, x=(x_hi, x_lo)):
                pe.wait_ge(parts_ready, u + 1)
                hi = w_hi[:, j % PARTS, :].rearrange("p (k n) -> p k n", k=UC)
                lo = w_lo[:, j % PARTS, :].rearrange("p (k n) -> p k n", k=UC)
                for c in range(n):
                    for tt in range(NT):
                        o = ps[:, bank + tt, 0:width]
                        s = slice(tt * P, (tt + 1) * P)
                        nc.tensor.matmul(o, x[0][:, k0 + c, s], hi[:, c, 0:width], start=first and c == 0, stop=False)
                        nc.tensor.matmul(o, x[0][:, k0 + c, s], lo[:, c, 0:width], start=False, stop=False)
                        m = nc.tensor.matmul(o, x[1][:, k0 + c, s], hi[:, c, 0:width], start=False,
                                             stop=last and c == n - 1)
                m.then_inc(parts_used, 1)

            def advance(n, x=(x_hi, x_lo)):
                for _ in range(n):
                    u = at[0]
                    b, place = block_of[u]
                    _, _, _, width, units = blocks[b]
                    if place == 0 and drains_before[b]:
                        pe.wait_ge(drained[pair_of[b]], drains_before[b])
                    unit(u, u % RAW, *units[place], width, 2 * pair_of[b], place == 0, place == len(units) - 1, x)
                    at[0] += 1

            def run(b, count):
                u, _, _, width, units = blocks[b]

                def body(n, i, r):
                    pair = pair_of[b + r]
                    pe.wait_ge(drained[pair], i + drains_before[b + r])
                    for j, (k0, m) in enumerate(units):
                        unit(n * 4 + (u + j), j, k0, m, width, 2 * pair, j == 0, j == len(units) - 1)

                each(pe, count, body)
                at[0] = u + 4 * count

            def turn(name, s, chunks, r=None):
                r = s % 2 if r is None else r
                k = s + turned_before[name]
                if not isinstance(k, int) or k >= 2:
                    pe.wait_ge(st_done, k - 1)
                for c, chunk in enumerate(chunks):
                    m = nc.tensor.transpose(ps[:, 6 + r, c * P:(c + 1) * P], chunk, ident[:])
                m.then_inc(st_turned, 1)

            def turn_group(name, g, src, ready):
                for tt in range(NT):
                    ready(2 * g + tt)
                    turn(name, 2 * g + tt, [src(tt, g * UC + c) for c in range(UC)])

            def staged(name, g, groups=4):
                pe.wait_ge(st_done, turned_before[name] + 2 * min(g + 1, groups))

            def first_block(name, src, ready, next_unit, groups=4):
                turn_group(name, 0, src, ready)
                for g in range(4):
                    if g + 1 < groups:
                        turn_group(name, g + 1, src, ready)
                    staged(name, g, groups)
                    next_unit(g)

            def last_and_first_block(name, src, ready, next_unit):
                for g in range(4):
                    advance(1)
                    if g:
                        turn_group(name, g - 1, src, ready)
                for g in range(4):
                    staged(name, g)
                    next_unit(g)
                    if g == 0:
                        turn_group(name, 3, src, ready)

            def of_res(tt, c):
                return res[:, tt, c * P:(c + 1) * P]

            def next_in_plan(g):
                advance(1)

            def turn_qk(n):
                zz, q, k, _, _ = jobs[n]
                if n:
                    pe.wait_ge(qk_copied, n)
                for m, c0 in enumerate((q, k)):
                    for tt in range(NT):
                        i = nc.tensor.transpose(ps[:, 7, (2 * m + tt) * P:(2 * m + tt + 1) * P],
                                                zz[:, tt, c0:c0 + HD], ident[:])
                i.then_inc(qk_turned, 1)

            def logits(n):
                kind = jobs[n][4]
                pe.wait_ge(qk_copied, n + 1)
                if n:
                    pe.wait_ge(negated, n)
                qT, kT = qkT[:, n % 2, 0:SEQ], qkT[:, n % 2, SEQ:2 * SEQ]
                for tt, keys in enumerate((P, SEQ)):
                    o = ps[:, 4, keys_of[tt]]
                    more = kind == "forget"
                    i = nc.tensor.matmul(o, qT[:, tt * P:(tt + 1) * P], kT[:, 0:keys], start=True, stop=not more)
                    if more:
                        nc.tensor.matmul(o, ones[:], rest_a[:, 0:keys], start=False, stop=tt == 0)
                        i = None
                    if more and tt == 1:
                        i = nc.tensor.matmul(ps[:, 4, 2 * P:3 * P], ones[:], rest_a[:, SEQ + P:2 * SEQ],
                                             start=False, stop=True)
                if kind == "selected":
                    g = (n - 32) // 2 // 4
                    for tt in range(NT):
                        i = nc.tensor.matmul(ps[:, 4, 384 + 16 * tt:384 + 16 * tt + NCMP], qT[:, tt * P:(tt + 1) * P],
                                             cmp_kT[:, 16 * g:16 * g + NCMP], start=True, stop=True)
                i.then_inc(logits_ready, 1)

            def turn_probs(n):
                pe.wait_ge(probs_ready, n + 1)
                if n:
                    pe.wait_ge(probs_copied, n)
                for c in range(3):
                    i = nc.tensor.transpose(ps[:, 5, c * P:(c + 1) * P], prob[:, n % 2, c * P:(c + 1) * P], ident[:])
                i.then_inc(probs_turned, 1)

            def mix(n):
                zz, _, _, vv, _ = jobs[n]
                pe.wait_ge(probs_copied, n + 1)
                if n:
                    pe.wait_ge(out_written, n)
                nc.tensor.matmul(ps[:, 6, 0:HD], probT[:, 0:P], zz[:, 0, vv:vv + HD], start=True, stop=True)
                nc.tensor.matmul(ps[:, 6, HD:2 * HD], probT[:, P:2 * P], zz[:, 0, vv:vv + HD], start=True, stop=False)
                nc.tensor.matmul(ps[:, 6, HD:2 * HD], probT[:, 2 * P:3 * P], zz[:, 1, vv:vv + HD],
                                 start=False, stop=True).then_inc(mixed, 1)

            def heads(n0, n1):
                turn_qk(n0)
                logits(n0)
                for n in range(n0, n1):
                    if n + 1 < n1:
                        turn_qk(n + 1)
                    if n < 16:
                        advance(beside[n])
                    if n > n0:
                        mix(n - 1)
                    if n >= 16:
                        advance(beside[n])
                    if n + 1 < n1:
                        logits(n + 1)
                    turn_probs(n)
                mix(n1 - 1)

            pe.wait_ge(first_landed, 32)
            first_block("n0", of_res, lambda s: pe.wait_ge(x_landed[s // 2], 16), next_in_plan)
            advance(20)
            advance(4)
            pe.wait_ge(rotated, 1)

            def turn_idx(p):
                if p:
                    pe.wait_ge(idx_copied, p)
                for tt in range(NT):
                    i = nc.tensor.transpose(ps[:, 7, tt * P:(tt + 1) * P],
                                            z0[:, tt, IQ + p * P:IQ + (p + 1) * P], ident[:])
                if p == 0:
                    for tt in range(NT):
                        i = nc.tensor.transpose(ps[:, 7, (2 + tt) * P:(3 + tt) * P], ik_twice[:, tt, :], ident[:])
                i.then_inc(idx_turned, 1)

            turn_idx(0)
            for p in range(8):
                if p < 7:
                    turn_idx(p + 1)
                pe.wait_ge(idx_copied, p + 1)
                for h in (2 * p, 2 * p + 1):
                    if h >= 2:
                        pe.wait_ge(relu_ready, h - 1)
                    half = slice(64 * (h % 2), 64 * (h % 2) + 64)
                    for tt, keys in enumerate((P, SEQ)):
                        i = nc.tensor.matmul(ps[:, 4 + h % 2, keys_of[tt]], qkT[half, p % 2, tt * P:(tt + 1) * P],
                                             probT[half, 0:keys], start=True, stop=True)
                    i.then_inc(dots_ready, 1)
                advance(1)
            advance(4)
            advance(8)
            pe.wait_ge(rotated, 2)
            pe.wait_ge(scored, 17)
            heads(0, 16)

            def gated_ready(layer):
                return lambda s: pe.wait_ge(group_gated, 4 * layer + s // 2 + 1)

            first_block("y0", lambda tt, c: z0[:, tt, G0 + c * P:G0 + (c + 1) * P], gated_ready(0), next_in_plan)
            advance(8)

            def residual_ready(s):
                b = L0_OUT + s // 2
                pe.wait_ge(drained[pair_of[b]], drains_before[b] + 1)

            last_and_first_block("n1", of_res, residual_ready, next_in_plan)

            advance(4)
            run(L1_QKV + 2, 4)
            advance(1)
            all_drained(pe, L1_QKV + 6)
            heads(16, 24)
            advance(1)
            all_drained(pe, L1_GATE)
            pe.wait_ge(const_landed, ALL_CONST)
            pe.wait_ge(made["const_made"], 1)
            heads(24, 32)
            first_block("y1", lambda tt, c: z1[:, tt, G1 + c * P:G1 + (c + 1) * P], gated_ready(1), next_in_plan)
            advance(8)

            def first_gate_unit(b):
                def unit_of(g):
                    if g == 0:
                        pe.wait_ge(drained[1], drained_before(b, 1))
                    u = first_unit[b] + g
                    unit(u, u % RAW, g * UC, UC, BW, 2, g == 0, g == 3)

                return unit_of

            def feed_forward(b, no, hname):
                u0 = first_unit[b]
                h0 = no * FB
                a0 = added_before(no)

                def product(u, bank):
                    for j in range(4):
                        unit(u + j, j, j * UC, UC, BW, bank, j == 0, j == 3)

                def turn_hidden(i):
                    pe.wait_ge(hid_ready, i + (h0 + 1))
                    pe.wait_ge(added, i * 4 + a0)
                    for s in range(2):
                        turn(hname, i * 2 + s, [hid[:, s, c * P:(c + 1) * P] for c in range(UC)], s)

                def down(u, i):
                    pe.wait_ge(st_done, i * 2 + (turned_before[hname] + 2))
                    for j in range(4):
                        if j >= 2:
                            pe.wait_ge(added, i * 4 + (a0 + j - 1))
                        unit(u + j, j, 0, UC, BW, 4 + 2 * (j % 2), True, True, (h_hi, h_lo))

                all_drained(pe, b)
                product(u0 + 4, 0)
                with pe.Fori(0, FB - 1) as i:
                    pe.wait_ge(ff_silu, i + (h0 + 1))
                    product(i * 12 + (u0 + 8), 2)
                    turn_hidden(i)
                    product(i * 12 + (u0 + 12), 0)
                    down(i * 12 + (u0 + 16), i)
                turn_hidden(FB - 1)
                down(u0 + 12 * FB - 4, FB - 1)
                at[0] = u0 + 12 * FB

            last_and_first_block("ff1", of_res, lambda s: pe.wait_ge(res_gained, s // 2 + 1), first_gate_unit(FF1))
            feed_forward(FF1, 0, "h1")

            def updated(no):
                return lambda s: pe.wait_ge(res_updated, 8 * no + s + 1)

            first_block("mix", of_res, updated(0), next_in_plan)
            advance(18)
            all_drained(pe, MIX_QKV)
            pe.wait_ge(st_done, turned_before["mix"] + 8)

            def turn_channels(c0):
                for b in range(LB):
                    for tt in range(NT):
                        i = nc.tensor.transpose(ps[:, 4 + b // 2, (b % 2) * SEQ + tt * P:(b % 2) * SEQ + (tt + 1) * P],
                                                z2[:, tt, c0 + b * P:c0 + (b + 1) * P], ident[:])
                return i

            turn_channels(ZX).then_inc(made["rec_x_turned"], 1)
            advance(2)
            pe.wait_ge(made["rec_padded"], 1)
            turn_channels(ZY).then_inc(made["rec_y_turned"], 1)
            advance(4)
            pe.wait_ge(made["rec_y_gelu"], 1)
            pe.wait_ge(made["rec_conv"], 1)
            pe.wait_ge(mix_landed, 64)
            for m, (done, free) in enumerate((("rec_r_product", None), ("rec_i_product", "rec_r_tanh"))):
                if free:
                    pe.wait_ge(made[free], 1)
                for b in range(LB):
                    i = nc.tensor.matmul(ps[:, 4 + b // 2, (b % 2) * SEQ:(b % 2 + 1) * SEQ], rg[:, m, b, :],
                                         by_block(r1)[:, b, :], start=True, stop=True)
                i.then_inc(made[done], 1)
                advance(2)
            advance(4)
            pe.wait_ge(made["rec_out_squared"], 1)
            for b in range(LB):
                i = nc.tensor.matmul(ps[:, 4, 0:SEQ], ones[:], by_block(r2)[:, b, :], start=b == 0, stop=b == LB - 1)
            i.then_inc(made["rec_summed"], 1)
            advance(2)
            pe.wait_ge(rotated, 3)
            pe.wait_ge(made["rec_norm_root"], 1)
            for m, c0 in enumerate((ZKC, ZVC)):
                for g in range(2):
                    for tt in range(NT):
                        i = nc.tensor.transpose(ps[:, 4 + m, g * SEQ + tt * P:g * SEQ + (tt + 1) * P],
                                                z2[:, tt, c0 + g * HD:c0 + (g + 1) * HD], ident[:])
                i.then_inc(made["cmp_turned"], 1)
            advance(2)
            xf = [x[:].rearrange("p k s -> p (k s)") for x in (x_hi, x_lo)]
            for m in range(2):
                b = CMP + m
                pe.wait_ge(made["cmp_lo"], m + 1)
                pe.wait_ge(drained[pair_of[b]], drains_before[b])
                for j in range(4):
                    u = first_unit[b] + j
                    pe.wait_ge(parts_ready, u + 1)
                    hi, lo = (w[:, j % PARTS, :].rearrange("p (l n) -> p l n", l=8) for w in (w_hi, w_lo))
                    for l in range(8):
                        c = 1024 * m + (8 * j + l) * 32
                        o = ps[0:32, 2 * pair_of[b], 0:256]
                        nc.tensor.matmul(o, xf[0][:, c:c + 32], hi[:, l, :], start=j + l == 0, stop=False)
                        nc.tensor.matmul(o, xf[0][:, c:c + 32], lo[:, l, :], start=False, stop=False)
                        i = nc.tensor.matmul(o, xf[1][:, c:c + 32], hi[:, l, :], start=False, stop=j == 3 and l == 7)
                    i.then_inc(parts_used, 1)
            at[0] = first_unit[MIX_OUT]
            for m in range(2):
                pe.wait_ge(drained[pair_of[CMP + m]], drains_before[CMP + m] + 1)
                for k in range(2):
                    i = nc.tensor.transpose(ps[:, 6, 64 * m + 32 * k:64 * m + 32 * k + 32],
                                            cmp_hid[m][:, k * P:(k + 1) * P], ident[0:32, 0:32])
            i.then_inc(made["cmp_hid_turned"], 1)
            pe.wait_ge(made["cmp_hidT_ready"], 1)
            for k in range(2):
                nc.tensor.matmul(ps[:, 7, 0:32], cmp_w2[:, 0, k, :], cmp_hidT[0][:, 32 * k:32 * k + 32],
                                 start=k == 0, stop=k == 1)
            for g in range(2):
                for k in range(2):
                    i = nc.tensor.matmul(ps[0:NCMP, 7, P * (g + 1):P * (g + 2)],
                                         cmp_hidT[1][:, 32 * k + 16 * g:32 * k + 16 * g + NCMP], cmp_w2[:, 1, k, :],
                                         start=k == 0, stop=k == 1)
            i.then_inc(made["cmp_kv_made"], 1)
            pe.wait_ge(made["cmp_kv_ready"], 1)
            pe.wait_ge(rotated, 4)
            heads(32, 48)
            pe.wait_ge(made["cmp_weighted"], 1)
            pe.wait_ge(out_written, 48)
            for h in range(8):
                if h:
                    pe.wait_ge(made["cmp_p_copied"], h)
                for tt in range(NT):
                    c = 240 + (2 * h + tt) * NCMP
                    i = nc.tensor.transpose(ps[0:NCMP, 5, tt * P:(tt + 1) * P], rest_a[:, c:c + NCMP], ident[:])
                i.then_inc(made["cmp_p_turned"], 1)
                pe.wait_ge(made["cmp_p_copied"], h + 1)
                if h:
                    pe.wait_ge(made["cmp_added"], h)
                for tt in range(NT):
                    i = nc.tensor.matmul(ps[:, 6, tt * HD:(tt + 1) * HD], probT[0:NCMP, tt * P:(tt + 1) * P],
                                         cmp_v[0:NCMP, h // 4, :], start=True, stop=True)
                i.then_inc(made["cmp_mixed"], 1)
            pe.wait_ge(y_ready, 1)
            pe.wait_ge(made["rec_lo"], 1)
            first_block("attn", lambda tt, c: scaled[:, tt, c % UC * P:(c % UC + 1) * P],
                        lambda s: pe.wait_ge(st_scaled, s + 1), next_in_plan, 2)
            advance(12)

            first_block("ff2", of_res, updated(1), first_gate_unit(FF2))
            feed_forward(FF2, 1, "h2")

            first_block("ple", of_res, updated(2), next_in_plan)
            advance(12)
            pe.wait_ge(p_landed, 16)
            for s in range(2):
                turn("p", s, [p_in[:, s, c * P:(c + 1) * P] for c in range(2)])
            pe.wait_ge(st_done, turned_before["p"] + 2)
            advance(4, (h_hi, h_lo))

        @block.scalar
        def _(act):
            at = [0]
            chain = [0]
            norms = [0]

            def link(ins):
                chain[0] += 1
                ins.then_inc(act_chain, 1)
                act.wait_ge(act_chain, chain[0])

            def split_hi(u, j):
                act.wait_ge(raw_landed[j], u * 4 + (16 - 4 * j))
                if not isinstance(u, int) or u >= PARTS:
                    act.wait_ge(parts_used, u - (PARTS - 1))
                n = unit_size(u)
                nc.scalar.activation(w_hi[:, j % PARTS, 0:n], raw[:, j, 0:n], ACT.Copy).then_inc(hi_ready, 1)

            def splits(u, j0, n):
                for k in range(n):
                    split_hi(u + k, (j0 + k) % RAW)

            def split_next(u):
                if u < N_UNITS:
                    split_hi(u, u % RAW)

            def drain(b):
                kind = drain_kind[b]
                if kind == "residual":
                    act.wait_ge(drained[pair_of[b]], drains_before[b] + 1)
                    if b >= L1_OUT:
                        squares(res_block(b - L1_OUT), post_ssq, b - L1_OUT, first_squared)
                    else:
                        squares(res_block(b - L0_OUT), next_ssq, b - L0_OUT)
                if kind == "gated":
                    act.wait_ge(drained[pair_of[b]], drains_before[b] + 1)
                    squares([place_of(b)[:, tt] for tt in range(NT)], post_ssq, b - PLE_PROJ)
                if kind in ("residual", "gated"):
                    return
                act.wait_ge(parts_used, first_unit[b] + len(blocks[b][4]))
                if kind == "copy":
                    for tt in range(NT):
                        i = nc.scalar.activation(place_of(b)[:, tt], summed(b)[:, tt], ACT.Copy,
                                                 scale=rstd[:, tt:tt + 1])
                    i.then_inc(drained[pair_of[b]], 1)
                elif kind == "output":
                    j = b - MIX_OUT
                    squares([summed(b)[:, tt] for tt in range(NT)], post_ssq, j, output_squared)
                elif kind == "gate":
                    skip = 8 if b == L1_GATE else 0
                    for tt in range(NT):
                        if skip:
                            nc.scalar.activation(place_of(b)[:, tt, 0:skip], summed(b)[:, tt, 0:skip], ACT.Copy,
                                                 scale=rstd[:, tt:tt + 1])
                        i = nc.scalar.activation(place_of(b)[:, tt, skip:], summed(b)[:, tt, skip:], ACT.Tanh,
                                                 scale=half_rstd[:, tt:tt + 1])
                    i.then_inc(gate_tanh, 1)
                elif kind == "tanh":
                    for tt in range(NT):
                        i = nc.scalar.activation(place_of(b)[:, tt], summed(b)[:, tt], ACT.Tanh,
                                                 scale=half_rstd[:, tt:tt + 1])
                    i.then_inc(drained[pair_of[b]], 1)
                elif kind == "gelu":
                    nc.scalar.activation(cmp_hid[b - CMP], ps[0:32, 2 * pair_of[b], 0:256],
                                         ACT.Gelu_apprx_tanh).then_inc(drained[pair_of[b]], 1)

            def squares(rows, sums, j, done=None):
                for tt in range(NT):
                    i = nc.scalar.activation(scaled[:, tt, 0:BW], rows[tt], ACT.Square,
                                             accum_out=sums[:, tt, j:j + 1])
                if done is None:
                    link(i)
                else:
                    i.then_inc(done, 1)
                    act.wait_ge(done, j + 1)

            def mean_of(sums, scale, bias, dst):
                for tt in range(NT):
                    link(nc.scalar.activation(small[:, tt, :], sums[:, tt, :], ACT.Copy, scale=scale, bias=bias / 4,
                                              accum_out=dst[:, tt:tt + 1]))

            def output_root(scale, bias):
                mean_of(post_ssq, scale, bias, root)
                nc.scalar.activation(root, root, ACT.Sqrt).then_inc(root_ready, 1)
                norms[0] += 1

            def res_block(j):
                return [res[:, tt, j * BW:(j + 1) * BW] for tt in range(NT)]

            def advance(n, held=False):
                for _ in range(n):
                    u = at[0]
                    if not held:
                        split_next(u + PARTS)
                    b, place = block_of[u]
                    if place == len(blocks[b][4]) - 1:
                        drain(b)
                    at[0] += 1

            def run(b, count, zz, c0):
                u = first_unit[b]

                def body(n, i, r):
                    splits(n * 4 + (u + 2), 2, 4)
                    pair = pair_of[b + r]
                    act.wait_ge(parts_used, n * 4 + (u + 4))
                    for tt in range(NT):
                        k = nc.scalar.activation(zz[:, tt, bass.ds(n * BW + c0, BW)], ps[:, 2 * pair + tt, :],
                                                 ACT.Copy, scale=rstd[:, tt:tt + 1])
                    k.then_inc(drained[pair], 1)

                each(act, count, body)
                at[0] = u + 4 * count

            def rms(src, n):
                for tt in range(NT):
                    link(nc.scalar.activation(work[:, 0:n], src(tt), ACT.Square, accum_out=ssq[:, tt:tt + 1]))
                link(nc.scalar.activation(root, ssq, ACT.Copy, scale=1.0 / n, bias=EPS))
                nc.scalar.activation(root, root, ACT.Sqrt).then_inc(root_ready, 1)
                norms[0] += 1

            def res_norm(ready=None):
                def norm(g):
                    if ready:
                        ready(g)
                        squares(res_block(g), next_ssq, g)
                    if g == 3:
                        mean_of(next_ssq, 1.0 / D, EPS, root)
                        nc.scalar.activation(root, root, ACT.Sqrt).then_inc(root_ready, 1)
                        norms[0] += 1
                        act.wait_ge(rstd_ready, norms[0])

                return norm

            def hi_group(name, g, gain=True):
                for s in (2 * g, 2 * g + 1):
                    dst = x_hi[:, g * UC:(g + 1) * UC, (s % 2) * P:(s % 2 + 1) * P]
                    if gain:
                        act.wait_ge(st_gained, gained_before[name] + s + 1)
                        nc.scalar.activation(dst, gained[:, s % 2], ACT.Copy).then_inc(st_hi, 1)
                    else:
                        act.wait_ge(st_turned, turned_before[name] + s + 1)
                        nc.scalar.activation(dst, ps[:, 6 + s % 2, :].rearrange("p (k n) -> p k n", k=UC),
                                             ACT.Copy).then_inc(st_hi, 1)

            def first_block(name, gain=True, norm=None, held=False):
                if held:
                    split_next(at[0] + 1)
                hi_group(name, 0, gain)
                if name == "n0":
                    splits(0, 0, 2)
                for g in range(4):
                    if g < 3:
                        hi_group(name, g + 1, gain)
                    if norm:
                        norm(g)
                    advance(1)

            def last_and_first_block(name, norm, between=None):
                for g in range(4):
                    advance(1)
                    if g:
                        hi_group(name, g - 1)
                    elif between:
                        between(2)
                for g in range(4):
                    if g == 3:
                        norm(g)
                    advance(1)
                    if g == 0:
                        if between:
                            between(3)
                        hi_group(name, 3)

            def copy_qk(n):
                kind = jobs[n][4]
                act.wait_ge(qk_turned, n + 1)
                if n >= 2:
                    act.wait_ge(logits_ready, n - 1)
                if kind == "forget":
                    h = n - 24
                    if n > 24:
                        act.wait_ge(logits_ready, n)
                    for tt in range(NT):
                        nc.scalar.activation(rest_a[:, tt * SEQ:(tt + 1) * SEQ], upto[:, tt, :], ACT.Copy,
                                             scale=neg_log_f[:, tt, h:h + 1])
                nc.scalar.activation(qkT[:, n % 2, :], ps[:, 7, :], ACT.Copy).then_inc(qk_copied, 1)

            def exponents(n):
                act.wait_ge(negated, n + 1)
                if n >= 2:
                    act.wait_ge(probs_turned, n - 1)
                for tt in range(NT):
                    i = nc.scalar.activation(prob[:, n % 2, keys_of[tt]], neg[:, n % 2, keys_of[tt]], ACT.Exp,
                                             scale=-1.0, bias=low[:, n % 2, tt:tt + 1],
                                             accum_out=total[:, n % 2, tt:tt + 1])
                i.then_inc(probs_ready, 1)

            def softplus(n):
                act.wait_ge(negated, n + 1)
                link(nc.scalar.activation(rest_a[:, 0:384], neg[:, n % 2, :], ACT.Abs))
                link(nc.scalar.activation(rest_a[:, 0:384], rest_a[:, 0:384], ACT.Exp, scale=-1.0))
                nc.scalar.activation(rest_a[:, 0:384], rest_a[:, 0:384], ACT.Ln, bias=1.0).then_inc(softplus_ready, 1)

            def stick_exponents(n):
                act.wait_ge(arg_ready, n - 15)
                if n >= 2:
                    act.wait_ge(probs_turned, n - 1)
                nc.scalar.activation(prob[:, n % 2, :], neg[:, n % 2, :], ACT.Exp).then_inc(probs_ready, 1)

            def heads(n0, n1):
                held, rest, flush = lagging(advance)
                copy_qk(n0)
                for n in range(n0, n1):
                    if n + 1 < n1:
                        copy_qk(n + 1)
                    if beside[n] >= 2:
                        held(n)
                    if jobs[n][4] == "stick":
                        softplus(n)
                        stick_exponents(n)
                    else:
                        exponents(n)
                    if beside[n] < 2:
                        held(n)
                    rest(n)
                flush()

            first_block("n0", norm=res_norm(lambda g: act.wait_ge(x_landed[g], 16)))
            advance(20)
            advance(4)

            def copy_idx(p):
                act.wait_ge(idx_turned, p + 1)
                if p >= 2:
                    act.wait_ge(dots_ready, 2 * p - 2)
                if p == 0:
                    nc.scalar.activation(probT[:, 0:SEQ], ps[:, 7, SEQ:2 * SEQ], ACT.Copy)
                nc.scalar.activation(qkT[:, p % 2, 0:SEQ], ps[:, 7, 0:SEQ], ACT.Copy).then_inc(idx_copied, 1)

            copy_idx(0)
            for p in range(8):
                if p < 7:
                    copy_idx(p + 1)
                for h in (2 * p, 2 * p + 1):
                    act.wait_ge(dots_ready, h + 1)
                    if h >= 2:
                        act.wait_ge(scored, h - 1)
                    nc.scalar.activation(neg[:, h % 2, :], ps[:, 4 + h % 2, 0:384], ACT.Relu,
                                         scale=0.125).then_inc(relu_ready, 1)
                advance(1)
            advance(12)
            heads(0, 16)
            first_block("y0", False)
            advance(8)
            last_and_first_block("n1", res_norm())

            advance(4)
            run(L1_QKV + 2, 4, z1, 2 * BW)
            advance(1)

            def forget_gates():
                act.wait_ge(made["forget_sum"], 1)
                link(nc.scalar.activation(forget_e, forget_x, ACT.Abs))
                link(nc.scalar.activation(forget_e, forget_e, ACT.Exp, scale=-1.0))
                nc.scalar.activation(forget_e, forget_e, ACT.Ln, bias=1.0).then_inc(made["forget_ln"], 1)
                act.wait_ge(made["forget_ln"], 2)

            heads(16, 24)
            forget_gates()
            advance(1)
            act.wait_ge(const_landed, ALL_CONST)
            heads(24, 32)
            def last_gain(j):
                act.wait_ge(res_gained, j + 1)
                squares(res_block(j), next_ssq, j)

            first_block("y1", False)
            for j in range(2):
                advance(1)
                last_gain(j)
                advance(3)

            def last_norm_and_ff1(g):
                mean_of(post_ssq, 1.0 / D, EPS, root)
                mean_of(next_ssq, 1.0 / D, 0.0, next_mean)
                nc.scalar.activation(root, root, ACT.Sqrt).then_inc(root_ready, 1)
                norms[0] += 1
                act.wait_ge(rstd_ready, norms[0])
                nc.scalar.activation(root, next_mean, ACT.Sqrt).then_inc(root_ready, 1)
                norms[0] += 1
                act.wait_ge(rstd_ready, norms[0])

            last_and_first_block("ff1", last_norm_and_ff1, last_gain)

            def feed_forward(b, no, hname):
                u0 = first_unit[b]
                h0 = no * FB

                def hidden_hi(i):
                    for s in range(2):
                        act.wait_ge(st_turned, i * 2 + (turned_before[hname] + s + 1))
                        nc.scalar.activation(h_hi[:, :, s * P:(s + 1) * P],
                                             ps[:, 6 + s, :].rearrange("p (k n) -> p k n", k=UC),
                                             ACT.Copy).then_inc(st_hi, 1)

                def gate_tanhs(u, i):
                    act.wait_ge(parts_used, u + 4)
                    if not isinstance(i, int) or i or h0:
                        act.wait_ge(hid_ready, i + h0)
                    for tt in range(NT):
                        k = nc.scalar.activation(silu[:, tt], ps[:, 2 + tt, :], ACT.Tanh, scale=half_rstd[:, tt:tt + 1])
                    k.then_inc(ff_tanh, 1)

                gate_tanhs(u0, 0)
                splits(u0 + 6, 2, 4)
                with act.Fori(0, FB - 1) as i:
                    u = i * 12 + (u0 + 8)
                    splits(u + 2, 2, 4)
                    hidden_hi(i)
                    gate_tanhs(u, i + 1)
                    splits(u + 6, 2, 4)
                    splits(u + 10, 2, 4)
                hidden_hi(FB - 1)
                at[0] = u0 + 12 * FB
                for j in range(4):
                    if j < 3:
                        split_next(at[0] - 2 + j)
                    act.wait_ge(added, added_before(no) + 4 * (FB - 1) + j + 1)
                    squares([out2[:, tt, j * BW:(j + 1) * BW] for tt in range(NT)], post_ssq, j)
                output_root(4.0 / D, 4 * EPS)

            def updated_norm(no):
                return res_norm(lambda g: act.wait_ge(res_updated, 8 * no + 2 * g + 2))

            feed_forward(FF1, 0, "h1")
            first_block("mix", norm=updated_norm(0), held=True)
            advance(8)
            act.wait_ge(made["angle_ready"], 1)
            nc.scalar.activation(turn_tab, turn_tab, ACT.Sin).then_inc(made["angle_sin"], 1)
            link(nc.scalar.activation(lam_x, cols[:, LAM:LAM + 8], ACT.Abs))
            nc.scalar.activation(lam_x, lam_x, ACT.Exp, scale=-1.0).then_inc(made["lam_exp"], 1)
            advance(10)
            act.wait_ge(made["rec_x_turned"], 1)
            four = lambda: ps[:, 4:8, :].rearrange("p k (b n) -> p (k b) n", b=2)
            nc.scalar.activation(r_pad[:, :, 3:3 + SEQ], four(), ACT.Copy).then_inc(made["rec_padded"], 1)
            advance(2)
            act.wait_ge(made["rec_y_turned"], 1)
            nc.scalar.activation(work[:, 0:2048].rearrange("p (b n) -> p b n", b=LB), four(),
                                 ACT.Gelu_apprx_tanh).then_inc(made["rec_y_gelu"], 1)
            advance(4)
            act.wait_ge(made["rec_r_product"], 1)
            for b in range(LB):
                i = nc.scalar.activation(by_block(r2)[:, b, :], four()[:, b, :], ACT.Tanh, scale=0.5,
                                         bias=half_ba[:, b:b + 1])
            i.then_inc(made["rec_r_tanh"], 1)
            advance(2)
            act.wait_ge(made["rec_i_product"], 1)
            for b in range(LB):
                i = nc.scalar.activation(by_block(r4)[:, b, :], four()[:, b, :], ACT.Tanh, scale=0.5,
                                         bias=half_bi[:, b:b + 1])
            i.then_inc(made["rec_i_tanh"], 1)
            advance(2)
            act.wait_ge(made["rec_log_a"], 1)
            nc.scalar.activation(r3, r2, ACT.Exp)
            nc.scalar.activation(r0, r2, ACT.Tanh).then_inc(made["rec_a"], 1)
            advance(1)
            act.wait_ge(made["rec_square"], 1)
            nc.scalar.activation(r2, r2, ACT.Sqrt, scale=-1.0).then_inc(made["rec_root"], 1)
            advance(3)
            act.wait_ge(made["rec_summed"], 1)
            link(nc.scalar.activation(r0[:, 0:SEQ], ps[:, 4, 0:SEQ], ACT.Copy, scale=1.0 / LRU, bias=EPS))
            nc.scalar.activation(r0[:, 0:SEQ], r0[:, 0:SEQ], ACT.Sqrt).then_inc(made["rec_norm_root"], 1)
            advance(4)
            xf = x_hi[:].rearrange("p k s -> p (k s)")
            for m in range(2):
                act.wait_ge(made["cmp_summed"], m + 1)
                nc.scalar.activation(xf[:, 1024 * m:1024 * (m + 1)], cmp_x[m], ACT.Copy).then_inc(made["cmp_hi"], 1)
            advance(2)
            act.wait_ge(made["rec_ready"], 1)
            nc.scalar.activation(x_hi[:, LB:2 * LB, :], by_block(r1), ACT.Copy).then_inc(made["rec_hi"], 1)
            act.wait_ge(made["nsa_gate_sum"], 1)
            nc.scalar.activation(nsa_gates, nsa_gates, ACT.Tanh, scale=0.5).then_inc(made["nsa_gate_tanh"], 1)
            advance(6)
            act.wait_ge(made["cmp_hid_turned"], 1)
            for m in range(2):
                i = nc.scalar.activation(cmp_hidT[m], ps[:, 6, 64 * m:64 * m + 64], ACT.Copy)
            i.then_inc(made["cmp_hidT_ready"], 1)
            act.wait_ge(made["cmp_kv_made"], 1)
            nc.scalar.activation(cmp_kT, ps[:, 7, 0:32], ACT.Copy)
            nc.scalar.activation(cmp_v[0:NCMP], ps[0:NCMP, 7, P:3 * P].rearrange("p (g n) -> p g n", g=2),
                                 ACT.Copy).then_inc(made["cmp_kv_ready"], 1)
            heads(32, 48)
            act.wait_ge(made["cmp_negated"], 1)
            nc.scalar.activation(rest_a[:, 240:480], cmp_logits, ACT.Exp, scale=-1.0).then_inc(made["cmp_probs"], 1)
            for h in range(8):
                act.wait_ge(made["cmp_p_turned"], h + 1)
                if h:
                    act.wait_ge(made["cmp_mixed"], h)
                nc.scalar.activation(probT[0:NCMP, 0:SEQ], ps[0:NCMP, 5, 0:SEQ],
                                     ACT.Copy).then_inc(made["cmp_p_copied"], 1)
            act.wait_ge(y_ready, 1)
            rms(lambda tt: o_attn[:, tt, :], LRU)
            act.wait_ge(rstd_ready, norms[0])
            for g in range(2):
                for tt in range(NT):
                    if g:
                        act.wait_ge(st_turned, turned_before["attn"] + tt + 1)
                    nc.scalar.activation(scaled[:, tt, :], o_attn[:, tt, g * BW:(g + 1) * BW], ACT.Copy,
                                         scale=rstd[:, tt:tt + 1]).then_inc(st_scaled, 1)
                hi_group("attn", g)
            advance(15)
            advance(1, held=True)
            output_root(1.0 / D, EPS)
            first_block("ff2", norm=updated_norm(1), held=True)
            feed_forward(FF2, 1, "h2")
            first_block("ple", norm=updated_norm(2), held=True)
            advance(12)
            for s in range(2):
                act.wait_ge(st_turned, turned_before["p"] + s + 1)
                nc.scalar.activation(h_hi[:, 0:2, s * P:(s + 1) * P],
                                     ps[:, 6 + s, 0:2 * P].rearrange("p (k n) -> p k n", k=2),
                                     ACT.Copy).then_inc(st_hi, 1)
            advance(4)
            output_root(1.0 / D, 4 * EPS)

        @block.vector
        def _(dve):
            at = [0]
            chain = [0]
            norms = [0]
            V = nc.vector

            def link(ins):
                chain[0] += 1
                ins.then_inc(dve_chain, 1)
                dve.wait_ge(dve_chain, chain[0])

            def split_lo(u, j):
                dve.wait_ge(hi_ready, u + 1)
                n = unit_size(u)
                V.tensor_tensor(w_lo[:, j % PARTS, 0:n], raw[:, j, 0:n], w_hi[:, j % PARTS, 0:n].bitcast(F32),
                                ALU.subtract).then_inc(parts_ready, 1)

            def splits(u, j0, n):
                for k in range(n):
                    split_lo(u + k, (j0 + k) % RAW)

            def drain(b):
                kind = drain_kind[b]
                done = lambda: dve.wait_ge(parts_used, first_unit[b] + len(blocks[b][4]))
                if kind == "residual":
                    done()
                    V.scalar_tensor_tensor(place_of(b), summed(b), 0.5, place_of(b), ALU.mult,
                                           ALU.add).then_inc(drained[pair_of[b]], 1)
                elif kind == "output":
                    done()
                    dve.wait_ge(grow_landed, 48)
                    j = b - MIX_OUT
                    dve.wait_ge(output_squared, j + 1)
                    V.tensor_tensor(place_of(b), summed(b), gain_row(j), ALU.mult).then_inc(drained[pair_of[b]], 1)
                elif kind == "gate":
                    skip = 8 if b == L1_GATE else 0
                    dve.wait_ge(gate_tanh, gate_no[b])
                    V.scalar_tensor_tensor(place_of(b)[:, :, skip:], place_of(b)[:, :, skip:], 1.0,
                                           summed(b)[:, :, skip:], ALU.add, ALU.mult).then_inc(drained[pair_of[b]], 1)
                elif kind == "gated":
                    done()
                    c0, width = blocks[b][2:4]
                    V.scalar_tensor_tensor(place_of(b), ple_gate[:, :, c0:c0 + width], 1.0, summed(b), ALU.add,
                                           ALU.mult).then_inc(drained[pair_of[b]], 1)
                    dve.wait_ge(drained[pair_of[b]], drains_before[b] + 1)
                    dve.wait_ge(grow_landed, 80)
                    j = b - PLE_PROJ
                    V.tensor_tensor(last_weighted[j], place_of(b), gain_row(j),
                                    ALU.mult)

            def gain_row(j):
                return grow[:, j * BW:(j + 1) * BW].unsqueeze(1).to_broadcast([P, NT, BW])

            def split_next(u):
                if u < N_UNITS:
                    split_lo(u, u % RAW)

            def advance(n, held=False):
                for _ in range(n):
                    u = at[0]
                    if not held:
                        split_next(u + PARTS)
                    b, place = block_of[u]
                    if place == len(blocks[b][4]) - 1:
                        drain(b)
                    at[0] += 1

            def run(b, count):
                u = first_unit[b]
                each(dve, count, lambda n, i, r: splits(n * 4 + (u + 2), 2, 4))
                at[0] = u + 4 * count

            def reciprocal_root(dst=None):
                norms[0] += 1
                dve.wait_ge(root_ready, norms[0])
                if dst is not None:
                    V.reciprocal(dst, root).then_inc(rstd_ready, 1)
                    dve.wait_ge(rstd_ready, norms[0])
                    return
                link(V.reciprocal(rstd, root))
                V.tensor_scalar(half_rstd, rstd, 0.5, None, ALU.mult)
                V.scalar_tensor_tensor(half_square, rstd, 0.5, rstd, ALU.mult, ALU.mult).then_inc(rstd_ready, 1)

            def lo_group(name, g, gain=True, between=None):
                banks = [ps[:, 6 + tt, :].rearrange("p (k n) -> p k n", k=UC) for tt in range(NT)]
                if gain:
                    for tt in range(NT):
                        dve.wait_ge(st_turned, turned_before[name] + 2 * g + tt + 1)
                        column = cols[:, GAIN[name] + g * UC:GAIN[name] + (g + 1) * UC]
                        V.tensor_tensor(gained[:, tt], banks[tt], column.unsqueeze(2).to_broadcast([P, UC, P]),
                                        ALU.mult).then_inc(st_gained, 1)
                if between:
                    between()
                for tt in range(NT):
                    dve.wait_ge(st_hi, turned_before[name] + 2 * g + tt + 1)
                    c = (slice(None), slice(g * UC, (g + 1) * UC), slice(tt * P, (tt + 1) * P))
                    V.tensor_tensor(x_lo[c], gained[:, tt] if gain else banks[tt], x_hi[c].bitcast(F32),
                                    ALU.subtract).then_inc(st_done, 1)

            def first_block(name, gain=True, norm=None, held=False, update=None):
                def ahead(g):
                    return (lambda: update(g)) if update and g < 4 else None

                if update:
                    update(0)
                lo_group(name, 0, gain, ahead(1))
                if held:
                    split_next(at[0] + 1)
                if name == "n0":
                    splits(0, 0, 2)
                for g in range(4):
                    if g < 3:
                        lo_group(name, g + 1, gain, ahead(g + 2))
                    elif norm:
                        norm()
                    advance(1)

            def last_and_first_block(name, norm, between=None):
                for g in range(4):
                    advance(1)
                    if g:
                        lo_group(name, g - 1)
                    elif between:
                        between(2)
                if between:
                    between(3)
                for g in range(4):
                    if g == 3:
                        norm()
                    advance(1)
                    if g == 0:
                        lo_group(name, 3)

            def add_output(src):
                def update(g):
                    c = slice(g * BW, (g + 1) * BW)
                    for tt in range(NT):
                        V.scalar_tensor_tensor(res[:, tt, c], src(g)[:, tt], output_rstd[:, tt:tt + 1], res[:, tt, c],
                                               ALU.mult, ALU.add).then_inc(res_updated, 1)

                return update

            def rotate(zz, tt, c0, n, step, half, cos, sin, last=None):
                v = zz[:, tt, c0:c0 + n * step].rearrange("p (h e) -> p h e", h=n)[:, :, 0:2 * half]
                v = v.rearrange("p h (w e) -> p h w e", w=2)
                a, b = (r[:, 0:n * 2 * half].rearrange("p (h w e) -> p h w e", h=n, w=2) for r in (rot_a, rot_b))
                both = lambda tab: tab.unsqueeze(1).unsqueeze(1).to_broadcast([P, n, 2, half])
                V.tensor_tensor(a, v, both(cos), ALU.mult)
                link(V.tensor_tensor(b, v, both(sin), ALU.mult))
                V.tensor_tensor(v[:, :, 0, :], a[:, :, 0, :], b[:, :, 1, :], ALU.subtract)
                i = V.tensor_tensor(v[:, :, 1, :], a[:, :, 1, :], b[:, :, 0, :], ALU.add)
                if last is None:
                    link(i)
                else:
                    i.then_inc(last, 1)

            def copy_probs(n):
                dve.wait_ge(probs_turned, n + 1)
                if n:
                    dve.wait_ge(mixed, n)
                V.tensor_copy(probT, ps[:, 5, 0:384]).then_inc(probs_copied, 1)

            def negate(n):
                kind = jobs[n][4]
                dve.wait_ge(logits_ready, n + 1)
                if n >= 2:
                    dve.wait_ge(probs_ready, n - 1)
                mask = {"sparse": rest_a[:, 0:384], "dilated": other_mask[:]}.get(kind, causal[:])
                if kind == "selected":
                    h = (n - 32) // 2
                    V.tensor_copy(cmp_logits[:, 30 * h:30 * h + 30].rearrange("p (t c) -> p t c", t=NT),
                                  ps[:, 4, 384:416].rearrange("p (t c) -> p t c", t=NT)[:, :, 0:NCMP])
                link(V.scalar_tensor_tensor(neg[:, n % 2, :], ps[:, 4, 0:384], -SCALE, mask, ALU.mult, ALU.add))
                for tt in range(NT):
                    i = V.tensor_reduce(low[:, n % 2, tt:tt + 1], neg[:, n % 2, keys_of[tt]], AX_X, ALU.min)
                i.then_inc(negated, 1)

            def stick_logits(n):
                dve.wait_ge(logits_ready, n + 1)
                if n >= 2:
                    dve.wait_ge(probs_ready, n - 1)
                V.scalar_tensor_tensor(neg[:, n % 2, :], ps[:, 4, 0:384], SCALE, other_mask[:], ALU.mult,
                                       ALU.subtract).then_inc(negated, 1)

            def stick_sums(n):
                dve.wait_ge(softplus_ready, n - 15)
                link(V.scalar_tensor_tensor(rest_a[:, 0:384], neg[:, n % 2, :], 0.0, rest_a[:, 0:384],
                                            ALU.max, ALU.add))
                for tt, (a, b) in enumerate(((0, P), (P, 3 * P))):
                    back = slice(b - 1, a - 1 if a else None, -1)
                    i = V.tensor_tensor_scan(rest_b[:, back], ones_row(b - a), rest_a[:, back], 0.0,
                                             ALU.mult, ALU.add)
                link(i)
                V.tensor_tensor(neg[:, n % 2, :], neg[:, n % 2, :], rest_b, ALU.subtract).then_inc(arg_ready, 1)

            def ones_row(n):
                return ones[:, 0:1].to_broadcast([P, n])

            def write_out(n):
                zz, q, _, _, kind = jobs[n]
                dve.wait_ge(mixed, n + 1)
                o = ps[:, 6, 0:2 * HD].rearrange("p (t d) -> p t d", t=NT)
                if kind == "stick":
                    V.tensor_copy(zz[:, :, q:q + HD], o).then_inc(out_written, 1)
                    return
                link(V.reciprocal(inv, total[:, n % 2, :]))
                if kind in ("selected", "window"):
                    h = (n - 32) // 2
                    c = 3 * h + (1 if kind == "selected" else 2)
                    link(V.tensor_tensor(share, inv, nsa_gates[:, :, c], ALU.mult))
                for tt in range(NT):
                    if kind in ("selected", "window"):
                        dst = o_attn[:, tt, h * HD:(h + 1) * HD]
                        if kind == "selected":
                            i = V.tensor_scalar(dst, o[:, tt, :], share[:, tt:tt + 1], None, ALU.mult)
                        else:
                            i = V.scalar_tensor_tensor(dst, o[:, tt, :], share[:, tt:tt + 1], dst, ALU.mult, ALU.add)
                    else:
                        i = V.tensor_scalar(zz[:, tt, q:q + HD], o[:, tt, :], inv[:, tt:tt + 1], None, ALU.mult)
                i.then_inc(out_written, 1)

            def heads(n0, n1):
                held, rest, flush = lagging(advance)
                for n in range(n0, n1):
                    if n > n0:
                        copy_probs(n - 1)
                    stick = jobs[n][4] == "stick"
                    (stick_logits if stick else negate)(n)
                    if beside[n] >= 2 and not stick:
                        held(n)
                    if n > n0:
                        write_out(n - 1)
                    if beside[n] < 2 or stick:
                        held(n)
                    if stick:
                        stick_sums(n)
                    rest(n)
                copy_probs(n1 - 1)
                write_out(n1 - 1)
                flush()

            def gate_heads(zz, layer, groups):
                dve.wait_ge(out_written, 16 * (layer + 1))
                all_drained(dve, (L0_OUT, L1_OUT)[layer])

                def gate(g):
                    for at_gate, at_head, width in groups[g]:
                        for tt in range(NT):
                            y = zz[:, tt, at_gate:at_gate + width]
                            i = V.scalar_tensor_tensor(y, y, rstd[:, tt:tt + 1], zz[:, tt, at_head:at_head + width],
                                                       ALU.mult, ALU.mult)
                    i.then_inc(group_gated, 1)

                return gate

            dve.wait_ge(first_landed, 32)
            first_block("n0", norm=reciprocal_root)
            advance(20)
            dve.wait_ge(const_landed, ALL_CONST)
            dve.wait_ge(made["const_made"], 1)
            all_drained(dve, L0_QKV + 6)
            for c0, k in ((IQ, 12), (IQ + 12 * 64, 5)):
                for tt in range(NT):
                    rotate(z0, tt, c0, k, 64, 32, rope64[:, 0, tt, :], rope64[:, 1, tt, :])
                    if c0 == IQ or tt == 0:
                        advance(1)
            link(V.tensor_scalar(idx_w, z0[:, :, IW:IW + 16], 0.25, None, ALU.mult))
            for m in range(2):
                i = V.tensor_copy(ik_twice[:, :, 64 * m:64 * m + 64], z0[:, :, IK:IK + 64])
            i.then_inc(rotated, 1)
            advance(1)
            score = rest_b
            for h in range(16):
                dve.wait_ge(relu_ready, h + 1)
                for tt in range(NT):
                    s, r, w = score[:, keys_of[tt]], neg[:, h % 2, keys_of[tt]], idx_w[:, tt, h:h + 1]
                    if h == 0:
                        i = V.tensor_scalar(s, r, w, None, ALU.mult)
                    else:
                        if tt == 0:
                            dve.wait_ge(scored, h)
                        i = V.scalar_tensor_tensor(s, r, w, s, ALU.mult, ALU.add)
                i.then_inc(scored, 1)
                if h % 2:
                    advance(1)
            dve.wait_ge(scored, 16)
            link(V.tensor_tensor(score, score, causal[:], ALU.subtract))
            for n in range(8):
                for tt in range(NT):
                    i = V.max(best8[:, tt, :], score[:, keys_of[tt]])
                link(i)
                for tt in range(NT):
                    i = V.match_replace(score[:, keys_of[tt]], best8[:, tt, :], score[:, keys_of[tt]], TAKEN)
                link(i)
                if n % 2:
                    advance(1)
            link(V.tensor_scalar(rest_a[:, 0:384], score, TAKEN / 2, BIG, ALU.is_gt, ALU.mult))
            V.tensor_tensor(rest_a[:, 0:384], rest_a[:, 0:384], causal[:], ALU.add).then_inc(scored, 1)
            dve.wait_ge(scored, 17)
            for c0, k in ((QA, 6), (QA + 6 * HD, 5), (QB, 6), (KB, 6)):
                if c0 == QB:
                    all_drained(dve, L0_GATE)
                for tt in range(NT):
                    rotate(z0, tt, c0, k, HD, 64, rope128[:, 0, tt, :], rope128[:, 1, tt, :],
                           rotated if c0 == KB and tt == NT - 1 else None)
                    advance(1)
            heads(0, 16)
            first_block("y0", False, update=gate_heads(z0, 0, (
                ((G0, QA, BW),), ((G0 + BW, QA + BW, BW),),
                ((G0 + 2 * BW, QA + 2 * BW, 256), (G0 + 1280, QB, 256)), ((G0 + 3 * BW, QB + 256, BW),))))
            advance(8)
            last_and_first_block("n1", reciprocal_root)

            advance(4)
            run(L1_QKV + 2, 4)
            advance(1)

            def forget_gates():
                dve.wait_ge(gate_tanh, gate_no[L1_GATE])
                b = forget_b.unsqueeze(1).to_broadcast([P, NT, 8])
                V.tensor_tensor(forget_x, z1[:, :, FL:FL + 8], b, ALU.add).then_inc(made["forget_sum"], 1)
                dve.wait_ge(made["forget_ln"], 1)
                link(V.tensor_scalar(forget_x, forget_x, -1.0, 0.0, ALU.mult, ALU.max))
                link(V.tensor_tensor(forget_x, forget_x, forget_e, ALU.add))
                V.tensor_scalar(neg_log_f, forget_x, 1.0 / SCALE, None, ALU.mult).then_inc(made["forget_ln"], 1)

            dve.wait_ge(strict_landed, 16)
            heads(16, 24)
            forget_gates()
            advance(1)
            heads(24, 32)
            def last_gain(j):
                dve.wait_ge(grow_landed, 16)
                dve.wait_ge(first_squared, j + 1)
                columns = res[:, :, j * BW:(j + 1) * BW]
                V.tensor_tensor(columns, columns, gain_row(j), ALU.mult).then_inc(res_gained, 1)

            first_block("y1", False, update=gate_heads(z1, 1, tuple(
                ((G1 + g * BW, (QC, QC + BW, QD, QD + BW)[g], BW),) for g in range(4))))
            for j in range(2):
                advance(1)
                last_gain(j)
                advance(3)

            def last_norm_and_ff1():
                norms[0] += 1
                dve.wait_ge(root_ready, norms[0])
                link(V.reciprocal(first_rstd, root))
                link(V.tensor_tensor(next_factor, first_rstd, first_rstd, ALU.mult))
                link(V.tensor_tensor(next_mean, next_mean, next_factor, ALU.mult))
                V.tensor_scalar(next_mean, next_mean, EPS, None, ALU.add).then_inc(rstd_ready, 1)
                norms[0] += 1
                dve.wait_ge(root_ready, norms[0])
                link(V.reciprocal(next_factor, root))
                link(V.tensor_tensor(rstd, next_factor, first_rstd, ALU.mult))
                V.tensor_scalar(half_rstd, rstd, 0.5, None, ALU.mult)
                V.scalar_tensor_tensor(half_square, rstd, 0.5, rstd, ALU.mult, ALU.mult).then_inc(rstd_ready, 1)

            last_and_first_block("ff1", last_norm_and_ff1, last_gain)
            for tt in range(NT):
                i = V.tensor_scalar(res[:, tt, :], res[:, tt, :], first_rstd[:, tt:tt + 1], None, ALU.mult)
            i.then_inc(res_ready, 1)

            def feed_forward(b, no, hname):
                u0 = first_unit[b]
                h0 = no * FB

                def hidden_lo(i):
                    for s in range(2):
                        dve.wait_ge(st_hi, i * 2 + (turned_before[hname] + s + 1))
                        V.tensor_tensor(h_lo[:, :, s * P:(s + 1) * P],
                                        ps[:, 6 + s, :].rearrange("p (k n) -> p k n", k=UC),
                                        h_hi[:, :, s * P:(s + 1) * P].bitcast(F32), ALU.subtract).then_inc(st_done, 1)

                def product(u, i):
                    dve.wait_ge(ff_tanh, i + (h0 + 1))
                    V.scalar_tensor_tensor(silu, silu, 1.0, ps[:, 2:4, :], ALU.add, ALU.mult).then_inc(ff_silu, 1)
                    splits(u + 8, 0, 2)
                    dve.wait_ge(ff_silu, i + (h0 + 1))
                    dve.wait_ge(parts_used, u + 8)
                    for tt in range(NT):
                        k = V.scalar_tensor_tensor(hid[:, tt], silu[:, tt], half_square[:, tt:tt + 1], ps[:, tt, :],
                                                   ALU.mult, ALU.mult)
                    k.then_inc(hid_ready, 1)

                def down_added(u, i, j):
                    dve.wait_ge(parts_used, u + (j + 1))
                    bank = 4 + 2 * (j % 2)
                    o = out2[:, :, j * BW:(j + 1) * BW]
                    V.tensor_tensor(o, o, ps[:, bank:bank + 2, :], ALU.add).then_inc(added, 1)

                splits(u0 + 6, 2, 2)
                product(u0, 0)
                dve.wait_ge(added, added_before(no))
                with dve.Fori(0, FB - 1) as i:
                    u = i * 12 + (u0 + 8)
                    splits(u + 2, 2, 4)
                    hidden_lo(i)
                    splits(u + 6, 2, 2)
                    product(u, i + 1)
                    for j in range(4):
                        splits(u + (10 + j), 2 + j, 1)
                        down_added(u + 8, i, j)
                u = u0 + 12 * FB - 4
                at[0] = u0 + 12 * FB
                hidden_lo(FB - 1)
                for j in range(4):
                    if j < 3:
                        split_next(at[0] - 2 + j)
                    down_added(u, FB - 1, j)
                    dve.wait_ge(added, added_before(no) + 4 * (FB - 1) + j + 1)
                    dve.wait_ge(grow_landed, 32 * (no + 1))
                    c = slice(j * BW, (j + 1) * BW)
                    i = V.tensor_tensor(ff_weighted[:, :, c], out2[:, :, c], gain_row(j), ALU.mult)
                i.then_inc(grow_used, 1)
                reciprocal_root(output_rstd)

            feed_forward(FF1, 0, "h1")

            dve.wait_ge(res_ready, 1)
            first_block("mix", norm=reciprocal_root, held=True,
                        update=add_output(lambda g: ff_weighted[:, :, g * BW:(g + 1) * BW]))
            advance(4)
            link(V.tensor_copy(pos_f, position[:]))
            for tt in range(NT):
                i = V.tensor_scalar(ang[:, tt, :], cols[:, INV:INV + 16], pos_f[:, tt:tt + 1], None, ALU.mult)
            link(i)
            link(V.tensor_scalar(cyc, ang, float(np.float32(0.5 / np.pi)), ROUND, ALU.mult, ALU.add))
            link(V.tensor_scalar(cyc, cyc, ROUND, None, ALU.subtract))
            for part in TWO_PI:
                link(V.scalar_tensor_tensor(ang, cyc, -part, ang, ALU.mult, ALU.add))
            advance(1)
            half_pi = float(np.float32(np.pi / 2))
            link(V.tensor_scalar(cyc, ang, half_pi, -2 * float(np.float32(np.pi)), ALU.is_gt, ALU.mult))
            link(V.scalar_tensor_tensor(turn_tab[:, 0], ang, half_pi, cyc, ALU.add, ALU.add))
            link(V.tensor_copy(turn_tab[:, 1], ang))
            pi = float(np.nextafter(np.float32(np.pi), np.float32(0)))
            V.tensor_scalar(turn_tab, turn_tab, pi, -pi, ALU.min, ALU.max).then_inc(made["angle_ready"], 1)
            V.tensor_scalar(half_ba, cols[:, BA:BA + 8], 0.5, None, ALU.mult)
            V.tensor_scalar(half_bi, cols[:, BI:BI + 8], 0.5, None, ALU.mult)
            advance(4)
            dve.wait_ge(made["lam_exp"], 1)
            link(V.tensor_scalar(lam_s, lam_x, 2.0, None, ALU.add))
            link(V.reciprocal(lam_s, lam_s))
            link(V.tensor_tensor(lam_s, lam_s, lam_x, ALU.mult))
            link(V.tensor_tensor(lam_s2, lam_s, lam_s, ALU.mult))
            link(V.tensor_scalar(lam_q, lam_s2, 1.0 / 17, None, ALU.mult))
            advance(1)
            for odd in (15, 13, 11, 9, 7, 5, 3):
                link(V.scalar_tensor_tensor(lam_q, lam_q, 1.0 / odd, lam_s2, ALU.add, ALU.mult))
            link(V.scalar_tensor_tensor(lam_q, lam_q, 1.0, lam_s, ALU.add, ALU.mult))
            advance(1)
            link(V.tensor_scalar(lam_s, cols[:, LAM:LAM + 8], -1.0, 0.0, ALU.mult, ALU.max))
            link(V.scalar_tensor_tensor(lam_s, lam_q, 2.0, lam_s, ALU.mult, ALU.add))
            link(V.tensor_scalar(m4sp, lam_s, -4.0, None, ALU.mult))
            V.memset(r_pad[:, :, 0:3], 0.0)
            advance(9)
            dve.wait_ge(made["rec_padded"], 1)
            for tap in range(4):
                for b in range(LB):
                    w = cols[:, CONV + 8 * tap + b:CONV + 8 * tap + b + 1]
                    src, dst = r_pad[:, b, tap:tap + SEQ], by_block(r1)[:, b, :]
                    if tap == 0:
                        i = V.tensor_scalar(dst, src, w, cols[:, CONVB + b:CONVB + b + 1], ALU.mult, ALU.add)
                    else:
                        i = V.scalar_tensor_tensor(dst, src, w, dst, ALU.mult, ALU.add)
                if tap < 3:
                    link(i)
                else:
                    i.then_inc(made["rec_conv"], 1)
                advance(1)
            advance(2)
            dve.wait_ge(made["rec_r_tanh"], 1)
            for b in range(LB):
                i = V.tensor_scalar(by_block(r2)[:, b, :], by_block(r2)[:, b, :], m4sp[:, b:b + 1], m4sp[:, b:b + 1],
                                    ALU.mult, ALU.add)
            i.then_inc(made["rec_log_a"], 1)
            advance(2)
            dve.wait_ge(made["rec_a"], 1)
            link(V.tensor_tensor(r2, r3, r3, ALU.mult))
            V.scalar_tensor_tensor(r2, r2, 1.0, r0, ALU.add, ALU.mult).then_inc(made["rec_square"], 1)
            advance(1)
            dve.wait_ge(made["rec_i_tanh"], 1)
            link(V.scalar_tensor_tensor(r4, r4, 1.0, r1, ALU.add, ALU.mult))
            dve.wait_ge(made["rec_root"], 1)
            link(V.scalar_tensor_tensor(r4, r4, 0.5, r2, ALU.mult, ALU.mult))
            advance(1)
            for b in range(LB):
                i = V.tensor_tensor_scan(by_block(r0)[:, b, :], by_block(r3)[:, b, :], by_block(r4)[:, b, :], 0.0,
                                         ALU.mult, ALU.add)
            link(i)
            advance(1)
            dve.wait_ge(made["rec_y_gelu"], 1)
            link(V.tensor_tensor(r1, r0, work[:, 0:2048], ALU.mult))
            V.tensor_tensor(r2, r1, r1, ALU.mult).then_inc(made["rec_out_squared"], 1)
            advance(1)
            dve.wait_ge(made["rec_summed"], 1)
            dve.wait_ge(made["angle_sin"], 1)
            all_drained(dve, MIX_QKV + 3)

            def turn_heads(c0, k, tt):
                rotate(z2, tt, c0, k, HD, 16, turn_tab[:, 0, tt, :], turn_tab[:, 1, tt, :],
                       rotated if c0 != ZKS and tt == NT - 1 else None)

            for tt in range(NT):
                turn_heads(ZQ, 10, tt)
                advance(1)
            advance(1)
            dve.wait_ge(made["cmp_cleared"], 1)
            for m, pos in enumerate((POSK, POSV)):
                dve.wait_ge(made["cmp_turned"], m + 1)
                x = cmp_x[m].rearrange("p (l g c) -> p l g c", l=32, g=2)
                for g in range(2):
                    for half in range(2):
                        src = ps[:, 4 + m, g * SEQ:(g + 1) * SEQ].rearrange("p (c l) -> p l c", l=16)
                        i = V.tensor_tensor(
                            x[:, 16 * half:16 * half + 16, g, 0:NCMP], src[:, :, half:half + NCMP],
                            cols[:, pos + 16 * half:pos + 16 * half + 16].unsqueeze(2).to_broadcast([P, 16, NCMP]),
                            ALU.add)
                i.then_inc(made["cmp_summed"], 1)
            advance(1)
            xf = [x[:].rearrange("p k s -> p (k s)") for x in (x_hi, x_lo)]
            for m in range(2):
                dve.wait_ge(made["cmp_hi"], m + 1)
                V.tensor_tensor(xf[1][:, 1024 * m:1024 * (m + 1)], cmp_x[m],
                                xf[0][:, 1024 * m:1024 * (m + 1)].bitcast(F32), ALU.subtract
                                ).then_inc(made["cmp_lo"], 1)
            dve.wait_ge(made["rec_norm_root"], 1)
            link(V.reciprocal(r0[:, SEQ:2 * SEQ], r0[:, 0:SEQ]))
            link(V.tensor_tensor(by_block(r1), by_block(r1),
                                 r0[:, SEQ:2 * SEQ].unsqueeze(1).to_broadcast([P, LB, SEQ]), ALU.mult))
            advance(1)
            V.tensor_tensor(by_block(r1), by_block(r1),
                            cols[:, GAIN["rec"]:GAIN["rec"] + LB].unsqueeze(2).to_broadcast([P, LB, SEQ]),
                            ALU.mult).then_inc(made["rec_ready"], 1)
            advance(1)
            bias = gate_bias.unsqueeze(1).to_broadcast([P, NT, 24])
            V.tensor_tensor(nsa_gates, z2[:, :, ZG:ZG + 24], bias, ALU.add).then_inc(made["nsa_gate_sum"], 1)
            all_drained(dve, CMP)
            for c0 in (ZKS, ZKW):
                for tt in range(NT):
                    turn_heads(c0, 2, tt)
                advance(1)
            dve.wait_ge(made["rec_hi"], 1)
            V.tensor_tensor(x_lo[:, LB:2 * LB, :], by_block(r1), x_hi[:, LB:2 * LB, :].bitcast(F32),
                            ALU.subtract).then_inc(made["rec_lo"], 1)
            dve.wait_ge(made["nsa_gate_tanh"], 1)
            link(V.tensor_scalar(nsa_gates, nsa_gates, 0.5, 0.5, ALU.mult, ALU.add))
            advance(4)
            heads(32, 48)
            cl = cmp_logits.rearrange("p (h c) -> p h c", c=NCMP)
            away = rest_a[:, 0:240]
            link(V.tensor_scalar(away, cmp_ok[:], -BIG, BIG, ALU.mult, ALU.add))
            link(V.scalar_tensor_tensor(cmp_logits, cmp_logits, -SCALE, away, ALU.mult, ALU.add))
            link(V.tensor_reduce(cmp_low, cl, AX_X, ALU.min))
            V.tensor_tensor(cl, cl, cmp_low.unsqueeze(2).to_broadcast([P, 16, NCMP]),
                            ALU.subtract).then_inc(made["cmp_negated"], 1)
            dve.wait_ge(made["cmp_probs"], 1)
            cp = rest_a[:, 240:480]
            link(V.tensor_reduce(cmp_sum, cp.rearrange("p (h c) -> p h c", c=NCMP), AX_X, ALU.add))
            link(V.reciprocal(cmp_sum, cmp_sum))
            gates0 = nsa_gates.rearrange("p t (h j) -> p h t j", j=3)[:, :, :, 0]
            cs = cmp_sum.rearrange("p (h t) -> p h t", t=NT)
            link(V.tensor_tensor(cs, cs, gates0, ALU.mult))
            V.tensor_tensor(cp, cp, cmp_ok[:], ALU.mult).then_inc(made["cmp_weighted"], 1)
            for h in range(8):
                dve.wait_ge(made["cmp_mixed"], h + 1)
                for tt in range(NT):
                    dst = o_attn[:, tt, h * HD:(h + 1) * HD]
                    i = V.scalar_tensor_tensor(dst, ps[:, 6, tt * HD:(tt + 1) * HD], cs[:, h, tt:tt + 1], dst,
                                               ALU.mult, ALU.add)
                i.then_inc(made["cmp_added"] if h < 7 else y_ready, 1)
            reciprocal_root()
            for g in range(2):
                lo_group("attn", g)
            advance(15)
            advance(1, held=True)
            reciprocal_root(output_rstd)
            first_block("ff2", norm=reciprocal_root, held=True,
                        update=add_output(lambda g: out2[:, :, g * BW:(g + 1) * BW]))
            feed_forward(FF2, 1, "h2")
            first_block("ple", norm=reciprocal_root, held=True,
                        update=add_output(lambda g: ff_weighted[:, :, g * BW:(g + 1) * BW]))
            advance(12)
            for s in range(2):
                dve.wait_ge(st_hi, turned_before["p"] + s + 1)
                V.tensor_tensor(h_lo[:, 0:2, s * P:(s + 1) * P],
                                ps[:, 6 + s, 0:2 * P].rearrange("p (k n) -> p k n", k=2),
                                h_hi[:, 0:2, s * P:(s + 1) * P].bitcast(F32), ALU.subtract).then_inc(st_done, 1)
            advance(4)
            reciprocal_root(output_rstd)
            update = add_output(lambda g: last_weighted[g])
            for g in range(4):
                update(g)


_WEIGHTS = {"w_in0": "w_in0", "w_out0": "w_out0", "w_in1": "w_in1", "w_out1": "w_out1", "w_in_2": "w_in_2",
            "w_out_2": "w_out_2", "w_ple_gate_2": "w_ple_gate_2", "w_ple_proj_2": "w_ple_proj_2",
            "ff1_w_gate": "ff1_w_gate_2", "ff1_w_up": "ff1_w_up_2", "ff1_w_down": "ff1_w_down_2",
            "ff2_w_gate": "ff2_w_gate_2", "ff2_w_up": "ff2_w_up_2", "ff2_w_down": "ff2_w_down_2",
            "rg_w_a": "rg_w_a_2", "rg_w_i": "rg_w_i_2", "cmp_k_w1": "cmp_k_w1_2", "cmp_v_w1": "cmp_v_w1_2",
            "cmp_k_w2": "cmp_k_w2_2", "cmp_v_w2": "cmp_v_w2_2"}


def kernel(**inputs):
    import concourse.bacc as bacc
    from concourse.bass_utils import run_bass_kernel_spmd as run

    g = {n: np.asarray(a) for n, a in inputs.items()}
    arrays = {}
    for name, source in _WEIGHTS.items():
        a = g[source]
        arrays[name] = a.reshape(a.shape[1:]) if source[-2:] == "_2" else a

    def by_columns(v):
        return v.reshape(-1, P).T

    const = constants()
    arrays["x"] = g["x"].reshape(SEQ, D)
    arrays["p"] = g["p_2"].reshape(SEQ, -1)
    arrays["positions"] = g["positions_2"].reshape(NT, P).T.astype(np.int32)
    arrays["rows"] = np.stack([g["norm_f"], g["ff1_post_g_2"][0], g["mix_post_g_2"][0], g["ff2_post_g_2"][0],
                               g["ple_post_g_2"][0]])
    arrays["cols"] = np.concatenate(
        [by_columns(v) for v in (g["norm0"], g["norm1"], g["ff1_pre_g_2"][0], g["mix_pre_g_2"][0],
                                 g["attn_out_g_2"][0], g["rec_out_g_2"][0], g["ff2_pre_g_2"][0],
                                 g["ple_pre_g_2"][0])]
        + [by_columns(g["conv_w_2"][0][k]) for k in range(4)]
        + [by_columns(g[n][0]) for n in ("conv_b_2", "rg_b_a_2", "rg_b_i_2", "rg_lambda_2")]
        + [const.pop("inv"), g["cmp_pos_k_2"][0].T, g["cmp_pos_v_2"][0].T], axis=1)
    arrays["b_f1"] = g["b_f1"].reshape(1, 8)
    arrays["nsa_gate_b"] = g["nsa_gate_b_2"].reshape(1, 24)
    arrays.update(const)
    arrays = {n: np.ascontiguousarray(a) for n, a in arrays.items()}

    nc = bacc.Bacc("TRN2", target_bir_lowering=False, num_devices=1)
    t = {n: nc.dram_tensor(f"in_{n}", a.shape, mybir.dt.from_np(a.dtype), kind="ExternalInput").ap()
         for n, a in arrays.items()}
    t["out"] = nc.dram_tensor("result", (SEQ, D), F32, kind="ExternalOutput").ap()
    for n in ("x", "p", "out"):
        t[n] = t[n].rearrange("(t p) d -> p t d", p=P)
    build(nc, t)
    r = run(nc, [{f"in_{n}": a for n, a in arrays.items()}], core_ids=[0])
    return r.results[0]["result"].reshape(1, SEQ, D)
```
